# Optimizing a Trainium2 kernel written in Bass

```python
import math
import jax, jax.numpy as jnp
from jax import lax
import numpy as np

D_MODEL = 1024
BATCH = 1
SEQ = 256
DEPTH = 1

HEAD_DIM = 64
SWA_HEADS = 8
SWA_KV_HEADS = 2
SWA_WINDOW = 128
SWA_BLOCK = 128
MOBA_HEADS = 8
MOBA_BLOCK = 256
MOBA_TOPK = 3
MOBA_Q_CHUNK = 16
N_EXPERTS = 64
TOP_K = 8
N_GROUPS = 8
TOPK_GROUPS = 4
EXPERT_FF = 256
SHARED_FF = 256
ROUTED_SCALE = 2.5
DISPATCH_BLOCK = 128
DEEPNORM_ALPHA = (2.0 * DEPTH) ** 0.25
DEEPNORM_BETA = (8.0 * DEPTH) ** -0.25
LN_EPS = 1e-5
NEG_INF = -1e30
SWA_Q_W = SWA_HEADS * HEAD_DIM
SWA_KV_W = SWA_KV_HEADS * HEAD_DIM
MOBA_W = MOBA_HEADS * HEAD_DIM
IN_COLS = SWA_Q_W + 2 * SWA_KV_W + 3 * MOBA_W + 2 * D_MODEL

kernel_name = "hybrid_swa_moba_gated_moe_deepnorm"

F32 = jnp.float32

def _alibi_slopes():
    n = SWA_HEADS + MOBA_HEADS
    s = 2.0 ** (-8.0 * np.arange(1, n + 1) / n)
    return jnp.asarray(s[:SWA_HEADS], F32), jnp.asarray(s[SWA_HEADS:], F32)

def _layernorm(x, g, b):
    xf = x.astype(F32)
    mu = xf.mean(-1, keepdims=True)
    var = jnp.mean(jnp.square(xf - mu), -1, keepdims=True)
    return ((xf - mu) * lax.rsqrt(var + LN_EPS) * g.astype(F32) + b.astype(F32)).astype(x.dtype)

def _swa_attention(q, k, v, sinks, slopes):
    B, S = q.shape[:2]
    G = SWA_HEADS // SWA_KV_HEADS
    nq = S // SWA_BLOCK
    qb = q.reshape(B, nq, SWA_BLOCK, SWA_KV_HEADS, G, HEAD_DIM)

    def band(t):
        tb = t.reshape(B, nq, SWA_BLOCK, SWA_KV_HEADS, HEAD_DIM)
        prev = jnp.pad(tb[:, :-1], ((0, 0), (1, 0), (0, 0), (0, 0), (0, 0)))
        return jnp.concatenate([prev, tb], axis=2)

    kk, vv = band(k), band(v)
    s = jnp.einsum('bnqhgd,bnkhd->bnhgqk', qb, kk, preferred_element_type=F32) * (HEAD_DIM ** -0.5)
    i = jnp.arange(SWA_BLOCK)[:, None]
    j = jnp.arange(2 * SWA_BLOCK)[None, :]
    dist = i + SWA_BLOCK - j
    kpos = jnp.arange(nq)[:, None, None] * SWA_BLOCK + j - SWA_BLOCK
    valid = (dist >= 0) & (dist < SWA_WINDOW) & (kpos >= 0)
    slope = slopes.reshape(SWA_KV_HEADS, G)[:, :, None, None]
    s = jnp.where(valid[None, :, None, None], s - slope * dist.astype(F32), NEG_INF)
    sink = sinks.astype(F32).reshape(SWA_KV_HEADS, G)[:, :, None, None]
    m = jnp.maximum(s.max(-1, keepdims=True), sink)
    e = jnp.exp(s - m)
    p = e / (e.sum(-1, keepdims=True) + jnp.exp(sink - m))
    o = jnp.einsum('bnhgqk,bnkhd->bnqhgd', p.astype(v.dtype), vv)
    return o.reshape(B, S, SWA_Q_W)

def _moba_attention(q, k, v, slopes):
    B, S, H, Dh = q.shape
    nb = -(-S // MOBA_BLOCK)
    s_pad = nb * MOBA_BLOCK
    pad = ((0, 0), (0, s_pad - S), (0, 0), (0, 0))
    k_blocks = jnp.pad(k, pad).reshape(B, nb, MOBA_BLOCK, H, Dh)
    k_mean = k_blocks.astype(F32).mean(2)
    kbh = k_blocks.transpose(0, 3, 1, 2, 4)
    vbh = jnp.pad(v, pad).reshape(B, nb, MOBA_BLOCK, H, Dh).transpose(0, 3, 1, 2, 4)
    tk = min(MOBA_TOPK, nb)
    scale = Dh ** -0.5
    b_ix = jnp.arange(B)[:, None, None]
    h_ix = jnp.arange(H)[None, :, None]
    j = jnp.arange(MOBA_BLOCK)
    QC = MOBA_Q_CHUNK

    def chunk(c):
        t0 = c * QC
        qc = lax.dynamic_slice_in_dim(q, t0, QC, axis=1).transpose(0, 2, 1, 3)
        t = t0 + jnp.arange(QC)
        own = t0 // MOBA_BLOCK
        gate = jnp.einsum('bhqd,bnhd->bhqn', qc.astype(F32), k_mean)
        gate = jnp.where(jnp.arange(nb) < own, gate, NEG_INF)
        _, sel = lax.top_k(gate, tk)
        sel_valid = jnp.arange(tk) < own
        flat = sel.reshape(B, H, QC * tk)
        kg = kbh[b_ix, h_ix, flat].reshape(B, H, QC, tk, MOBA_BLOCK, Dh)
        vg = vbh[b_ix, h_ix, flat].reshape(B, H, QC, tk, MOBA_BLOCK, Dh)
        s_sel = jnp.einsum('bhqd,bhqnkd->bhqnk', qc, kg, preferred_element_type=F32) * scale
        dist_sel = t[:, None, None] - (sel[..., None] * MOBA_BLOCK + j)
        s_sel = jnp.where(sel_valid[:, None], s_sel - slopes[:, None, None, None] * dist_sel.astype(F32), NEG_INF)
        k_own = lax.dynamic_slice_in_dim(kbh, own, 1, axis=2)[:, :, 0]
        v_own = lax.dynamic_slice_in_dim(vbh, own, 1, axis=2)[:, :, 0]
        s_own = jnp.einsum('bhqd,bhkd->bhqk', qc, k_own, preferred_element_type=F32) * scale
        dist_own = t[:, None] - (own * MOBA_BLOCK + j)[None, :]
        s_own = jnp.where(dist_own >= 0, s_own - slopes[:, None, None] * dist_own.astype(F32), NEG_INF)
        s_all = jnp.concatenate([s_sel.reshape(B, H, QC, tk * MOBA_BLOCK), s_own], axis=-1)
        p = jax.nn.softmax(s_all, axis=-1).astype(v.dtype)
        p_sel = p[..., :tk * MOBA_BLOCK].reshape(B, H, QC, tk, MOBA_BLOCK)
        p_own = p[..., tk * MOBA_BLOCK:]
        o = jnp.einsum('bhqnk,bhqnkd->bhqd', p_sel, vg) + jnp.einsum('bhqk,bhkd->bhqd', p_own, v_own)
        return o.transpose(0, 2, 1, 3)

    out = lax.map(chunk, jnp.arange(S // QC))
    return out.transpose(1, 0, 2, 3, 4).reshape(B, S, H * Dh)

def _swiglu(x, wg, wu, wd):
    return (jax.nn.silu(x @ wg) * (x @ wu)) @ wd

def _grouped_experts(xf, top_idx, top_w, w_gate, w_up, w_down):
    T = xf.shape[0]
    n_pairs = T * TOP_K
    e_flat = top_idx.reshape(-1)
    tok_flat = jnp.repeat(jnp.arange(T, dtype=jnp.int32), TOP_K)
    w_flat = top_w.reshape(-1)
    order = jnp.argsort(e_flat)
    e_s, tok_s, w_s = e_flat[order], tok_flat[order], w_flat[order]
    counts = jnp.bincount(e_flat, length=N_EXPERTS)
    padded = (counts + DISPATCH_BLOCK - 1) // DISPATCH_BLOCK * DISPATCH_BLOCK
    raw_start = jnp.cumsum(counts) - counts
    pad_end = jnp.cumsum(padded)
    pad_start = pad_end - padded
    dest = pad_start[e_s] + (jnp.arange(n_pairs) - raw_start[e_s])
    n_pad = n_pairs + N_EXPERTS * DISPATCH_BLOCK
    n_blk = n_pad // DISPATCH_BLOCK
    buf_tok = jnp.zeros((n_pad,), jnp.int32).at[dest].set(tok_s)
    buf_w = jnp.zeros((n_pad,), xf.dtype).at[dest].set(w_s)
    blk_e = jnp.minimum(jnp.searchsorted(pad_end, jnp.arange(n_blk) * DISPATCH_BLOCK, side='right'), N_EXPERTS - 1)

    def step(acc, inp):
        tok, wt, e = inp
        xb = xf[tok]
        y = _swiglu(xb, w_gate[e], w_up[e], w_down[e]) * wt[:, None]
        return acc.at[tok].add(y), None

    out, _ = lax.scan(step, jnp.zeros_like(xf),
                      (buf_tok.reshape(n_blk, DISPATCH_BLOCK), buf_w.reshape(n_blk, DISPATCH_BLOCK), blk_e))
    return out

def _moe(xf, w_router, router_bias, w_exp_gate, w_exp_up, w_exp_down, w_sh_gate, w_sh_up, w_sh_down):
    T = xf.shape[0]
    scores = jax.nn.sigmoid(jnp.einsum('td,de->te', xf, w_router, preferred_element_type=F32))
    biased = scores + router_bias.astype(F32)
    grp = biased.reshape(T, N_GROUPS, N_EXPERTS // N_GROUPS)
    grp_score = lax.top_k(grp, 2)[0].sum(-1)
    _, grp_idx = lax.top_k(grp_score, TOPK_GROUPS)
    grp_mask = jax.nn.one_hot(grp_idx, N_GROUPS, dtype=F32).sum(-2) > 0
    exp_mask = jnp.repeat(grp_mask, N_EXPERTS // N_GROUPS, axis=-1)
    _, top_idx = lax.top_k(jnp.where(exp_mask, biased, NEG_INF), TOP_K)
    top_w = jnp.take_along_axis(scores, top_idx, axis=-1)
    top_w = top_w / top_w.sum(-1, keepdims=True) * ROUTED_SCALE
    routed = _grouped_experts(xf, top_idx, top_w.astype(xf.dtype), w_exp_gate, w_exp_up, w_exp_down)
    return routed + _swiglu(xf, w_sh_gate, w_sh_up, w_sh_down)

def setup_inputs(seed: int = 0) -> dict:
    key = jax.random.key(seed)
    ks = jax.random.split(key, 18)
    D, L, E, F = D_MODEL, DEPTH, N_EXPERTS, EXPERT_FF
    nrm = jax.random.normal
    col_scale = np.ones((IN_COLS,), np.float32)
    va0 = SWA_Q_W + SWA_KV_W
    col_scale[va0:va0 + SWA_KV_W] = DEEPNORM_BETA
    vb0 = SWA_Q_W + 2 * SWA_KV_W + 2 * MOBA_W
    col_scale[vb0:vb0 + MOBA_W] = DEEPNORM_BETA
    return {
        "x": nrm(ks[0], (BATCH, SEQ, D), F32),
        "w_in": nrm(ks[1], (L, D, IN_COLS), F32) * (D ** -0.5) * jnp.asarray(col_scale),
        "swa_sinks": nrm(ks[2], (L, SWA_HEADS), F32) * 0.5,
        "w_branch_swa": nrm(ks[3], (L, SWA_Q_W, D), F32) * (SWA_Q_W ** -0.5) * DEEPNORM_BETA,
        "w_branch_moba": nrm(ks[4], (L, MOBA_W, D), F32) * (MOBA_W ** -0.5) * DEEPNORM_BETA,
        "w_out": nrm(ks[5], (L, D, D), F32) * (D ** -0.5) * DEEPNORM_BETA,
        "ln1_g": 1.0 + 0.05 * nrm(ks[6], (L, D), F32),
        "ln1_b": 0.02 * nrm(ks[7], (L, D), F32),
        "w_router": nrm(ks[8], (L, D, E), F32) * (D ** -0.5),
        "router_bias": 0.01 * nrm(ks[9], (L, E), F32),
        "w_exp_gate": nrm(ks[10], (L, E, D, F), F32) * (D ** -0.5) * DEEPNORM_BETA,
        "w_exp_up": nrm(ks[11], (L, E, D, F), F32) * (D ** -0.5) * DEEPNORM_BETA,
        "w_exp_down": nrm(ks[12], (L, E, F, D), F32) * (F ** -0.5) * DEEPNORM_BETA,
        "w_sh_gate": nrm(ks[13], (L, D, SHARED_FF), F32) * (D ** -0.5) * DEEPNORM_BETA,
        "w_sh_up": nrm(ks[14], (L, D, SHARED_FF), F32) * (D ** -0.5) * DEEPNORM_BETA,
        "w_sh_down": nrm(ks[15], (L, SHARED_FF, D), F32) * (SHARED_FF ** -0.5) * DEEPNORM_BETA,
        "ln2_g": 1.0 + 0.05 * nrm(ks[16], (L, D), F32),
        "ln2_b": 0.02 * nrm(ks[17], (L, D), F32),
    }

def reference(x, w_in, swa_sinks, w_branch_swa, w_branch_moba, w_out, ln1_g, ln1_b, w_router, router_bias,
              w_exp_gate, w_exp_up, w_exp_down, w_sh_gate, w_sh_up, w_sh_down, ln2_g, ln2_b):
    B, S, D = x.shape
    slopes_swa, slopes_moba = _alibi_slopes()
    sizes = [SWA_Q_W, SWA_KV_W, SWA_KV_W, MOBA_W, MOBA_W, MOBA_W, D_MODEL, D_MODEL]
    offsets = []
    acc = 0
    for sz in sizes[:-1]:
        acc += sz
        offsets.append(acc)
    h = x
    for l in range(DEPTH):
        proj = h @ w_in[l]
        qa, ka, va, qb, kb, vb, ga, gb = jnp.split(proj, offsets, axis=-1)
        att_a = _swa_attention(qa.reshape(B, S, SWA_HEADS, HEAD_DIM), ka.reshape(B, S, SWA_KV_HEADS, HEAD_DIM),
                               va.reshape(B, S, SWA_KV_HEADS, HEAD_DIM), swa_sinks[l], slopes_swa)
        att_b = _moba_attention(qb.reshape(B, S, MOBA_HEADS, HEAD_DIM), kb.reshape(B, S, MOBA_HEADS, HEAD_DIM),
                                vb.reshape(B, S, MOBA_HEADS, HEAD_DIM), slopes_moba)
        y_a = att_a @ w_branch_swa[l]
        y_b = att_b @ w_branch_moba[l]
        mix = (jax.nn.sigmoid(ga) * y_a + jax.nn.sigmoid(gb) * y_b) @ w_out[l]
        h = _layernorm(DEEPNORM_ALPHA * h + mix, ln1_g[l], ln1_b[l])
        ffn = _moe(h.reshape(B * S, D), w_router[l], router_bias[l], w_exp_gate[l], w_exp_up[l], w_exp_down[l],
                   w_sh_gate[l], w_sh_up[l], w_sh_down[l]).reshape(B, S, D)
        h = _layernorm(DEEPNORM_ALPHA * h + ffn, ln2_g[l], ln2_b[l])
    return h


_drawn_inputs = setup_inputs


def setup_inputs(seed=0):
    import zlib

    import numpy as np

    out = dict(_drawn_inputs(seed))
    spreads = {}
    factors = {'swa_sinks': 8.0, 'router_bias': 2.677, 'ln2_b': 2.881}
    for name, (base, spread) in spreads.items():
        noise = np.random.default_rng([zlib.crc32(name.encode()), seed]).standard_normal(out[name].shape)
        drawn = base * np.exp(spread * noise) if base else spread * noise
        out[name] = __import__('jax').numpy.asarray(drawn.astype(out[name].dtype))
    for name, factor in factors.items():
        out[name] = (out[name] * factor).astype(out[name].dtype)
    return out
```

```python
from contextlib import ExitStack

import concourse.bass as bass
from concourse import mybir

F32 = mybir.dt.float32
BF16 = mybir.dt.bfloat16
I32 = mybir.dt.int32
ALU = mybir.AluOpType
ACT = mybir.ActivationFunctionType
AX_X = mybir.AxisListType.X

P = 128
SEQ = 256
TILES = SEQ // P
D = 1024
KC = D // P
HEAD_DIM = 64
SWA_HEADS = 8
MOBA_HEADS = 8
N_EXPERTS = 64
N_GROUPS = 8
PER_GROUP = N_EXPERTS // N_GROUPS
TOPK_GROUPS = 4
FF = 256
ROUTED_SCALE = 2.5
ALPHA = 2.0 ** 0.25
LN_EPS = 1e-5
NEG_INF = -1e30
BIG = 3e38

IN_COLS = 4352
CHUNK = 768
N_CHUNKS = -(-IN_COLS // CHUNK)
GATE_COL = 2304

RING = 6
SLOT = 3 * KC * FF
W_UP = KC * FF
W_DOWN = 2 * KC * FF
SLOTS = 64
PAIRS = N_EXPERTS // 2
ROUNDS = SEQ // SLOTS
UNROLL = RING // 2
LOADS_PEELED = UNROLL
EXTRA = 2

SWA_PAIRS = SWA_HEADS // 2
HEAD_PAIRS = (SWA_HEADS + MOBA_HEADS) // 2
SLOPES = [2.0 ** (-8.0 * (i + 1) / (SWA_HEADS + MOBA_HEADS)) for i in range(SWA_HEADS + MOBA_HEADS)]
ATT_SCALE = HEAD_DIM ** -0.5

QKV_UNITS = 16
GATE_UNITS = 2 * D // P
UNITS = QKV_UNITS + GATE_UNITS


def heads_of(pair):
    if pair < SWA_PAIRS:
        return [(pair, pair), (pair + SWA_PAIRS, pair + SWA_PAIRS)]
    c = pair - SWA_PAIRS
    return [(SWA_HEADS + 2 * c + i, 2 * c + i) for i in range(2)]


def evacuated(unit):
    if unit < QKV_UNITS:
        return ("act" if unit % 2 == 0 else "dve"), unit // 2 + 1
    return "act", QKV_UNITS // 2 + unit - QKV_UNITS + 1


def block_program(nc, x, w_in, swa_sinks, w_branch_swa, w_branch_moba, w_out, ln1_g, ln1_b, w_router, router_bias,
                  w_exp_gate, w_exp_up, w_exp_down, w_sh_gate, w_sh_up, w_sh_down, ln2_g, ln2_b, out):
    with ExitStack() as ctx:
        def sb(name, shape, dt=F32):
            return ctx.enter_context(nc.sbuf_tensor(name, shape, dt))

        def sem(name):
            return ctx.enter_context(nc.semaphore(name))

        bank = [ctx.enter_context(nc.psum_tensor(f"bank{i}", [P, 512], F32)) for i in range(8)]

        ring = sb("ring", [P, RING, SLOT])
        h_sb = sb("h_sb", [P, TILES, D])
        hT = sb("hT", [P, KC, SEQ])
        gates = sb("gates", [P, GATE_UNITS, SEQ])
        scratch = sb("scratch", [P, 6144])
        ident = sb("ident", [P, P])
        before = sb("before", [P, P], BF16)
        ones = sb("ones", [P, P], BF16)
        dist_swa = sb("dist_swa", [P, 384])
        dist_moba = sb("dist_moba", [P, 384])
        place_ids = sb("place_ids", [P, SLOTS])
        wr_sb = sb("wr_sb", [P, KC, N_EXPERTS])

        def piece(base, at, shape):
            n = 1
            for s in shape:
                n *= s
            v = base[:, at:at + n]
            if len(shape) == 2:
                v = v.rearrange("p (a b) -> p a b", b=shape[1])
            if len(shape) == 3:
                v = v.rearrange("p (a b c) -> p a b c", b=shape[1], c=shape[2])
            return v

        q_swa = piece(scratch, 0, (4, SEQ))
        q_moba = piece(scratch, 1024, (4, SEQ))
        k_swa = piece(scratch, 2048, (SEQ,))
        v_swa = piece(scratch, 2304, (TILES, P))
        k_moba = piece(scratch, 2560, (4, SEQ))
        v_moba = piece(scratch, 3584, (TILES, 512))
        prob = piece(scratch, 4608, (2, 2, 384))
        ln1_gb = piece(scratch, 2560, (2, D))
        tail = ring[:, RING - 1, W_DOWN:SLOT]
        probT = piece(tail, 0, (2, 2, 384))
        row_max = piece(tail, 1536, (16, 2))
        neg_max = piece(tail, 1568, (16, 2))
        row_sum = piece(tail, 1600, (16, 2))
        sink_exp = piece(tail, 1632, (16, 2))
        inv_sum = piece(tail, 1664, (16, 2))
        sinks = piece(tail, 1696, (SWA_HEADS,))
        sinks8 = piece(tail, 1704, (SWA_HEADS,))
        choose = [piece(scratch, 256 * i, (TILES, P)) for i in range(3)]
        choose_w = [piece(scratch, 768 + 256 * i, (TILES, P)) for i in range(3)]
        turned_sb = [piece(scratch, 1536 + 512 * i, (512,)) for i in range(3)]
        xg = piece(scratch, 3072, (KC, P))
        silu_sb = piece(scratch, 4096, (FF,))
        hid = piece(scratch, 4352, (FF,))
        y_sb = piece(scratch, 4608, (D,))
        sh_silu = piece(scratch, 4608, (2, SEQ))
        sh_hidT = piece(scratch, 5120, (2, SEQ))
        gflat = gates[:, :, :].rearrange("p a b -> p (a b)")
        W66 = N_EXPERTS + EXTRA
        r_exp = piece(gflat, 0, (TILES, N_EXPERTS))
        r_one = piece(gflat, 128, (TILES, N_EXPERTS))
        score = piece(gflat, 256, (TILES, N_EXPERTS))
        biased = piece(gflat, 384, (TILES, N_EXPERTS))
        top_in_group = piece(gflat, 512, (TILES * N_GROUPS, 8))
        group_sum = piece(gflat, 640, (TILES, 2 * N_GROUPS))
        group_top = piece(gflat, 672, (TILES, 8))
        group_pick = piece(gflat, 688, (TILES, 8))
        group_marked = piece(gflat, 704, (TILES, 2 * N_GROUPS))
        group_on = piece(gflat, 736, (TILES * N_GROUPS, 1))
        group_off = piece(gflat, 752, (TILES * N_GROUPS, 1))
        masked = piece(gflat, 768, (TILES, N_EXPERTS))
        expert_top = piece(gflat, 896, (TILES, 8))
        expert_marked = piece(gflat, 912, (TILES, N_EXPERTS))
        weight_sum = piece(gflat, 1040, (TILES, 1))
        weight_inv = piece(gflat, 1042, (TILES, 1))
        most = piece(gflat, 1044, (1,))
        over_f = piece(gflat, 1045, (1,))
        over = piece(gflat, 1046, (1,)).bitcast(I32)
        ln_stats = piece(gflat, 1048, (TILES, 12))
        ln_mv = piece(gflat, 1072, (TILES, 2))
        ln_rstd = piece(gflat, 1076, (TILES, 1))
        ln_shift = piece(gflat, 1078, (TILES, 1))
        ln_var = piece(gflat, 1080, (TILES, 1))
        ln_root = piece(gflat, 1082, (TILES, 1))
        masked_sum = piece(gflat, 1088, (TILES, N_EXPERTS))
        bias_r = piece(gflat, 1216, (N_EXPERTS,))
        chosen = piece(gflat, 1280, (TILES * N_EXPERTS // 2,)).bitcast(BF16).rearrange("p (t e) -> p t e", t=TILES)
        weight = piece(gflat, 1408, (TILES, W66))
        place = piece(gflat, 1544, (TILES, W66))
        ln2_gb = piece(ring[:, RING - 2, :], 0, (2, D))

        x_in = [sem(f"x_in{t}") for t in range(TILES)]
        w_in_in = [sem(f"w_in_in{c}") for c in range(N_CHUNKS)]
        branch_in = [sem("branch_swa_in"), sem("branch_moba_in")]
        w_out_in = [sem("w_out_in0"), sem("w_out_in1")]
        shared_in, sinks_in, router_in, bias_in = sem("shared_in"), sem("sinks_in"), sem("router_in"), sem("bias_in")
        ln1_in, ln2_in = sem("ln1_in"), sem("ln2_in")
        gate_up_in = [sem(f"gate_up_in{s}") for s in range(RING)]
        down_in = [sem(f"down_in{s}") for s in range(RING)]
        out_done = sem("out_done")
        const_step, const_ready = sem("const_step"), sem("const_ready")
        dve_step, act_step = sem("dve_step"), sem("act_step")
        x_turned, xT_act, xT_dve = sem("x_turned"), sem("xT_act"), sem("xT_dve")
        proj_done, proj_act, proj_dve = sem("proj_done"), sem("proj_act"), sem("proj_dve")
        scores_done, biased_done, max_done, exp_done = sem("scores_done"), sem("biased_done"), sem("max_done"), sem("exp_done")
        prob_ready, prob_turned, probT_ready = sem("prob_ready"), sem("prob_turned"), sem("probT_ready")
        pv_done, att_ready = sem("pv_done"), sem("att_ready")
        branch_done, mix_ready, w_out_done = sem("branch_done"), sem("mix_ready"), sem("w_out_done")
        ln_var_ready, ln_root_ready, ln_stat, ln_norm, ln_gain, ln_ready = sem("ln_var_ready"), sem("ln_root_ready"), sem("ln_stat"), sem("ln_norm"), sem("ln_gain"), sem("ln_ready")
        h_turned, hT_act, hT_dve = sem("h_turned"), sem("hT_act"), sem("hT_dve")
        logits_done, logit_exp = sem("logits_done"), sem("logit_exp")
        chosen_ready, lines_done, over_ready = sem("chosen_ready"), sem("lines_done"), sem("over_ready")
        shared_gu, shared_silu, shared_hid, shared_done = sem("shared_gu"), sem("shared_silu"), sem("shared_hid"), sem("shared_done")
        choose_ready, choose_w_ready = sem("choose_ready"), sem("choose_w_ready")
        gather_lo, gather_hi, xg_lo, xg_hi = sem("gather_lo"), sem("gather_hi"), sem("xg_lo"), sem("xg_hi")
        gate_up_done, silu_done, hid_ready = sem("gate_up_done"), sem("silu_done"), sem("hid_ready")
        turned, turned_ready = sem("turned"), sem("turned_ready")
        down_lo, down_hi, y_lo, y_hi = sem("down_lo"), sem("down_hi"), sem("y_lo"), sem("y_hi")
        moe_done, round_ready = sem("moe_done"), sem("round_ready")

        R_LO, R_HI, R_GU, R_T = bank[0], bank[1], bank[2], bank[3]
        acc = [bank[4], bank[5], bank[6], bank[7]]
        w_out_bank = [bank[0], bank[1], bank[6], bank[7]]

        def slot_gate(s):
            return ring[:, s, 0:W_UP].rearrange("p (k f) -> p k f", k=KC)

        def slot_up(s):
            return ring[:, s, W_UP:W_DOWN].rearrange("p (k f) -> p k f", k=KC)

        def slot_gate_up(s):
            return ring[:, s, 0:W_DOWN].rearrange("p (g k f) -> p k g f", g=2, k=KC)

        def slot_down(s):
            return ring[:, s, W_DOWN:SLOT].rearrange("p (c n) -> p c n", c=FF // P)

        def chunk_view(c):
            w = min(CHUNK, IN_COLS - c * CHUNK)
            return ring[:, c, 0:KC * w].rearrange("p (k n) -> p k n", k=KC), w

        block = ctx.enter_context(nc.Block())

        PER_ROUND = [len(range(s, PAIRS, UNROLL)) for s in range(UNROLL)]

        def unit_outputs():
            res = []
            for u in range(QKV_UNITS):
                b = bank[u % 2]
                if u < 4:
                    res.append((q_swa[:, u, :], b[:, 0:SEQ]))
                elif u == 4:
                    res.append((k_swa, b[:, 0:SEQ]))
                elif u == 5:
                    res.append((v_swa, b[:, 0:SEQ].rearrange("p (t n) -> p t n", t=TILES)))
                elif u < 10:
                    res.append((q_moba[:, u - 6, :], b[:, 0:SEQ]))
                elif u < 14:
                    res.append((k_moba[:, u - 10, :], b[:, 0:SEQ]))
                else:
                    res.append((v_moba[:, u - 14, :], b[:, :]))
            return res

        @block.sync
        def _(sp):
            def load_expert(e, slot):
                sp.dma_start(slot_gate(slot), w_exp_gate[0, e].rearrange("(k p) f -> p k f", p=P)).then_inc(gate_up_in[slot], 16)
                sp.dma_start(slot_up(slot), w_exp_up[0, e].rearrange("(k p) f -> p k f", p=P)).then_inc(gate_up_in[slot], 16)
                sp.dma_start(slot_down(slot), w_exp_down[0, e].rearrange("(c p) n -> p c n", p=P)).then_inc(down_in[slot], 16)

            def load_pair(q, j, rnd):
                sp.wait_ge(down_hi, rnd * PAIRS + q - (UNROLL - 1))
                for i in range(2):
                    load_expert(2 * q + i, 2 * j + i)

            sp.dma_start(h_sb[:, 0, :], x[0, 0:P, :]).then_inc(x_in[0], 16)
            w_in_v = w_in[0].rearrange("(k p) n -> p k n", p=P)
            for c in range(N_CHUNKS):
                v, w = chunk_view(c)
                sp.dma_start(v, w_in_v[:, :, c * CHUNK:c * CHUNK + w]).then_inc(w_in_in[c], 16)
            sp.wait_ge(proj_done, 6)
            b0 = ring[:, 0, 0:4 * D].rearrange("p (c n) -> p c n", c=4)
            for i in range(2):
                sp.dma_start(b0[64 * i:64 * i + 64], w_branch_swa[0, 256 * i:256 * i + 256].rearrange("(c p) n -> p c n", p=64)).then_inc(branch_in[0], 16)
            sp.wait_ge(proj_done, 12)
            sp.dma_start(ring[:, 1, 0:4 * D].rearrange("p (c n) -> p c n", c=4),
                         w_branch_moba[0].rearrange("(c p) n -> p c n", p=P)).then_inc(branch_in[1], 16)
            w_out_v = w_out[0].rearrange("(k p) n -> p k n", p=P)
            sp.wait_ge(proj_done, QKV_UNITS)
            sp.dma_start(ring[:, 2, :].rearrange("p (k n) -> p k n", k=6), w_out_v[:, 0:6]).then_inc(w_out_in[0], 16)
            sp.wait_ge(proj_done, QKV_UNITS + 6)
            sp.dma_start(ring[:, 3, 0:2 * D].rearrange("p (k n) -> p k n", k=2), w_out_v[:, 6:8]).then_inc(w_out_in[1], 16)
            sp.wait_ge(proj_done, QKV_UNITS + 12)
            sp.dma_start(slot_gate(4), w_sh_gate[0].rearrange("(k p) f -> p k f", p=P)).then_inc(shared_in, 16)
            sp.dma_start(slot_up(4), w_sh_up[0].rearrange("(k p) f -> p k f", p=P)).then_inc(shared_in, 16)
            sp.dma_start(slot_down(4), w_sh_down[0].rearrange("(c p) n -> p c n", p=P)).then_inc(shared_in, 16)
            sp.wait_ge(att_ready, HEAD_PAIRS)
            sp.wait_ge(proj_done, UNITS)
            for i, v in enumerate((ln1_g, ln1_b)):
                sp.dma_start(ln1_gb[:, i, :], v[0:1, :].partition_broadcast(P)).then_inc(ln1_in, 16)
            load_expert(5, 5)
            sp.wait_ge(branch_done, KC)
            for e in (0, 1):
                load_expert(e, e)
            sp.wait_ge(w_out_done, 2)
            for e in (2, 3):
                load_expert(e, e)
            sp.wait_ge(shared_done, 1)
            load_expert(4, 4)

            def load_rest(rnd):
                turns = (PAIRS - LOADS_PEELED) // UNROLL
                with sp.Fori(1, 1 + turns) as it:
                    for j in range(UNROLL):
                        load_pair(it * UNROLL + j, j, rnd)
                for q in range(LOADS_PEELED + turns * UNROLL, PAIRS):
                    load_pair(q, q % UNROLL, rnd)

            load_rest(0)
            sp.wait_ge(over_ready, 1)
            more = sp.value_load(over[0:1, 0:1], min_val=0, max_val=1)
            with sp.If(more == 1):
                with sp.Fori(1, ROUNDS) as rnd:
                    sp.wait_ge(down_hi, rnd * PAIRS)
                    for q in range(LOADS_PEELED):
                        for i in range(2):
                            load_expert(2 * q + i, 2 * q + i)
                    load_rest(rnd)
                sp.wait_ge(down_hi, ROUNDS * PAIRS)
            sp.wait_ge(down_hi, PAIRS - 2)
            for i, v in enumerate((ln2_g, ln2_b)):
                sp.dma_start(ln2_gb[:, i, :], v[0:1, :].partition_broadcast(P)).then_inc(ln2_in, 16)
            for t in range(TILES):
                sp.wait_ge(ln_ready, TILES + t + 1)
                sp.dma_start(out[0, t * P:(t + 1) * P, :], h_sb[:, t, :]).then_inc(out_done, 16)
            sp.wait_ge(out_done, 16 * TILES)

        @block.gpsimd
        def _(pool):
            n = 0

            def step(ins):
                nonlocal n
                n += 1
                ins.then_inc(const_step, 1)
                pool.wait_ge(const_step, n)

            step(pool.memset(ident[:, :], 0.0))
            pool.affine_select(out=ident[:, :], in_=ident[:, :], compare_op=ALU.not_equal, fill=1.0,
                               base=0, pattern=[[-1, P]], channel_multiplier=1).then_inc(const_ready, 1)
            for dist in (dist_swa, dist_moba):
                step(pool.iota(dist[:, 0:256], [[1, 256]], base=-P, channel_multiplier=-1, allow_small_or_imprecise_dtypes=True))
                step(pool.iota(dist[:, 256:384], [[1, P]], base=0, channel_multiplier=-1, allow_small_or_imprecise_dtypes=True))
                step(pool.affine_select(out=dist[:, 0:256], in_=dist[:, 0:256], compare_op=ALU.is_ge, fill=NEG_INF,
                                        base=P, pattern=[[-1, 256]], channel_multiplier=1))
                step(pool.affine_select(out=dist[:, 256:384], in_=dist[:, 256:384], compare_op=ALU.is_ge, fill=NEG_INF,
                                        base=0, pattern=[[-1, P]], channel_multiplier=1))
            step(pool.affine_select(out=dist_swa[:, 0:256], in_=dist_swa[:, 0:256], compare_op=ALU.is_gt, fill=NEG_INF,
                                    base=0, pattern=[[1, 256]], channel_multiplier=-1))
            step(pool.memset(ones[:, :], 1.0))
            step(pool.affine_select(out=before[:, :], in_=ones[:, :], compare_op=ALU.is_gt, fill=0.0,
                                    base=0, pattern=[[1, P]], channel_multiplier=-1))
            pool.iota(place_ids[:, :], [[1, SLOTS]], base=1, channel_multiplier=0,
                      allow_small_or_imprecise_dtypes=True).then_inc(const_ready, 1)
            for l, (gb, loaded) in enumerate(((ln1_gb, ln1_in), (ln2_gb, ln2_in))):
                pool.wait_ge(loaded, 32)
                for t in range(TILES):
                    pool.wait_ge(ln_gain, l * TILES + t + 1)
                    pool.tensor_tensor(h_sb[:, t, :], h_sb[:, t, :], gb[:, 1, :], ALU.add).then_inc(ln_ready, 1)

        @block.scalar
        def _(act):
            act.dma_start(h_sb[:, 1, :], x[0, P:2 * P, :]).then_inc(x_in[1], 16)
            act.dma_start(sinks, swa_sinks[0:1, :].partition_broadcast(P)).then_inc(sinks_in, 16)
            act.dma_start(wr_sb[:, :, :], w_router[0].rearrange("(k p) e -> p k e", p=P)).then_inc(router_in, 16)
            for t in range(TILES):
                act.wait_ge(x_turned, 2 * t + 1)
                act.activation(hT[:, 0:4, t * P:(t + 1) * P], bank[4 + 2 * t][:, :].rearrange("p (k n) -> p k n", k=4),
                               ACT.Copy).then_inc(xT_act, 1)
            units = unit_outputs()
            for u in range(0, QKV_UNITS, 2):
                act.wait_ge(proj_done, u + 1)
                act.activation(units[u][0], units[u][1], ACT.Copy).then_inc(proj_act, 1)
            act.wait_ge(sinks_in, 16)
            for pr in range(HEAD_PAIRS):
                for h in range(2):
                    i = 2 * pr + h
                    act.wait_ge(max_done, i + 1)
                    for part, cols in enumerate((slice(0, 256), slice(256, 384))):
                        p_ap = prob[:, pr % 2, h, cols]
                        last = act.activation(p_ap, p_ap, ACT.Exp, bias=neg_max[:, i, part:part + 1], scale=ATT_SCALE,
                                              accum_out=row_sum[:, i, part:part + 1])
                    if pr < SWA_PAIRS:
                        head = heads_of(pr)[h][1]
                        last = act.activation(sink_exp[:, i, :], neg_max[:, i, :], ACT.Exp, bias=sinks[:, head:head + 1])
                    last.then_inc(exp_done, 1)
                for g in (2 * pr, 2 * pr + 1):
                    act.wait_ge(proj_done, QKV_UNITS + g + 1)
                    act.activation(gates[:, g, :], bank[g % 2][:, 0:SEQ], ACT.Exp, scale=-1.0).then_inc(proj_act, 1)
                for h in range(2):
                    act.wait_ge(prob_turned, 2 * pr + h + 1)
                    if pr >= 2:
                        act.wait_ge(pv_done, pr - 1)
                    act.activation(probT[:, pr % 2, h, :], bank[5 + h][:, 0:384], ACT.Copy).then_inc(probT_ready, 1)

            def normalise(l):
                act.wait_ge(ln_var_ready, l + 1)
                act.activation(ln_root, ln_var, ACT.Sqrt).then_inc(ln_root_ready, 1)
                act.wait_ge(ln_stat, l + 1)
                for t in range(TILES):
                    act.activation(h_sb[:, t, :], h_sb[:, t, :], ACT.Identity, bias=ln_shift[:, t, :],
                                   scale=ln_rstd[:, t, :]).then_inc(ln_norm, 1)

            normalise(0)
            act.dma_start(bias_r, router_bias[0:1, :].partition_broadcast(P)).then_inc(bias_in, 16)
            for t in range(TILES):
                act.wait_ge(h_turned, 2 * t + 1)
                act.activation(hT[:, 0:4, t * P:(t + 1) * P], bank[2 + 2 * t][:, :].rearrange("p (k n) -> p k n", k=4),
                               ACT.Copy).then_inc(hT_act, 1)
            act.wait_ge(logits_done, 1)
            act.activation(r_exp, bank[0][:, 0:2 * P].rearrange("p (t e) -> p t e", t=TILES)[:, :, 0:N_EXPERTS],
                           ACT.Exp, scale=-1.0).then_inc(logit_exp, 1)
            for c in range(2):
                act.wait_ge(shared_gu, c + 1)
                act.activation(sh_silu[:, c, :], bank[4 + 2 * c][:, 0:SEQ], ACT.Silu).then_inc(shared_silu, 1)

            def take_lo(n, rnd):
                act.wait_ge(gather_lo, rnd * PAIRS + n + 1)
                act.activation(xg[:, 0:4, :], R_LO[:, :].rearrange("p (k n) -> p k n", k=4), ACT.Copy).then_inc(xg_lo, 1)

            def take_turned(p, j, rnd, cols):
                act.wait_ge(turned, rnd * (PAIRS + 1) + p + 2)
                act.activation(turned_sb[j][:, cols], R_T[:, cols], ACT.Copy).then_inc(turned_ready, 1)

            def pair(p, j, rnd, last):
                act.wait_ge(gate_up_done, rnd * PAIRS + p + 1)
                if not (isinstance(p, int) and isinstance(rnd, int) and p + rnd == 0):
                    act.wait_ge(hid_ready, rnd * PAIRS + p)
                act.activation(silu_sb, R_GU[:, 0:FF], ACT.Silu).then_inc(silu_done, 1)
                if not last:
                    take_lo(p + 1, rnd)
                take_turned(p, j, rnd, slice(0, 256 if last else 512))
                act.wait_ge(down_lo, rnd * PAIRS + p + 1)
                act.activation(y_sb[:, 0:512], R_LO[:, :], ACT.Copy).then_inc(y_lo, 1)

            def all_pairs(rnd):
                take_lo(0, rnd)
                take_turned(-1, UNROLL - 1, rnd, slice(256, 512))
                pair(0, 0, rnd, False)
                with act.Fori(0, (PAIRS - 2) // UNROLL) as it:
                    for i in range(UNROLL):
                        pair(it * UNROLL + (1 + i), (1 + i) % UNROLL, rnd, False)
                pair(PAIRS - 1, (PAIRS - 1) % UNROLL, rnd, True)

            all_pairs(0)
            more = act.value_load(over[0:1, 0:1], min_val=0, max_val=1)
            with act.If(more == 1):
                with act.Fori(1, ROUNDS) as rnd:
                    all_pairs(rnd)
            normalise(1)

        @block.vector
        def _(dve):
            n = 0

            def step(ins):
                nonlocal n
                n += 1
                ins.then_inc(dve_step, 1)
                dve.wait_ge(dve_step, n)

            for t in range(TILES):
                dve.wait_ge(x_turned, 2 * t + 2)
                dve.tensor_copy(hT[:, 4:8, t * P:(t + 1) * P],
                                bank[5 + 2 * t][:, :].rearrange("p (k n) -> p k n", k=4)).then_inc(xT_dve, 1)
            units = unit_outputs()
            for u in range(1, QKV_UNITS, 2):
                dve.wait_ge(proj_done, u + 1)
                dve.tensor_copy(units[u][0], units[u][1]).then_inc(proj_dve, 1)
            dve.wait_ge(sinks_in, 16)
            step(dve.tensor_scalar(sinks8, sinks, 1.0 / ATT_SCALE, None, ALU.mult))
            dve.wait_ge(const_ready, 2)

            def take_att(pr):
                att = q_swa[:, pr, :] if pr < SWA_PAIRS else q_moba[:, pr - SWA_PAIRS, :]
                dve.wait_ge(pv_done, pr + 1)
                dve.tensor_copy(att, bank[4][:, 0:SEQ]).then_inc(att_ready, 1)

            parts = (slice(0, 256), slice(256, 384))
            for pr in range(HEAD_PAIRS):
                dist = dist_swa if pr < SWA_PAIRS else dist_moba
                for h, (slope, head) in enumerate(heads_of(pr)):
                    i = 2 * pr + h
                    p_ap = prob[:, pr % 2, h, :]
                    dve.wait_ge(scores_done, i + 1)
                    if pr >= 2:
                        dve.wait_ge(prob_turned, i - 3)
                    dve.scalar_tensor_tensor(out=p_ap, in0=dist[:, :], scalar=SLOPES[slope] / ATT_SCALE,
                                             in1=bank[2 + h][:, 0:384], op0=ALU.mult, op1=ALU.add).then_inc(biased_done, 1)
                    dve.wait_ge(biased_done, i + 1)
                    for part, cols in enumerate(parts):
                        last = dve.tensor_reduce(row_max[:, i, part:part + 1], p_ap[:, cols], AX_X, ALU.max)
                    step(last)
                    if pr < SWA_PAIRS:
                        dve.tensor_scalar(neg_max[:, i, :], row_max[:, i, :], sinks8[:, head:head + 1], -ATT_SCALE,
                                          ALU.max, ALU.mult).then_inc(max_done, 1)
                    else:
                        dve.tensor_scalar(neg_max[:, i, :], row_max[:, i, :], -ATT_SCALE, None, ALU.mult).then_inc(max_done, 1)
                if pr >= 1:
                    take_att(pr - 1)
                for h in range(2):
                    i = 2 * pr + h
                    dve.wait_ge(exp_done, i + 1)
                    if pr < SWA_PAIRS:
                        step(dve.tensor_tensor(row_sum[:, i, :], row_sum[:, i, :], sink_exp[:, i, :], ALU.add))
                    step(dve.reciprocal(inv_sum[:, i, :], row_sum[:, i, :]))
                    for part, cols in enumerate(parts):
                        p_ap = prob[:, pr % 2, h, cols]
                        last = dve.tensor_scalar(p_ap, p_ap, inv_sum[:, i, part:part + 1], None, ALU.mult)
                    last.then_inc(prob_ready, 1)
                dve.wait_ge(proj_act, QKV_UNITS // 2 + 2 * pr + 2)
                g = gates[:, 2 * pr:2 * pr + 2, :]
                step(dve.tensor_scalar(g, g, 1.0, None, ALU.add))
                step(dve.reciprocal(g, g))
            take_att(HEAD_PAIRS - 1)

            for j in range(KC):
                dve.wait_ge(branch_done, j + 1)
                for b in range(2):
                    g = gates[:, KC * b + j, :]
                    last = dve.tensor_tensor(g, g, bank[2 + 2 * (j % 2) + b][:, 0:SEQ], ALU.mult)
                step(last)
                dve.tensor_tensor(gates[:, j, :], gates[:, j, :], gates[:, KC + j, :], ALU.add).then_inc(mix_ready, 1)

            def layer_norm(l, gb, loaded, banks):
                for t in range(TILES):
                    for half in range(2):
                        cols = slice(512 * half, 512 * half + 512)
                        last = dve.scalar_tensor_tensor(out=h_sb[:, t, cols], in0=h_sb[:, t, cols], scalar=ALPHA,
                                                        in1=banks[2 * t + half][:, :], op0=ALU.mult, op1=ALU.add)
                    step(last)
                    for half in range(2):
                        last = dve.bn_stats(ln_stats[:, t, 6 * half:6 * half + 6], h_sb[:, t, 512 * half:512 * half + 512])
                    step(last)
                    step(dve.bn_aggr(ln_mv[:, t, :], ln_stats[:, t, :]))
                dve.tensor_scalar(ln_var, ln_mv[:, :, 1:2], LN_EPS, None, ALU.add).then_inc(ln_var_ready, 1)
                dve.wait_ge(ln_root_ready, l + 1)
                step(dve.reciprocal(ln_rstd, ln_root))
                dve.scalar_tensor_tensor(out=ln_shift, in0=ln_mv[:, :, 0:1], scalar=-1.0, in1=ln_rstd,
                                         op0=ALU.mult, op1=ALU.mult).then_inc(ln_stat, 1)
                dve.wait_ge(loaded, 32)
                for t in range(TILES):
                    dve.wait_ge(ln_norm, l * TILES + t + 1)
                    dve.tensor_tensor(h_sb[:, t, :], h_sb[:, t, :], gb[:, 0, :], ALU.mult).then_inc(ln_gain, 1)

            dve.wait_ge(w_out_done, 2)
            layer_norm(0, ln1_gb, ln1_in, w_out_bank)

            dve.memset(group_sum, -BIG)
            dve.memset(group_pick, -BIG)
            dve.memset(weight, 0.0)
            step(dve.memset(place, 0.0))

            for t in range(TILES):
                dve.wait_ge(h_turned, 2 * t + 2)
                dve.tensor_copy(hT[:, 4:8, t * P:(t + 1) * P],
                                bank[3 + 2 * t][:, :].rearrange("p (k n) -> p k n", k=4)).then_inc(hT_dve, 1)

            dve.wait_ge(logit_exp, 1)
            step(dve.tensor_scalar(r_one, r_exp, 1.0, None, ALU.add))
            step(dve.reciprocal(score, r_one))
            dve.wait_ge(bias_in, 16)
            step(dve.tensor_tensor(biased, score, bias_r.unsqueeze(1).to_broadcast([P, TILES, N_EXPERTS]), ALU.add))
            groups = biased.rearrange("p t (g e) -> p (t g) e", e=PER_GROUP)
            for g in range(TILES * N_GROUPS):
                last = dve.max(top_in_group[:, g, :], groups[:, g, :])
            step(last)
            top2 = top_in_group.rearrange("p (t g) e -> p t g e", t=TILES)
            step(dve.tensor_tensor(group_sum[:, :, 0:N_GROUPS], top2[:, :, :, 0], top2[:, :, :, 1], ALU.add))
            for t in range(TILES):
                last = dve.max(group_top[:, t, :], group_sum[:, t, :])
            step(last)
            step(dve.tensor_copy(group_pick[:, :, 0:TOPK_GROUPS], group_top[:, :, 0:TOPK_GROUPS]))
            for t in range(TILES):
                last = dve.match_replace(out=group_marked[:, t, :], in_to_replace=group_pick[:, t, :],
                                         in_values=group_sum[:, t, :], imm_value=BIG)
            step(last)
            step(dve.tensor_scalar(group_on.rearrange("p (t g) o -> p t (g o)", t=TILES), group_marked[:, :, 0:N_GROUPS],
                                   BIG, None, ALU.is_equal))
            step(dve.tensor_scalar(group_off, group_on, -NEG_INF, NEG_INF, ALU.mult, ALU.add))
            spread = [P, TILES * N_GROUPS, PER_GROUP]
            masked_g = masked.rearrange("p t (g e) -> p (t g) e", e=PER_GROUP)
            masked_sum_g = masked_sum.rearrange("p t (g e) -> p (t g) e", e=PER_GROUP)
            step(dve.tensor_tensor(masked_g, groups, group_on.to_broadcast(spread), ALU.mult))
            step(dve.tensor_tensor(masked_sum_g, masked_g, group_off.to_broadcast(spread), ALU.add))
            for t in range(TILES):
                last = dve.max(expert_top[:, t, :], masked_sum[:, t, :])
            step(last)
            for t in range(TILES):
                last = dve.match_replace(out=expert_marked[:, t, :], in_to_replace=expert_top[:, t, :],
                                         in_values=masked_sum[:, t, :], imm_value=BIG)
            step(last)
            dve.tensor_scalar(chosen, expert_marked, BIG, None, ALU.is_equal).then_inc(chosen_ready, 1)
            dve.wait_ge(chosen_ready, 1)
            step(dve.tensor_tensor(masked, score, chosen, ALU.mult))
            step(dve.tensor_reduce(weight_sum, masked, AX_X, ALU.add))
            step(dve.reciprocal(weight_inv, weight_sum))
            for t in range(TILES):
                last = dve.tensor_scalar(weight[:, t, 0:N_EXPERTS], masked[:, t, :], weight_inv[:, t, :], ROUTED_SCALE,
                                         ALU.mult, ALU.mult)
            step(last)

            for c in range(2):
                dve.wait_ge(shared_silu, c + 1)
                dve.tensor_tensor(sh_hidT[:, c, :], sh_silu[:, c, :], bank[5 + 2 * c][:, 0:SEQ], ALU.mult).then_inc(shared_hid, 1)

            dve.wait_ge(lines_done, 1)
            lines = bank[3][:, 0:3 * N_EXPERTS].rearrange("p (t e) -> p t e", t=3)
            dve.scalar_tensor_tensor(out=place[:, :, 0:N_EXPERTS], in0=lines[:, 0:TILES, :], scalar=1.0, in1=chosen,
                                     op0=ALU.add, op1=ALU.mult)
            step(dve.tensor_reduce(most, lines[:, TILES, :], AX_X, ALU.max))
            step(dve.tensor_scalar(over_f, most, SLOTS + 0.5, None, ALU.is_gt))
            dve.tensor_copy(over, over_f).then_inc(over_ready, 1)
            dve.wait_ge(const_ready, 2)

            def choose_for(q, j):
                shape = [P, TILES, 2, SLOTS]
                dve.tensor_tensor(choose[j].rearrange("p t (e s) -> p t e s", e=2),
                                  place[:, :, bass.ds(2 * q, 2)].unsqueeze(3).to_broadcast(shape),
                                  place_ids[:, :].unsqueeze(1).unsqueeze(1).to_broadcast(shape), ALU.is_equal).then_inc(choose_ready, 1)

            def weigh(q, j, rnd):
                shape = [P, TILES, 2, SLOTS]
                dve.wait_ge(choose_ready, rnd * (PAIRS + 1) + q + 1)
                dve.tensor_tensor(choose_w[j].rearrange("p t (e s) -> p t e s", e=2),
                                  weight[:, :, bass.ds(2 * q, 2)].unsqueeze(3).to_broadcast(shape),
                                  choose[j].rearrange("p t (e s) -> p t e s", e=2), ALU.mult).then_inc(choose_w_ready, 1)

            def take_hi(q, rnd):
                dve.wait_ge(gather_hi, rnd * PAIRS + q + 1)
                dve.tensor_copy(xg[:, 4:8, :], R_HI[:, :].rearrange("p (k n) -> p k n", k=4)).then_inc(xg_hi, 1)

            def pair(p, j, rnd, last):
                if not last:
                    if not (isinstance(p, int) and isinstance(rnd, int) and p + rnd == 0):
                        dve.wait_ge(turned, rnd * (PAIRS + 1) + p)
                    choose_for(p + 2, (j + 2) % UNROLL)
                dve.wait_ge(silu_done, rnd * PAIRS + p + 1)
                dve.tensor_tensor(hid, silu_sb, R_GU[:, FF:2 * FF], ALU.mult).then_inc(hid_ready, 1)
                if not last:
                    weigh(p + 2, (j + 2) % UNROLL, rnd)
                    take_hi(p + 1, rnd)
                dve.wait_ge(down_hi, rnd * PAIRS + p + 1)
                dve.tensor_copy(y_sb[:, 512:1024], R_HI[:, :]).then_inc(y_hi, 1)

            def all_pairs(rnd):
                for q in range(2):
                    choose_for(q, q)
                    weigh(q, q, rnd)
                take_hi(0, rnd)
                pair(0, 0, rnd, False)
                with dve.Fori(0, (PAIRS - 2) // UNROLL) as it:
                    for i in range(UNROLL):
                        pair(it * UNROLL + (1 + i), (1 + i) % UNROLL, rnd, False)
                pair(PAIRS - 1, (PAIRS - 1) % UNROLL, rnd, True)

            all_pairs(0)
            dve.wait_ge(over_ready, 1)
            more = dve.value_load(over[0:1, 0:1], min_val=0, max_val=1)
            with dve.If(more == 1):
                with dve.Fori(1, ROUNDS) as rnd:
                    dve.wait_ge(turned, rnd * (PAIRS + 1))
                    dve.tensor_scalar(place_ids[:, :], place_ids[:, :], float(SLOTS), None, ALU.add).then_inc(round_ready, 1)
                    dve.wait_ge(round_ready, rnd)
                    all_pairs(rnd)
            dve.wait_ge(moe_done, 1)
            layer_norm(1, ln2_gb, ln2_in, acc)

        @block.tensor
        def _(pe):
            def turn(banks, done):
                for t in range(TILES):
                    for g in range(2):
                        for kk in range(4):
                            k = 4 * g + kk
                            last = pe.transpose(banks[2 * t + g][:, kk * P:(kk + 1) * P], h_sb[:, t, k * P:(k + 1) * P], ident[:, :])
                        last.then_inc(done, 1)

            pe.wait_ge(const_ready, 1)
            for t in range(TILES):
                pe.wait_ge(x_in[t], 16)
            turn([bank[4], bank[5], bank[6], bank[7]], x_turned)
            pe.wait_ge(xT_act, 2)
            pe.wait_ge(xT_dve, 2)

            def project(u):
                b = bank[u % 2]
                if u >= 2:
                    who, count = evacuated(u - 2)
                    pe.wait_ge(proj_act if who == "act" else proj_dve, count)
                if u == 5:
                    w, _ = chunk_view(0)
                    for t in range(TILES):
                        for k in range(KC):
                            last = pe.matmul(b[:, t * P:(t + 1) * P], hT[:, k, t * P:(t + 1) * P], w[:, k, 640:768],
                                             start=(k == 0), stop=(k == KC - 1))
                elif u in (14, 15):
                    w, _ = chunk_view(2)
                    t = u - 14
                    for k in range(KC):
                        last = pe.matmul(b[:, :], hT[:, k, t * P:(t + 1) * P], w[:, k, 256:768],
                                         start=(k == 0), stop=(k == KC - 1))
                else:
                    if u < 5:
                        col = P * u
                    elif u < 14:
                        col = 768 + 128 * (u - 6)
                    else:
                        col = GATE_COL + P * (u - QKV_UNITS)
                    c, off = col // CHUNK, col % CHUNK
                    pe.wait_ge(w_in_in[c], 16)
                    w, _ = chunk_view(c)
                    for k in range(KC):
                        if u < SWA_PAIRS:
                            for g in range(2):
                                col = HEAD_DIM * (SWA_PAIRS * g + u)
                                last = pe.matmul(b[64 * g:64 * g + 64, 0:SEQ], w[:, k, col:col + HEAD_DIM], hT[:, k, :],
                                                 start=(k == 0), stop=(k == KC - 1))
                        else:
                            last = pe.matmul(b[:, 0:SEQ], w[:, k, off:off + P], hT[:, k, :],
                                             start=(k == 0), stop=(k == KC - 1))
                last.then_inc(proj_done, 1)

            for u in range(QKV_UNITS):
                project(u)

            def score(pr):
                q = q_swa[:, pr, :] if pr < SWA_PAIRS else q_moba[:, pr - SWA_PAIRS, :]
                k = k_swa if pr < SWA_PAIRS else k_moba[:, pr - SWA_PAIRS, :]
                for h in range(2):
                    rows = slice(64 * h, 64 * h + 64)
                    if pr >= 1:
                        pe.wait_ge(biased_done, 2 * (pr - 1) + h + 1)
                    pe.matmul(bank[2 + h][:, 0:256], q[rows, P:SEQ], k[rows, 0:SEQ], start=True, stop=True)
                    pe.matmul(bank[2 + h][:, 256:384], q[rows, 0:P], k[rows, 0:P], start=True, stop=True).then_inc(scores_done, 1)

            def turn_prob(pr):
                for h in range(2):
                    pe.wait_ge(prob_ready, 2 * pr + h + 1)
                    if pr >= 1:
                        pe.wait_ge(probT_ready, 2 * (pr - 1) + h + 1)
                    for to, fr in ((0, 256), (128, 0), (256, 128)):
                        last = pe.transpose(bank[5 + h][:, to:to + P], prob[:, pr % 2, h, fr:fr + P], ident[:, :])
                    last.then_inc(prob_turned, 1)

            def times_v(pr):
                pe.wait_ge(probT_ready, 2 * pr + 2)
                if pr >= 1:
                    pe.wait_ge(att_ready, pr)
                for h, (_, head) in enumerate(heads_of(pr)):
                    rows = slice(64 * h, 64 * h + 64)
                    if pr < SWA_PAIRS:
                        v = [v_swa[:, t, 64 * h:64 * h + 64] for t in range(TILES)]
                    else:
                        v = [v_moba[:, t, 64 * head:64 * head + 64] for t in range(TILES)]
                    pe.matmul(bank[4][rows, 0:SEQ], v[0], probT[:, pr % 2, h, 0:256], start=True, stop=False)
                    last = pe.matmul(bank[4][rows, P:SEQ], v[1], probT[:, pr % 2, h, 256:384], start=False, stop=True)
                last.then_inc(pv_done, 1)

            pe.wait_ge(proj_act, QKV_UNITS // 2)
            pe.wait_ge(proj_dve, QKV_UNITS // 2)
            for pr in range(HEAD_PAIRS):
                score(pr)
                if pr >= 1:
                    times_v(pr - 1)
                project(QKV_UNITS + 2 * pr)
                project(QKV_UNITS + 2 * pr + 1)
                turn_prob(pr)
            times_v(HEAD_PAIRS - 1)

            w_swa = ring[:, 0, 0:4 * D].rearrange("p (c n) -> p c n", c=4)
            w_moba = ring[:, 1, 0:4 * D].rearrange("p (c n) -> p c n", c=4)
            w_o = [ring[:, 2, :].rearrange("p (k n) -> p k n", k=6)[:, k, :] for k in range(6)]
            w_o += [ring[:, 3, 0:2 * D].rearrange("p (k n) -> p k n", k=2)[:, k, :] for k in range(2)]

            def project_out(k):
                pe.wait_ge(mix_ready, k + 1)
                for t in range(TILES):
                    for half in range(2):
                        last = pe.matmul(w_out_bank[2 * t + half][:, :], gates[:, k, t * P:(t + 1) * P],
                                         w_o[k][:, 512 * half:512 * half + 512], start=(k == 0), stop=(k == KC - 1))
                    if k == KC - 1:
                        last.then_inc(w_out_done, 1)

            pe.wait_ge(branch_in[0], 32)
            pe.wait_ge(branch_in[1], 16)
            pe.wait_ge(att_ready, HEAD_PAIRS)
            pe.wait_ge(biased_done, 2 * HEAD_PAIRS)
            for j in range(KC):
                if j >= 2:
                    pe.wait_ge(mix_ready, j - 1)
                for b, (w, att) in enumerate(((w_swa, q_swa), (w_moba, q_moba))):
                    for c in range(4):
                        last = pe.matmul(bank[2 + 2 * (j % 2) + b][:, 0:SEQ], w[:, c, j * P:(j + 1) * P], att[:, c, :],
                                         start=(c == 0), stop=(c == 3))
                last.then_inc(branch_done, 1)
                if j == 1:
                    pe.wait_ge(w_out_in[0], 16)
                    pe.wait_ge(w_out_in[1], 16)
                    pe.wait_ge(proj_act, QKV_UNITS // 2 + GATE_UNITS)
                if j >= 1:
                    project_out(j - 1)
            project_out(KC - 1)

            for t in range(TILES):
                pe.wait_ge(ln_ready, t + 1)
                for g in range(2):
                    for kk in range(4):
                        k = 4 * g + kk
                        last = pe.transpose(bank[2 + 2 * t + g][:, kk * P:(kk + 1) * P], h_sb[:, t, k * P:(k + 1) * P], ident[:, :])
                    last.then_inc(h_turned, 1)
            pe.wait_ge(hT_act, 2)
            pe.wait_ge(hT_dve, 2)
            pe.wait_ge(router_in, 16)
            for t in range(TILES):
                for k in range(KC):
                    last = pe.matmul(bank[0][:, t * P:(t + 1) * P], hT[:, k, t * P:(t + 1) * P],
                                     wr_sb[:, k, :].unsqueeze(1).to_broadcast([P, 2, N_EXPERTS]),
                                     start=(k == 0), stop=(k == KC - 1))
            last.then_inc(logits_done, 1)

            pe.wait_ge(shared_in, 48)
            for c in range(2):
                for i, w in enumerate((slot_gate(4), slot_up(4))):
                    for k in range(KC):
                        last = pe.matmul(bank[4 + 2 * c + i][:, 0:SEQ], w[:, k, c * P:(c + 1) * P], hT[:, k, :],
                                         start=(k == 0), stop=(k == KC - 1))
                last.then_inc(shared_gu, 1)
            pe.wait_ge(const_ready, 2)
            pe.wait_ge(chosen_ready, 1)
            cols = [slice(i * N_EXPERTS, (i + 1) * N_EXPERTS) for i in range(3)]
            pe.matmul(bank[3][:, cols[0]], before[:, :], chosen[:, 0, :], start=True, stop=True)
            pe.matmul(bank[3][:, cols[1]], ones[:, :], chosen[:, 0, :], start=True, stop=False)
            pe.matmul(bank[3][:, cols[1]], before[:, :], chosen[:, 1, :], start=False, stop=True)
            pe.matmul(bank[3][:, cols[2]], ones[:, :], chosen[:, 0, :], start=True, stop=False)
            pe.matmul(bank[3][:, cols[2]], ones[:, :], chosen[:, 1, :], start=False, stop=True).then_inc(lines_done, 1)
            pe.wait_ge(shared_hid, 2)
            for t in range(TILES):
                for half in range(2):
                    for c in range(2):
                        last = pe.matmul(acc[2 * t + half][:, :], sh_hidT[:, c, t * P:(t + 1) * P],
                                         slot_down(4)[:, c, 512 * half:512 * half + 512],
                                         start=(c == 0), stop=(c == 1))
            last.then_inc(shared_done, 1)

            def gather(q, j, rnd):
                pe.wait_ge(choose_ready, rnd * (PAIRS + 1) + q + 1)
                for g, (b, done) in enumerate(((R_LO, gather_lo), (R_HI, gather_hi))):
                    for kk in range(4):
                        k = 4 * g + kk
                        for t in range(TILES):
                            last = pe.matmul(b[:, kk * P:(kk + 1) * P], h_sb[:, t, k * P:(k + 1) * P], choose[j][:, t, :],
                                             start=(t == 0), stop=(t == TILES - 1))
                    last.then_inc(done, 1)

            def turn_choice(q, j, rnd):
                pe.wait_ge(choose_w_ready, rnd * (PAIRS + 1) + q + 1)
                for t in range(TILES):
                    last = pe.transpose(R_T[:, 256 + t * P:256 + (t + 1) * P], choose_w[j][:, t, :], ident[:, :])
                return last

            def scatter(j):
                tc = turned_sb[(j - 1) % UNROLL]
                for t in range(TILES):
                    for half in range(2):
                        last = pe.matmul(acc[2 * t + half][:, :], tc[:, 256 + t * P:256 + (t + 1) * P],
                                         y_sb[:, 512 * half:512 * half + 512], start=False, stop=False, skip_group_check=True)
                return last

            def pair(p, turn_no, j, rnd, first, last_pair):
                fill = rnd * PER_ROUND[j] + turn_no + 1
                for i in range(2):
                    pe.wait_ge(gate_up_in[2 * j + i], fill * 32)
                for k in range(KC):
                    for i in range(2):
                        last = pe.matmul(R_GU[64 * i:64 * i + 64, :], xg[:, k, 64 * i:64 * i + 64],
                                         slot_gate_up(2 * j + i)[:, k, :, :], start=(k == 0), stop=(k == KC - 1))
                last.then_inc(gate_up_done, 1)
                if not last_pair:
                    if not first:
                        pe.wait_ge(y_lo, rnd * PAIRS + p)
                        pe.wait_ge(y_hi, rnd * PAIRS + p)
                    gather(p + 1, (j + 1) % UNROLL, rnd)
                    turn_choice(p + 1, (j + 1) % UNROLL, rnd)
                pe.wait_ge(hid_ready, rnd * PAIRS + p + 1)
                for c in range(FF // P):
                    last = pe.transpose(R_T[:, c * P:(c + 1) * P], hid[:, c * P:(c + 1) * P], ident[:, :])
                last.then_inc(turned, 1)
                if not first:
                    if last_pair:
                        pe.wait_ge(y_lo, rnd * PAIRS + p)
                        pe.wait_ge(y_hi, rnd * PAIRS + p)
                    scatter((j - 1) % UNROLL)
                pe.wait_ge(turned_ready, rnd * (PAIRS + 1) + p + 2)
                if not last_pair:
                    pe.wait_ge(xg_lo, rnd * PAIRS + p + 2)
                    pe.wait_ge(xg_hi, rnd * PAIRS + p + 2)
                for i in range(2):
                    pe.wait_ge(down_in[2 * j + i], fill * 16)
                for half, (b, done) in enumerate(((R_LO, down_lo), (R_HI, down_hi))):
                    for c in range(FF // P):
                        for i in range(2):
                            last = pe.matmul(b[64 * i:64 * i + 64, :], turned_sb[j][:, c * P + 64 * i:c * P + 64 * i + 64],
                                             slot_down(2 * j + i)[:, c, 512 * half:512 * half + 512],
                                             start=(c == 0), stop=(c == FF // P - 1))
                    last.then_inc(done, 1)

            def all_pairs(rnd):
                gather(0, 0, rnd)
                turn_choice(0, 0, rnd).then_inc(turned, 1)
                pe.wait_ge(xg_lo, rnd * PAIRS + 1)
                pe.wait_ge(xg_hi, rnd * PAIRS + 1)
                pe.wait_ge(turned_ready, rnd * (PAIRS + 1) + 1)
                pair(0, 0, 0, rnd, True, False)
                with pe.Fori(0, (PAIRS - 2) // UNROLL) as it:
                    for i in range(UNROLL):
                        p = 1 + i
                        pair(it * UNROLL + p, it + p // UNROLL, p % UNROLL, rnd, False, False)
                last = PAIRS - 1
                pair(last, last // UNROLL, last % UNROLL, rnd, False, True)

            pe.wait_ge(over_ready, 1)
            all_pairs(0)
            more = pe.value_load(over[0:1, 0:1], min_val=0, max_val=1)
            with pe.If(more == 1):
                with pe.Fori(1, ROUNDS) as rnd:
                    pe.wait_ge(y_lo, rnd * PAIRS)
                    pe.wait_ge(y_hi, rnd * PAIRS)
                    scatter((PAIRS - 1) % UNROLL)
                    all_pairs(rnd)
                pe.wait_ge(y_lo, ROUNDS * PAIRS)
                pe.wait_ge(y_hi, ROUNDS * PAIRS)
            pe.wait_ge(y_lo, PAIRS)
            pe.wait_ge(y_hi, PAIRS)
            scatter((PAIRS - 1) % UNROLL).then_inc(moe_done, 1)


_INS = ["x", "w_in", "swa_sinks", "w_branch_swa", "w_branch_moba", "w_out", "ln1_g", "ln1_b", "w_router", "router_bias",
        "w_exp_gate", "w_exp_up", "w_exp_down", "w_sh_gate", "w_sh_up", "w_sh_down", "ln2_g", "ln2_b"]


def kernel(**inputs):
    import numpy as np
    import concourse.bacc as bacc
    from concourse.bass_utils import run_bass_kernel_spmd

    nc = bacc.Bacc("TRN2", target_bir_lowering=False, num_devices=1)
    arrays, args = {}, []
    for name in _INS:
        a = np.ascontiguousarray(inputs[name])
        arrays[f"in_{name}_dram"] = a
        args.append(nc.dram_tensor(f"in_{name}_dram", a.shape, mybir.dt.from_np(a.dtype), kind="ExternalInput").ap())
    out = nc.dram_tensor("out_0_dram", (1, SEQ, D), F32, kind="ExternalOutput").ap()
    block_program(nc, *args, out)
    r = run_bass_kernel_spmd(nc, [arrays], core_ids=[0])
    return r.results[0]["out_0_dram"]
```

```python
from contextlib import ExitStack

import concourse.bass as bass
from concourse import mybir

F32 = mybir.dt.float32
F32R = mybir.dt.float32r
BF16 = mybir.dt.bfloat16
I32 = mybir.dt.int32
ALU = mybir.AluOpType
ACT = mybir.ActivationFunctionType
AX_X = mybir.AxisListType.X

P = 128
SEQ = 256
TILES = SEQ // P
D = 1024
KC = D // P
HEAD_DIM = 64
SWA_HEADS = 8
MOBA_HEADS = 8
N_EXPERTS = 64
N_GROUPS = 8
PER_GROUP = N_EXPERTS // N_GROUPS
TOPK_GROUPS = 4
FF = 256
ROUTED_SCALE = 2.5
ALPHA = 2.0 ** 0.25
LN_EPS = 1e-5
NEG_INF = -1e30
BIG = 3e38

IN_COLS = 4352
CHUNK = 768
N_CHUNKS = -(-IN_COLS // CHUNK)
K_COL = 512
GATE_COL = 2304

RING = 6
SLOT = 3 * KC * FF
W_UP = KC * FF
W_DOWN = 2 * KC * FF
SLOTS = 64
PAIRS = N_EXPERTS // 2
ROUNDS = SEQ // SLOTS
UNROLL = RING // 2
LOADS_PEELED = UNROLL
EXTRA = 2


SWA_PAIRS = SWA_HEADS // 2
HEAD_PAIRS = (SWA_HEADS + MOBA_HEADS) // 2
SLOPES = [2.0 ** (-8.0 * (i + 1) / (SWA_HEADS + MOBA_HEADS)) for i in range(SWA_HEADS + MOBA_HEADS)]
ATT_SCALE = HEAD_DIM ** -0.5

QKV_UNITS = 16
GATE_UNITS = 2 * D // P
UNITS = QKV_UNITS + GATE_UNITS
FIRST_OF_CHUNK = (1, 2, 6, 12, 16, 22, 28)


def heads_of(pair):
    if pair < SWA_PAIRS:
        return [(pair, pair), (pair + SWA_PAIRS, pair + SWA_PAIRS)]
    c = pair - SWA_PAIRS
    return [(SWA_HEADS + 2 * c + i, 2 * c + i) for i in range(2)]


def ln_columns(layer_norm, tile):
    edge = 384 if (layer_norm, tile) == (1, 0) else 768
    return slice(0, edge), slice(edge, D)


def evacuated(unit):
    if unit < QKV_UNITS:
        return ("act" if unit % 2 == 0 else "dve"), unit // 2 + 1
    return "act", QKV_UNITS // 2 + unit - QKV_UNITS + 1


def block_program(nc, x, w_in, swa_sinks, w_branch_swa, w_branch_moba, w_out, ln1_g, ln1_b, w_router, router_bias,
                  w_exp_gate, w_exp_up, w_exp_down, w_sh_gate, w_sh_up, w_sh_down, ln2_g, ln2_b, out):
    with ExitStack() as ctx:
        def sem(name):
            return ctx.enter_context(nc.semaphore(name))

        bank = [ctx.enter_context(nc.psum_tensor(f"bank{i}", [P, 512], F32)) for i in range(8)]

        ring_at, h_at = 0, RING * SLOT
        const_at = h_at + TILES * D
        gates_at = const_at + 896
        work_at = gates_at + GATE_UNITS * SEQ
        sbuf_base = -(-nc.sbuf_base // 32) * 32
        sbuf_end = nc.sbuf_usable_end

        def at(name, offset, shape, dt=F32):
            n = mybir.dt.size(dt)
            for s in shape:
                n *= s
            assert sbuf_base + 4 * offset + n <= sbuf_end, name
            return nc.alloc_sbuf_tensor_at(name, [P, *shape], dt, offset=sbuf_base + 4 * offset)

        ring = at("ring", ring_at, [RING, SLOT])
        h_sb = at("h_sb", h_at, [TILES, D])
        ident = at("ident", const_at, [P])
        before = at("before", const_at + 128, [P], BF16)
        ones = at("ones", const_at + 192, [P], BF16)
        place_ids = at("place_ids", const_at + 256, [SLOTS])
        wr_sb = at("wr_sb", const_at + 320, [KC, N_EXPERTS])
        bias_r = at("bias_r", const_at + 832, [N_EXPERTS])[:, :]
        gates = at("gates", gates_at, [GATE_UNITS, SEQ])
        tables = at("tables", gates_at, [GATE_UNITS * SEQ])
        att = at("att", work_at, [HEAD_PAIRS, SEQ])
        q_swa, q_moba = att[:, 0:SWA_PAIRS, :], att[:, SWA_PAIRS:HEAD_PAIRS, :]
        k_swa = at("k_swa", work_at + 2048, [SEQ])[:, :]
        v_swa = at("v_swa", work_at + 2304, [TILES, P])[:, :, :]
        k_moba = at("k_moba", work_at + 2560, [4, SEQ])
        v_moba = at("v_moba", work_at + 3584, [TILES, 512])
        prob = at("prob", work_at + 4608, [2, 2, 384])
        hT = at("hT", work_at + 6144, [KC, SEQ])
        dist_swa = at("dist_swa", work_at + 8192, [384])
        dist_moba = at("dist_moba", work_at + 8576, [384])
        xT = at("xT", work_at + 2560, [KC, SEQ])
        xT_lo = at("xT_lo", work_at + 6144, [KC, SEQ], F32R)
        xT_hi = at("xT_hi", gates_at, [KC, SEQ], F32R)
        xT_hi_kept = at("xT_hi_kept", ring_at + SLOT + 4 * D, [KC, SEQ], F32R)
        chunk_lo = [at(f"chunk_lo{c}", ring_at + c * SLOT, [SLOT], F32R) for c in range(N_CHUNKS)]
        w_hi = [at(f"w_hi{i}", gates_at + KC * SEQ + i * D, [KC, P], F32R) for i in range(2)]
        w_hi += [at("w_hi2", ring_at + (RING - 1) * SLOT + W_DOWN, [KC, P], F32R)]
        w_hi_gate = [at(f"w_hi_gate{i}", ring_at + 2 * (i // 2) * SLOT + (4 + i % 2) * D, [KC, P], F32R) for i in range(4)]
        w_hi_v = [at("w_hi_v0", ring_at + 4 * D, [KC, SEQ], F32R), at("w_hi_v1", gates_at + KC * SEQ, [KC, SEQ], F32R)]
        q_lo = [at("q_lo0", work_at + 1024, [KC, P], F32R), at("q_lo1", work_at + 4608, [KC, P], F32R)]
        SLOT_3 = ring_at + 3 * SLOT
        att_lo = at("att_lo", work_at, [HEAD_PAIRS, SEQ], F32R)
        att_hi = at("att_hi", SLOT_3 + 2 * D, [HEAD_PAIRS, SEQ], F32R)
        mix_lo = at("mix_lo", gates_at, [KC, SEQ], F32R)
        mix_hi = at("mix_hi", gates_at + KC * SEQ, [KC, SEQ], F32R)
        branch_hi_at = [SLOT_3 + 4 * D, SLOT_3 + 5 * D, ring_at + 4 * D, ring_at + 5 * D, ring_at + SLOT + 4 * D, ring_at + SLOT + 5 * D]
        branch_hi = [at(f"branch_hi{i}", a, [KC, P], F32R) for i, a in enumerate(branch_hi_at)]
        out_hi_at = [work_at + 6144, work_at + 7168, work_at + 4608, SLOT_3 + 4 * D, SLOT_3 + 5 * D]
        out_hi = [at(f"out_hi{i}", a, [D], F32R) for i, a in enumerate(out_hi_at)]
        ln1_gb = at("ln1_gb", work_at + 2560, [2, D])
        sh_silu = at("sh_silu", work_at + 3072, [2, SEQ])
        sh_hidT = at("sh_hidT", work_at + 3584, [2, SEQ])
        h_part = [at(f"h_part{i}", work_at + 1024 * i, [TILES, D], BF16) for i in range(3)]
        y_top = at("y_top", work_at + 3072, [D], F32R)
        y_rest = at("y_rest", work_at + 4096, [D], F32R)
        choiceT = [at(f"choiceT{i}", work_at + 6272 + 256 * i, [SEQ], F32R) for i in range(3)]
        choose = [at(f"choose{i}", work_at + 5888 + 128 * i, [TILES, P], BF16) for i in range(3)]
        choose_w = [at(f"choose_w{i}", work_at + 5120 + 256 * i, [TILES, P]) for i in range(3)]
        xg = at("xg", work_at + 7040, [KC, P])
        silu_sb = at("silu_sb", work_at + 8064, [FF])
        hid = at("hid", work_at + 8320, [FF])
        hidT = at("hidT", work_at + 8576, [FF])
        choice_wT = at("choice_wT", work_at + 8832, [SEQ])

        def piece(base, at, shape):
            n = 1
            for s in shape:
                n *= s
            v = base[:, at:at + n]
            if len(shape) == 2:
                v = v.rearrange("p (a b) -> p a b", b=shape[1])
            if len(shape) == 3:
                v = v.rearrange("p (a b c) -> p a b c", b=shape[1], c=shape[2])
            return v

        tail = ring[:, RING - 1, W_DOWN:SLOT]
        probT = piece(tail, 0, (2, 2, 384))
        row_max = piece(tail, 1536, (16, 2))
        neg_max = piece(tail, 1568, (16, 2))
        row_sum = piece(tail, 1600, (16, 2))
        sink_exp = piece(tail, 1632, (16, 2))
        inv_sum = piece(tail, 1664, (16, 2))
        sinks = piece(tail, 1696, (SWA_HEADS,))
        sinks8 = piece(tail, 1704, (SWA_HEADS,))
        W66 = N_EXPERTS + EXTRA
        r_exp = piece(tables, 0, (TILES, N_EXPERTS))
        r_one = piece(tables, 128, (TILES, N_EXPERTS))
        score = piece(tables, 256, (TILES, N_EXPERTS))
        biased = piece(tables, 384, (TILES, N_EXPERTS))
        top_in_group = piece(tables, 512, (TILES * N_GROUPS, 8))
        group_sum = piece(tables, 640, (TILES, 2 * N_GROUPS))
        group_top = piece(tables, 672, (TILES, 8))
        group_pick = piece(tables, 688, (TILES, 8))
        group_marked = piece(tables, 704, (TILES, 2 * N_GROUPS))
        group_on = piece(tables, 736, (TILES * N_GROUPS, 1))
        group_off = piece(tables, 752, (TILES * N_GROUPS, 1))
        masked = piece(tables, 768, (TILES, N_EXPERTS))
        expert_top = piece(tables, 896, (TILES, 8))
        expert_marked = piece(tables, 912, (TILES, N_EXPERTS))
        weight_sum = piece(tables, 1040, (TILES, 1))
        weight_inv = piece(tables, 1042, (TILES, 1))
        most = piece(tables, 1044, (1,))
        over_f = piece(tables, 1045, (1,))
        over = piece(tables, 1046, (1,)).bitcast(I32)
        masked_sum = piece(tables, 1088, (TILES, N_EXPERTS))
        chosen = piece(tables, 1280, (TILES * N_EXPERTS // 2,)).bitcast(BF16).rearrange("p (t e) -> p t e", t=TILES)
        weight = piece(tables, 1408, (TILES, W66))
        place = piece(tables, 1544, (TILES, W66))
        place_weight = [piece(tables, 1680 + 2 * i, (1,)) for i in range(3)]
        h_rem = piece(tables, 1792, (TILES, D))
        ln_tables = at("ln_tables", work_at + 8192, [64])
        ln_stats = piece(ln_tables, 0, (TILES, 12))
        ln_mv = piece(ln_tables, 24, (TILES, 2))
        ln_rstd = piece(ln_tables, 28, (TILES, 1))
        ln_var = piece(ln_tables, 30, (TILES, 1))
        ln_root = piece(ln_tables, 32, (TILES, 1))
        ln_shift = piece(ln_tables, 34, (TILES, 1))
        unused = piece(ln_tables, 36, (1,))
        ln2_gb = piece(ring[:, RING - 2, :], 0, (2, D))


        x_in = [sem(f"x_in{t}") for t in range(TILES)]
        w_in_in = [sem(f"w_in_in{c}") for c in range(N_CHUNKS)]
        kv_swa_in = sem("kv_swa_in")
        branch_in = [sem("branch_swa_in"), sem("branch_moba_in")]
        w_out_in = [sem(f"w_out_in{i}") for i in range(3)]
        shared_in, sinks_in, router_in, bias_in = sem("shared_in"), sem("sinks_in"), sem("router_in"), sem("bias_in")
        ln1_in, ln2_in = sem("ln1_in"), sem("ln2_in")
        gate_up_in = [sem(f"gate_up_in{s}") for s in range(RING)]
        down_in = [sem(f"down_in{s}") for s in range(RING)]
        out_done = sem("out_done")
        pool_step, const_ready = sem("pool_step"), sem("const_ready")
        dve_step, act_step = sem("dve_step"), sem("act_step")
        x_turned, xT_act, xT_dve = sem("x_turned"), sem("xT_act"), sem("xT_dve")
        xT_hi_ready, xT_lo_ready, xT_kept = sem("xT_hi_ready"), sem("xT_lo_ready"), sem("xT_kept")
        w_hi_ready, w_lo_ready, w_lo_gate = sem("w_hi_ready"), sem("w_lo_ready"), sem("w_lo_gate")
        proj_done, proj_act, proj_dve = sem("proj_done"), sem("proj_act"), sem("proj_dve")
        scores_done, biased_done, max_done, exp_done = sem("scores_done"), sem("biased_done"), sem("max_done"), sem("exp_done")
        prob_ready, prob_turned, probT_ready = sem("prob_ready"), sem("prob_turned"), sem("probT_ready")
        gate_sum, gate_ready = sem("gate_sum"), sem("gate_ready")
        pv_done, att_ready = sem("pv_done"), sem("att_ready")
        att_hi_ready, att_lo_pool, att_lo_dve = sem("att_hi_ready"), sem("att_lo_pool"), sem("att_lo_dve")
        branch_hi_ready, branch_lo_ready = sem("branch_hi_ready"), sem("branch_lo_ready")
        out_hi_ready, out_lo_ready, out_step = sem("out_hi_ready"), sem("out_lo_ready"), sem("out_step")
        mixed, mix_hi_ready, mix_ready = sem("mixed"), sem("mix_hi_ready"), sem("mix_ready")
        branch_done, w_out_done = sem("branch_done"), sem("w_out_done")
        ln_var_ready, ln_root_ready, ln_rstd_ready, ln_norm = sem("ln_var_ready"), sem("ln_root_ready"), sem("ln_rstd_ready"), sem("ln_norm")
        ln_dve, ln_pool = sem("ln_dve"), sem("ln_pool")
        h_turned, hT_act, hT_dve = sem("h_turned"), sem("hT_act"), sem("hT_dve")
        logits_done, logit_exp = sem("logits_done"), sem("logit_exp")
        chosen_ready, lines_done, over_ready = sem("chosen_ready"), sem("lines_done"), sem("over_ready")
        shared_gu, shared_silu, shared_hid, shared_done = sem("shared_gu"), sem("shared_silu"), sem("shared_hid"), sem("shared_done")
        choose_ready, choose_w_ready = sem("choose_ready"), sem("choose_w_ready")
        gather_lo, gather_hi, xg_lo, xg_hi = sem("gather_lo"), sem("gather_hi"), sem("xg_lo"), sem("xg_hi")
        gate_up_done, silu_done, hid_ready = sem("gate_up_done"), sem("silu_done"), sem("hid_ready")
        turned, turned_ready = sem("turned"), sem("turned_ready")
        down_lo, down_hi, y_top_ready, y_ready = sem("down_lo"), sem("down_hi"), sem("y_top_ready"), sem("y_ready")
        choice_ready, part_ready, rem_ready = sem("choice_ready"), sem("part_ready"), sem("rem_ready")
        moe_done, round_ready = sem("moe_done"), sem("round_ready")

        R_LO, R_HI, R_GU, R_T = bank[0], bank[1], bank[2], bank[3]
        acc = [bank[4], bank[5], bank[6], bank[7]]
        w_out_bank = [bank[0], bank[1], bank[6], bank[7]]

        def static_zero(*counts):
            return all(isinstance(c, int) for c in counts) and sum(counts) == 0

        def slot_gate(s):
            return ring[:, s, 0:W_UP].rearrange("p (k f) -> p k f", k=KC)

        def slot_up(s):
            return ring[:, s, W_UP:W_DOWN].rearrange("p (k f) -> p k f", k=KC)

        def slot_gate_up(s):
            return ring[:, s, 0:W_DOWN].rearrange("p (g k f) -> p k g f", g=2, k=KC)

        def slot_down(s):
            return ring[:, s, W_DOWN:SLOT].rearrange("p (c n) -> p c n", c=FF // P)

        def chunk_view(c):
            w = min(CHUNK, IN_COLS - c * CHUNK)
            return ring[:, c, 0:KC * w].rearrange("p (k n) -> p k n", k=KC), w

        block = ctx.enter_context(nc.Block())

        PER_ROUND = [len(range(s, PAIRS, UNROLL)) for s in range(UNROLL)]

        def unit_outputs():
            res = []
            for u in range(QKV_UNITS):
                b = bank[u % 2]
                if u == 0:
                    res.append((v_swa, b[:, 0:SEQ].rearrange("p (t n) -> p t n", t=TILES)))
                elif u == 1:
                    res.append((k_swa, b[:, 0:SEQ]))
                elif u < 6:
                    res.append((q_swa[:, u - 2, :], b[:, 0:SEQ]))
                elif u < 10:
                    res.append((q_moba[:, u - 6, :], b[:, 0:SEQ]))
                elif u < 14:
                    res.append((k_moba[:, u - 10, :], b[:, 0:SEQ]))
                else:
                    half = slice(256 * (u - 14), 256 * (u - 13))
                    res.append((v_moba[:, :, half], b[:, :].rearrange("p (t n) -> p t n", t=TILES)))
            return res

        def unit_weights(u):
            if 2 <= u < 6:
                w, _ = chunk_view(0)
                w = w[:, :, 0:K_COL].rearrange("p k (g h d) -> p k g h d", g=2, h=SWA_PAIRS)[:, :, :, u - 2, :]
                return 0, w, w_hi[u % 3], q_lo[u % 2]
            if u == 1:
                col, width = K_COL, P
            elif u < 14:
                col, width = 768 + P * (u - 6), P
            elif u < QKV_UNITS:
                col, width = 1792 + 256 * (u - 14), 256
            else:
                col, width = GATE_COL + P * (u - QKV_UNITS), P
            c, off = col // CHUNK, col % CHUNK
            full = min(CHUNK, IN_COLS - c * CHUNK)
            lo = chunk_lo[c][:, 0:KC * full].rearrange("p (k n) -> p k n", k=KC)[:, :, off:off + width]
            hi = w_hi[u % 3] if u < 14 else w_hi_v[u - 14] if u < QKV_UNITS else w_hi_gate[u % 4]
            return c, chunk_view(c)[0][:, :, off:off + width], hi, lo

        def split_hi(act, u):
            c, w, hi, _ = unit_weights(u)
            if u in FIRST_OF_CHUNK:
                act.wait_ge(kv_swa_in if u == 1 else w_in_in[c], 16)
            done = 0 if u < 4 else u - 2 if u < 14 else 6 if u == 14 else 14 if u == 15 else 15 if u < 18 else 16 if u < 20 else u - 3
            if done:
                act.wait_ge(proj_done, done)
            if 2 <= u < 6:
                hi = hi[:, :, :].rearrange("p k (g d) -> p k g d", g=2)
            else:
                hi = hi[:, :, :]
            act.activation(hi, w, ACT.Copy).then_inc(w_hi_ready, 1)

        def split_lo(eng, u):
            _, w, hi, lo = unit_weights(u)
            eng.wait_ge(w_hi_ready, u)
            hi, lo = hi[:, :, :], lo[:, :, :]
            if 2 <= u < 6:
                hi = hi.rearrange("p k (g d) -> p k g d", g=2)
                lo = lo.rearrange("p k (g d) -> p k g d", g=2)
            if u in (4, 5):
                eng.wait_ge(proj_done, u - 1)
            eng.tensor_tensor(lo, w, hi.bitcast(F32), ALU.subtract).then_inc(w_lo_ready if u < QKV_UNITS else w_lo_gate, 1)

        def branch_weights(b, j):
            cols = slice(j * P, (j + 1) * P)
            return (ring[:, b, 0:4 * D].rearrange("p (c n) -> p c n", c=4)[:, :, cols],
                    chunk_lo[b][:, 0:4 * D].rearrange("p (c n) -> p c n", c=4)[:, :, cols])

        def out_weights(k):
            slot, row = (2, k) if k < 6 else (3, k - 6)
            return ring[:, slot, row * D:(row + 1) * D], chunk_lo[slot][:, row * D:(row + 1) * D]

        BRANCH_PLACE = [0, 1, 2, 3, 4, 5, 0, 1]
        OUT_PLACE = [0, 1, 2, 3, 4, 0, 1, 2]

        @block.sync
        def _(sp):
            def load_gate_up(e, slot):
                sp.dma_start(slot_gate(slot), w_exp_gate[0, e].rearrange("(k p) f -> p k f", p=P)).then_inc(gate_up_in[slot], 16)
                sp.dma_start(slot_up(slot), w_exp_up[0, e].rearrange("(k p) f -> p k f", p=P)).then_inc(gate_up_in[slot], 16)

            def load_down(e, slot):
                sp.dma_start(slot_down(slot), w_exp_down[0, e].rearrange("(c p) n -> p c n", p=P)).then_inc(down_in[slot], 16)

            def load_expert(e, slot):
                load_gate_up(e, slot)
                load_down(e, slot)

            def load_pair(q, j, rnd):
                sp.wait_ge(gate_up_done, rnd * PAIRS + q - (UNROLL - 1))
                for i in range(2):
                    load_gate_up(2 * q + i, 2 * j + i)
                sp.wait_ge(down_hi, rnd * PAIRS + q - (UNROLL - 1))
                for i in range(2):
                    load_down(2 * q + i, 2 * j + i)

            sp.dma_start(h_sb[:, 0, :], x[0, 0:P, :]).then_inc(x_in[0], 16)
            w_in_v = w_in[0].rearrange("(k p) n -> p k n", p=P)
            for c in range(N_CHUNKS):
                v, w = chunk_view(c)
                if c == 0:
                    for cols, loaded in ((slice(K_COL, w), kv_swa_in), (slice(0, K_COL), w_in_in[0])):
                        sp.dma_start(v[:, :, cols], w_in_v[:, :, cols]).then_inc(loaded, 16)
                else:
                    sp.dma_start(v, w_in_v[:, :, c * CHUNK:c * CHUNK + w]).then_inc(w_in_in[c], 16)
            sp.wait_ge(proj_done, 6)
            b0 = ring[:, 0, 0:4 * D].rearrange("p (c n) -> p c n", c=4)
            for i in range(2):
                sp.dma_start(b0[64 * i:64 * i + 64], w_branch_swa[0, 256 * i:256 * i + 256].rearrange("(c p) n -> p c n", p=64)).then_inc(branch_in[0], 16)
            sp.wait_ge(proj_done, 12)
            sp.dma_start(ring[:, 1, 0:4 * D].rearrange("p (c n) -> p c n", c=4),
                         w_branch_moba[0].rearrange("(c p) n -> p c n", p=P)).then_inc(branch_in[1], 16)
            w_out_v = w_out[0].rearrange("(k p) n -> p k n", p=P)
            sp.wait_ge(proj_done, QKV_UNITS)
            sp.dma_start(ring[:, 2, 0:4 * D].rearrange("p (k n) -> p k n", k=4), w_out_v[:, 0:4]).then_inc(w_out_in[0], 16)
            sp.wait_ge(proj_done, QKV_UNITS + 6)
            sp.dma_start(ring[:, 3, 0:2 * D].rearrange("p (k n) -> p k n", k=2), w_out_v[:, 6:8]).then_inc(w_out_in[1], 16)
            sp.wait_ge(proj_done, QKV_UNITS + 12)
            sp.dma_start(slot_gate(4), w_sh_gate[0].rearrange("(k p) f -> p k f", p=P)).then_inc(shared_in, 16)
            sp.dma_start(slot_up(4), w_sh_up[0].rearrange("(k p) f -> p k f", p=P)).then_inc(shared_in, 16)
            sp.dma_start(slot_down(4), w_sh_down[0].rearrange("(c p) n -> p c n", p=P)).then_inc(shared_in, 16)
            sp.wait_ge(att_ready, HEAD_PAIRS)
            sp.wait_ge(proj_done, UNITS)
            sp.dma_start(ring[:, 2, 4 * D:6 * D].rearrange("p (k n) -> p k n", k=2), w_out_v[:, 4:6]).then_inc(w_out_in[2], 16)
            for i, v in enumerate((ln1_g, ln1_b)):
                sp.dma_start(ln1_gb[:, i, :], v[0:1, :].partition_broadcast(P)).then_inc(ln1_in, 16)
            load_expert(5, 5)
            sp.wait_ge(branch_done, KC)
            for e in (0, 1):
                load_expert(e, e)
            sp.wait_ge(w_out_done, 2)
            for e in (2, 3):
                load_expert(e, e)
            sp.wait_ge(shared_gu, 2)
            load_gate_up(4, 4)

            def load_rest(rnd):
                turns = (PAIRS - LOADS_PEELED) // UNROLL
                with sp.Fori(1, 1 + turns) as it:
                    for j in range(UNROLL):
                        load_pair(it * UNROLL + j, j, rnd)
                for q in range(LOADS_PEELED + turns * UNROLL, PAIRS):
                    load_pair(q, q % UNROLL, rnd)

            load_rest(0)
            sp.wait_ge(over_ready, 1)
            more = sp.value_load(over[0:1, 0:1], min_val=0, max_val=1)
            with sp.If(more == 1):
                with sp.Fori(1, ROUNDS) as rnd:
                    sp.wait_ge(down_hi, rnd * PAIRS)
                    for q in range(LOADS_PEELED):
                        for i in range(2):
                            load_expert(2 * q + i, 2 * q + i)
                    load_rest(rnd)
                sp.wait_ge(down_hi, ROUNDS * PAIRS)
            sp.wait_ge(down_hi, PAIRS - 2)
            for i, v in enumerate((ln2_g, ln2_b)):
                sp.dma_start(ln2_gb[:, i, :], v[0:1, :].partition_broadcast(P)).then_inc(ln2_in, 16)
            for t in range(TILES):
                sp.wait_ge(ln_dve, TILES + t + 1)
                sp.wait_ge(ln_pool, TILES + t + 1)
                sp.dma_start(out[0, t * P:(t + 1) * P, :], h_sb[:, t, :]).then_inc(out_done, 16)
            sp.wait_ge(out_done, 16 * TILES)

        @block.gpsimd
        def _(pool):
            n = 0

            def step(ins):
                nonlocal n
                n += 1
                ins.then_inc(pool_step, 1)
                pool.wait_ge(pool_step, n)

            step(pool.memset(ident[:, :], 0.0))
            pool.affine_select(out=ident[:, :], in_=ident[:, :], compare_op=ALU.not_equal, fill=1.0,
                               base=0, pattern=[[-1, P]], channel_multiplier=1).then_inc(const_ready, 1)
            for dist in (dist_swa, dist_moba):
                step(pool.iota(dist[:, 0:256], [[1, 256]], base=-P, channel_multiplier=-1, allow_small_or_imprecise_dtypes=True))
                step(pool.iota(dist[:, 256:384], [[1, P]], base=0, channel_multiplier=-1, allow_small_or_imprecise_dtypes=True))
                step(pool.affine_select(out=dist[:, 0:256], in_=dist[:, 0:256], compare_op=ALU.is_ge, fill=NEG_INF,
                                        base=P, pattern=[[-1, 256]], channel_multiplier=1))
                step(pool.affine_select(out=dist[:, 256:384], in_=dist[:, 256:384], compare_op=ALU.is_ge, fill=NEG_INF,
                                        base=0, pattern=[[-1, P]], channel_multiplier=1))
            step(pool.affine_select(out=dist_swa[:, 0:256], in_=dist_swa[:, 0:256], compare_op=ALU.is_gt, fill=NEG_INF,
                                    base=0, pattern=[[1, 256]], channel_multiplier=-1))
            step(pool.memset(ones[:, :], 1.0))
            step(pool.affine_select(out=before[:, :], in_=ones[:, :], compare_op=ALU.is_gt, fill=0.0,
                                    base=0, pattern=[[1, P]], channel_multiplier=-1))
            pool.iota(place_ids[:, :], [[1, SLOTS]], base=1, channel_multiplier=0,
                      allow_small_or_imprecise_dtypes=True).then_inc(const_ready, 1)
            pool.wait_ge(proj_done, 12)
            pool.wait_ge(xT_hi_ready, 4)
            pool.tensor_copy(xT_hi_kept[:, :, :], xT_hi[:, :, :].bitcast(F32)).then_inc(xT_kept, 1)
            for u in range(QKV_UNITS, QKV_UNITS + 4):
                split_lo(pool, u)

            def split_branch_lo(j):
                pool.wait_ge(branch_hi_ready, j + 1)
                for b in range(2):
                    w, lo = branch_weights(b, j)
                    hi = branch_hi[BRANCH_PLACE[j]][:, 4 * b:4 * b + 4, :]
                    last = pool.tensor_tensor(lo, w, hi.bitcast(F32), ALU.subtract)
                last.then_inc(branch_lo_ready, 1)

            for pr in range(HEAD_PAIRS):
                if pr < HEAD_PAIRS - 2:
                    split_lo(pool, QKV_UNITS + 2 * pr + 4)
                pool.wait_ge(proj_act, QKV_UNITS // 2 + 2 * pr + 2)
                g = gates[:, 2 * pr:2 * pr + 2, :]
                pool.tensor_scalar(g, g, 1.0, None, ALU.add).then_inc(gate_sum, 1)
                if pr < HEAD_PAIRS - 2:
                    split_lo(pool, QKV_UNITS + 2 * pr + 5)
                else:
                    split_branch_lo(pr - (HEAD_PAIRS - 2))
                if pr == HEAD_PAIRS - 2:
                    pool.wait_ge(att_hi_ready, 1)
                    a = slice(0, SWA_PAIRS)
                    pool.tensor_tensor(att_lo[:, a, :], att[:, a, :], att_hi[:, a, :].bitcast(F32), ALU.subtract).then_inc(att_lo_pool, 1)
            for j in range(2, KC):
                split_branch_lo(j)
            for k in range(KC):
                pool.wait_ge(out_hi_ready, k + 1)
                w, lo = out_weights(k)
                pool.tensor_tensor(lo, w, out_hi[OUT_PLACE[k]][:, :].bitcast(F32), ALU.subtract).then_inc(out_lo_ready, 1)
            for l, (gb, loaded) in enumerate(((ln1_gb, ln1_in), (ln2_gb, ln2_in))):
                pool.wait_ge(loaded, 32)
                for t in range(TILES):
                    cols = ln_columns(l, t)[1]
                    v = h_sb[:, t, cols]
                    pool.wait_ge(ln_norm, l * TILES + t + 1)
                    step(pool.tensor_tensor(v, v, gb[:, 0, cols], ALU.mult))
                    pool.tensor_tensor(v, v, gb[:, 1, cols], ALU.add).then_inc(ln_pool, 1)
                if l == 0:
                    pool.wait_ge(part_ready, 1)
                    pool.tensor_tensor(h_rem, h_sb[:, :, :], h_part[0][:, :, :], ALU.subtract).then_inc(rem_ready, 1)
                    pool.wait_ge(rem_ready, 1)
                    pool.wait_ge(part_ready, 2)
                    pool.tensor_tensor(h_part[2][:, :, :], h_rem, h_part[1][:, :, :], ALU.subtract).then_inc(part_ready, 1)

        @block.scalar
        def _(act):
            act.dma_start(h_sb[:, 1, :], x[0, P:2 * P, :]).then_inc(x_in[1], 16)
            act.dma_start(sinks, swa_sinks[0:1, :].partition_broadcast(P)).then_inc(sinks_in, 16)
            act.dma_start(bias_r, router_bias[0:1, :].partition_broadcast(P)).then_inc(bias_in, 16)
            act.dma_start(wr_sb[:, :, :], w_router[0].rearrange("(k p) e -> p k e", p=P)).then_inc(router_in, 16)
            for t in range(TILES):
                act.wait_ge(x_turned, 2 * t + 1)
                act.activation(xT[:, 0:4, t * P:(t + 1) * P], bank[4 + 2 * t][:, :].rearrange("p (k n) -> p k n", k=4),
                               ACT.Copy).then_inc(xT_act, 1)
            for t in range(TILES):
                for g in range(2):
                    if g == 1:
                        act.wait_ge(xT_dve, t + 1)
                    act.activation(xT_hi[:, 4 * g:4 * g + 4, t * P:(t + 1) * P],
                                   bank[4 + 2 * t + g][:, :].rearrange("p (k n) -> p k n", k=4), ACT.Copy).then_inc(xT_hi_ready, 1)
            units = unit_outputs()
            for u in range(1, 4):
                split_hi(act, u)
            for u in range(QKV_UNITS):
                if u % 2 == 0:
                    act.wait_ge(proj_done, u + 1)
                    act.activation(units[u][0], units[u][1], ACT.Copy).then_inc(proj_act, 1)
                for n in {11: (14,), 12: (), 13: (15,), 14: (16, 17), 15: (18, 19)}.get(u, (u + 3,) if u else ()):
                    split_hi(act, n)
            act.wait_ge(sinks_in, 16)

            def exponentials(pr):
                for h in range(2):
                    i = 2 * pr + h
                    act.wait_ge(max_done, i + 1)
                    for part, cols in enumerate((slice(0, 256), slice(256, 384))):
                        p_ap = prob[:, pr % 2, h, cols]
                        last = act.activation(p_ap, p_ap, ACT.Exp, bias=neg_max[:, i, part:part + 1], scale=ATT_SCALE,
                                              accum_out=row_sum[:, i, part:part + 1])
                    if pr < SWA_PAIRS:
                        head = heads_of(pr)[h][1]
                        last = act.activation(sink_exp[:, i, :], neg_max[:, i, :], ACT.Exp, bias=sinks[:, head:head + 1])
                    last.then_inc(exp_done, 1)

            def gate_exp(g):
                act.wait_ge(proj_done, QKV_UNITS + g + 1)
                act.activation(gates[:, g, :], bank[g % 2][:, 0:SEQ], ACT.Exp, scale=-1.0).then_inc(proj_act, 1)

            def take_att(pr):
                att = q_swa[:, pr, :] if pr < SWA_PAIRS else q_moba[:, pr - SWA_PAIRS, :]
                act.wait_ge(pv_done, pr + 1)
                act.activation(att, bank[4][:, 0:SEQ], ACT.Copy).then_inc(att_ready, 1)

            def split_att_hi(first, end):
                act.wait_ge(att_ready, end)
                act.wait_ge(proj_done, QKV_UNITS + 6)
                act.activation(att_hi[:, first:end, :], att[:, first:end, :], ACT.Copy).then_inc(att_hi_ready, 1)

            def split_branch_hi(j):
                if j == 0:
                    act.wait_ge(branch_in[0], 32)
                    act.wait_ge(branch_in[1], 16)
                    act.wait_ge(proj_done, QKV_UNITS + 6)
                elif j == 2:
                    act.wait_ge(proj_done, UNITS)
                elif j >= 6:
                    act.wait_ge(branch_done, j - 5)
                for b in range(2):
                    last = act.activation(branch_hi[BRANCH_PLACE[j]][:, 4 * b:4 * b + 4, :], branch_weights(b, j)[0], ACT.Copy)
                last.then_inc(branch_hi_ready, 1)

            def split_out_hi(k):
                if k == 0:
                    act.wait_ge(w_out_in[0], 16)
                elif k == 2:
                    act.wait_ge(prob_turned, 2 * HEAD_PAIRS)
                elif k in (3, 4):
                    act.wait_ge(branch_done, k + 4)
                elif k >= 5:
                    act.wait_ge(out_step, k - 4)
                if k == 4:
                    act.wait_ge(w_out_in[2], 16)
                if k == 6:
                    act.wait_ge(w_out_in[1], 16)
                act.activation(out_hi[OUT_PLACE[k]][:, :], out_weights(k)[0], ACT.Copy).then_inc(out_hi_ready, 1)

            exponentials(0)
            for pr in range(HEAD_PAIRS):
                gate_exp(2 * pr)
                if pr >= 1:
                    take_att(pr - 1)
                if pr < HEAD_PAIRS - 2:
                    split_hi(act, QKV_UNITS + 2 * pr + 4)
                if pr < HEAD_PAIRS - 1:
                    exponentials(pr + 1)
                gate_exp(2 * pr + 1)
                for h in range(2):
                    act.wait_ge(prob_turned, 2 * pr + h + 1)
                    if pr >= 2:
                        act.wait_ge(pv_done, pr - 1)
                    act.activation(probT[:, pr % 2, h, :], bank[5 + h][:, 0:384], ACT.Copy).then_inc(probT_ready, 1)
                if pr < HEAD_PAIRS - 2:
                    split_hi(act, QKV_UNITS + 2 * pr + 5)
                if pr == HEAD_PAIRS - 2:
                    split_branch_hi(0)
                    split_att_hi(0, SWA_PAIRS)
            split_att_hi(SWA_PAIRS, HEAD_PAIRS - 1)
            split_branch_hi(1)
            take_att(HEAD_PAIRS - 1)
            split_att_hi(HEAD_PAIRS - 1, HEAD_PAIRS)
            for j in range(2, 6):
                split_branch_hi(j)
            for j in range(KC):
                if j in (1, 2):
                    split_branch_hi(5 + j)
                if j in (3, 4, 5):
                    split_out_hi(j - 3)
                act.wait_ge(mixed, j + 1)
                act.activation(mix_hi[:, j, :], gates[:, j, :], ACT.Copy).then_inc(mix_hi_ready, 1)
            for k in range(3, KC):
                split_out_hi(k)

            def load_table(function):
                act.activation(unused, ident[:, 0:1], function)

            def root(l, t):
                act.wait_ge(ln_var_ready, l * TILES + t + 1)
                act.activation(ln_root[:, t, :], ln_var[:, t, :], ACT.Sqrt).then_inc(ln_root_ready, 1)

            def take_turned_h(t, g):
                act.wait_ge(h_turned, 2 * t + g + 1)
                act.activation(hT[:, 4 * g:4 * g + 4, t * P:(t + 1) * P],
                               bank[2 + 2 * t + g][:, :].rearrange("p (k n) -> p k n", k=4), ACT.Copy).then_inc(hT_act, 1)

            def centre(l, t):
                act.wait_ge(ln_rstd_ready, l * TILES + t + 1)
                v = h_sb[:, t, ln_columns(l, t)[1]]
                act.activation(v, v, ACT.Identity, bias=ln_shift[:, t, :], scale=ln_rstd[:, t, :]).then_inc(ln_norm, 1)

            act.wait_ge(const_ready, 1)
            load_table(ACT.Sqrt)
            root(0, 0)
            centre(0, 0)
            take_turned_h(0, 0)
            take_turned_h(0, 1)
            root(0, 1)
            centre(0, 1)
            load_table(ACT.Exp)
            take_turned_h(1, 0)
            act.wait_ge(ln_dve, TILES)
            act.wait_ge(ln_pool, TILES)
            act.activation(h_part[0][:, :, :], h_sb[:, :, :], ACT.Copy).then_inc(part_ready, 1)
            act.wait_ge(logits_done, 1)
            act.activation(r_exp, bank[0][:, 0:2 * P].rearrange("p (t e) -> p t e", t=TILES)[:, :, 0:N_EXPERTS],
                           ACT.Exp, scale=-1.0).then_inc(logit_exp, 1)
            act.wait_ge(rem_ready, 1)
            act.activation(h_part[1][:, :, :], h_rem, ACT.Copy).then_inc(part_ready, 1)
            for c in range(2):
                act.wait_ge(shared_gu, c + 1)
                act.activation(sh_silu[:, c, :], bank[4 + 2 * c][:, 0:SEQ], ACT.Silu).then_inc(shared_silu, 1)

            def take_lo(n, rnd):
                act.wait_ge(gather_lo, rnd * PAIRS + n + 1)
                act.activation(xg[:, 0:4, :], R_LO[:, :].rearrange("p (k n) -> p k n", k=4), ACT.Copy).then_inc(xg_lo, 1)

            def take_turned(p, j, rnd, what):
                act.wait_ge(turned, rnd * (PAIRS + 1) + p + 2)
                if "hidden" in what:
                    last = act.activation(hidT[:, :], R_T[:, 0:FF], ACT.Copy)
                if "choice" in what:
                    if not static_zero(p + 1, rnd):
                        act.wait_ge(choice_ready, rnd * PAIRS + p + 1)
                    last = act.activation(choice_wT[:, :], R_T[:, 256:512], ACT.Copy, accum_out=place_weight[(j + 1) % UNROLL])
                last.then_inc(turned_ready, 1)

            def pair(p, j, rnd, last):
                act.wait_ge(gate_up_done, rnd * PAIRS + p + 1)
                if not static_zero(p, rnd):
                    act.wait_ge(hid_ready, rnd * PAIRS + p)
                act.activation(silu_sb[:, :], R_GU[:, 0:FF], ACT.Silu).then_inc(silu_done, 1)
                if static_zero(p, rnd):
                    act.wait_ge(shared_done, 1)
                    act.dma_start(slot_down(4), w_exp_down[0, 4].rearrange("(c p) n -> p c n", p=P)).then_inc(down_in[4], 16)
                if not last:
                    take_lo(p + 1, rnd)
                take_turned(p, j, rnd, "hidden" if last else "hidden and choice")
                for half, (b, done) in enumerate(((R_LO, down_lo), (R_HI, down_hi))):
                    act.wait_ge(done, rnd * PAIRS + p + 1)
                    act.activation(y_top[:, 512 * half:512 * half + 512], b[:, :], ACT.Copy).then_inc(y_top_ready, 1)

            def all_pairs(rnd):
                take_lo(0, rnd)
                take_turned(-1, UNROLL - 1, rnd, "choice")
                pair(0, 0, rnd, False)
                with act.Fori(0, (PAIRS - 2) // UNROLL) as it:
                    for i in range(UNROLL):
                        pair(it * UNROLL + (1 + i), (1 + i) % UNROLL, rnd, False)
                pair(PAIRS - 1, (PAIRS - 1) % UNROLL, rnd, True)

            all_pairs(0)
            more = act.value_load(over[0:1, 0:1], min_val=0, max_val=1)
            with act.If(more == 1):
                with act.Fori(1, ROUNDS) as rnd:
                    all_pairs(rnd)
            load_table(ACT.Sqrt)
            for t in range(TILES):
                root(1, t)
                centre(1, t)

        @block.vector
        def _(dve):
            n = 0

            def step(ins):
                nonlocal n
                n += 1
                ins.then_inc(dve_step, 1)
                dve.wait_ge(dve_step, n)

            for t in range(TILES):
                dve.wait_ge(x_turned, 2 * t + 2)
                dve.tensor_copy(xT[:, 4:8, t * P:(t + 1) * P],
                                bank[5 + 2 * t][:, :].rearrange("p (k n) -> p k n", k=4)).then_inc(xT_dve, 1)
            units = unit_outputs()
            for t in range(TILES):
                for g in range(2):
                    dve.wait_ge(xT_hi_ready, 2 * t + g + 1)
                    if g == 0:
                        dve.wait_ge(xT_act, t + 1)
                    v = (slice(None), slice(4 * g, 4 * g + 4), slice(t * P, (t + 1) * P))
                    if g == 1:
                        dve.wait_ge(xT_dve, t + 1)
                    dve.tensor_tensor(xT_lo[v], xT[v], xT_hi[v].bitcast(F32), ALU.subtract).then_inc(xT_lo_ready, 1)
            for u in range(1, 4):
                split_lo(dve, u)
            for u in range(1, QKV_UNITS):
                if u % 2 == 1:
                    dve.wait_ge(proj_done, u + 1)
                    dve.tensor_copy(units[u][0], units[u][1]).then_inc(proj_dve, 1)
                if u + 3 < QKV_UNITS:
                    split_lo(dve, u + 3)
            dve.wait_ge(sinks_in, 16)
            step(dve.tensor_scalar(sinks8, sinks, 1.0 / ATT_SCALE, None, ALU.mult))
            dve.wait_ge(const_ready, 2)

            parts = (slice(0, 256), slice(256, 384))

            def bias(pr):
                dist = dist_swa if pr < SWA_PAIRS else dist_moba
                for h, (slope, head) in enumerate(heads_of(pr)):
                    i = 2 * pr + h
                    p_ap = prob[:, pr % 2, h, :]
                    dve.wait_ge(scores_done, i + 1)
                    if pr >= 2:
                        dve.wait_ge(prob_turned, i - 3)
                    dve.scalar_tensor_tensor(out=p_ap, in0=dist[:, :], scalar=SLOPES[slope] / ATT_SCALE,
                                             in1=bank[2 + h][:, 0:384], op0=ALU.mult, op1=ALU.add).then_inc(biased_done, 1)
                    dve.wait_ge(biased_done, i + 1)
                    for part, cols in enumerate(parts):
                        last = dve.tensor_reduce(row_max[:, i, part:part + 1], p_ap[:, cols], AX_X, ALU.max)
                    step(last)
                    if pr < SWA_PAIRS:
                        dve.tensor_scalar(neg_max[:, i, :], row_max[:, i, :], sinks8[:, head:head + 1], -ATT_SCALE,
                                          ALU.max, ALU.mult).then_inc(max_done, 1)
                    else:
                        dve.tensor_scalar(neg_max[:, i, :], row_max[:, i, :], -ATT_SCALE, None, ALU.mult).then_inc(max_done, 1)

            def divide(pr):
                for h in range(2):
                    i = 2 * pr + h
                    dve.wait_ge(exp_done, i + 1)
                    if pr < SWA_PAIRS:
                        step(dve.tensor_tensor(row_sum[:, i, :], row_sum[:, i, :], sink_exp[:, i, :], ALU.add))
                    step(dve.reciprocal(inv_sum[:, i, :], row_sum[:, i, :]))
                    for part, cols in enumerate(parts):
                        p_ap = prob[:, pr % 2, h, cols]
                        last = dve.tensor_scalar(p_ap, p_ap, inv_sum[:, i, part:part + 1], None, ALU.mult)
                    last.then_inc(prob_ready, 1)

            def sigmoid(pr):
                dve.wait_ge(gate_sum, pr + 1)
                g = gates[:, 2 * pr:2 * pr + 2, :]
                dve.reciprocal(g, g).then_inc(gate_ready, 1)

            bias(0)
            for pr in range(HEAD_PAIRS):
                divide(pr)
                if pr < HEAD_PAIRS - 1:
                    bias(pr + 1)
                if pr >= 1:
                    sigmoid(pr - 1)
            for group, a in enumerate((slice(SWA_PAIRS, HEAD_PAIRS - 1), slice(HEAD_PAIRS - 1, HEAD_PAIRS))):
                dve.wait_ge(att_hi_ready, group + 2)
                dve.tensor_tensor(att_lo[:, a, :], att[:, a, :], att_hi[:, a, :].bitcast(F32), ALU.subtract).then_inc(att_lo_dve, 1)
            def mix_rest(j):
                dve.wait_ge(mix_hi_ready, j + 1)
                dve.tensor_tensor(mix_lo[:, j, :], gates[:, j, :], mix_hi[:, j, :].bitcast(F32), ALU.subtract).then_inc(mix_ready, 1)

            dve.wait_ge(gate_ready, HEAD_PAIRS - 1)
            for j in range(KC):
                if j == KC - 2:
                    dve.wait_ge(gate_ready, HEAD_PAIRS + 1)
                dve.wait_ge(branch_done, j + 1)
                for b in range(2):
                    g = gates[:, KC * b + j, :]
                    last = dve.tensor_tensor(g, g, bank[2 + 2 * (j % 2) + b][:, 0:SEQ], ALU.mult)
                step(last)
                dve.tensor_tensor(gates[:, j, :], gates[:, j, :], gates[:, KC + j, :], ALU.add).then_inc(mixed, 1)
                if j >= 1:
                    mix_rest(j - 1)
                if j in (2, 4):
                    if j == 2:
                        dve.wait_ge(gate_sum, HEAD_PAIRS)
                    g = gates[:, GATE_UNITS - 2 + (j == 4), :]
                    dve.reciprocal(g, g).then_inc(gate_ready, 1)
            mix_rest(KC - 1)

            def layer_norm(l, gb, loaded, banks, banks_done):
                for t in range(TILES):
                    dve.wait_ge(banks_done, t + 1)
                    for half in range(2):
                        cols = slice(512 * half, 512 * half + 512)
                        last = dve.scalar_tensor_tensor(out=h_sb[:, t, cols], in0=h_sb[:, t, cols], scalar=ALPHA,
                                                        in1=banks[2 * t + half][:, :], op0=ALU.mult, op1=ALU.add)
                    step(last)
                    for half in range(2):
                        last = dve.bn_stats(ln_stats[:, t, 6 * half:6 * half + 6], h_sb[:, t, 512 * half:512 * half + 512])
                    step(last)
                    step(dve.bn_aggr(ln_mv[:, t, :], ln_stats[:, t, :]))
                    dve.tensor_scalar(ln_var[:, t, :], ln_mv[:, t, 1:2], LN_EPS, None, ALU.add).then_inc(ln_var_ready, 1)
                    if t == 0:
                        dve.wait_ge(loaded, 32)
                    cols = ln_columns(l, t)[0]
                    v = h_sb[:, t, cols]
                    step(dve.scalar_tensor_tensor(out=v, in0=v, scalar=ln_mv[:, t, 0:1], in1=gb[:, 0, cols],
                                                  op0=ALU.subtract, op1=ALU.mult))
                    dve.wait_ge(ln_root_ready, l * TILES + t + 1)
                    step(dve.reciprocal(ln_rstd[:, t, :], ln_root[:, t, :]))
                    dve.scalar_tensor_tensor(out=ln_shift[:, t, :], in0=ln_mv[:, t, 0:1], scalar=-1.0, in1=ln_rstd[:, t, :],
                                             op0=ALU.mult, op1=ALU.mult).then_inc(ln_rstd_ready, 1)
                    dve.scalar_tensor_tensor(out=v, in0=v, scalar=ln_rstd[:, t, :], in1=gb[:, 1, cols],
                                             op0=ALU.mult, op1=ALU.add).then_inc(ln_dve, 1)

            layer_norm(0, ln1_gb, ln1_in, w_out_bank, w_out_done)

            dve.memset(group_sum, -BIG)
            dve.memset(group_pick, -BIG)
            dve.memset(weight, 0.0)
            step(dve.memset(place, 0.0))

            dve.wait_ge(h_turned, 2 * TILES)
            dve.tensor_copy(hT[:, 4:8, P:SEQ], bank[5][:, :].rearrange("p (k n) -> p k n", k=4)).then_inc(hT_dve, 1)

            dve.wait_ge(logit_exp, 1)
            step(dve.tensor_scalar(r_one, r_exp, 1.0, None, ALU.add))
            step(dve.reciprocal(score, r_one))
            dve.wait_ge(bias_in, 16)
            step(dve.tensor_tensor(biased, score, bias_r.unsqueeze(1).to_broadcast([P, TILES, N_EXPERTS]), ALU.add))
            groups = biased.rearrange("p t (g e) -> p (t g) e", e=PER_GROUP)
            for g in range(TILES * N_GROUPS):
                last = dve.max(top_in_group[:, g, :], groups[:, g, :])
            step(last)
            top2 = top_in_group.rearrange("p (t g) e -> p t g e", t=TILES)
            step(dve.tensor_tensor(group_sum[:, :, 0:N_GROUPS], top2[:, :, :, 0], top2[:, :, :, 1], ALU.add))
            for t in range(TILES):
                last = dve.max(group_top[:, t, :], group_sum[:, t, :])
            step(last)
            step(dve.tensor_copy(group_pick[:, :, 0:TOPK_GROUPS], group_top[:, :, 0:TOPK_GROUPS]))
            for t in range(TILES):
                last = dve.match_replace(out=group_marked[:, t, :], in_to_replace=group_pick[:, t, :],
                                         in_values=group_sum[:, t, :], imm_value=BIG)
            step(last)
            step(dve.tensor_scalar(group_on.rearrange("p (t g) o -> p t (g o)", t=TILES), group_marked[:, :, 0:N_GROUPS],
                                   BIG, None, ALU.is_equal))
            step(dve.tensor_scalar(group_off, group_on, -NEG_INF, NEG_INF, ALU.mult, ALU.add))
            spread = [P, TILES * N_GROUPS, PER_GROUP]
            masked_g = masked.rearrange("p t (g e) -> p (t g) e", e=PER_GROUP)
            masked_sum_g = masked_sum.rearrange("p t (g e) -> p (t g) e", e=PER_GROUP)
            step(dve.tensor_tensor(masked_g, groups, group_on.to_broadcast(spread), ALU.mult))
            step(dve.tensor_tensor(masked_sum_g, masked_g, group_off.to_broadcast(spread), ALU.add))
            for t in range(TILES):
                last = dve.max(expert_top[:, t, :], masked_sum[:, t, :])
            step(last)
            for t in range(TILES):
                last = dve.match_replace(out=expert_marked[:, t, :], in_to_replace=expert_top[:, t, :],
                                         in_values=masked_sum[:, t, :], imm_value=BIG)
            step(last)
            dve.tensor_scalar(chosen, expert_marked, BIG, None, ALU.is_equal).then_inc(chosen_ready, 1)
            dve.wait_ge(chosen_ready, 1)
            step(dve.tensor_tensor(masked, score, chosen, ALU.mult))
            step(dve.tensor_reduce(weight_sum, masked, AX_X, ALU.add))
            step(dve.reciprocal(weight_inv, weight_sum))
            for t in range(TILES):
                last = dve.tensor_scalar(weight[:, t, 0:N_EXPERTS], masked[:, t, :], weight_inv[:, t, :], ROUTED_SCALE,
                                         ALU.mult, ALU.mult)
            step(last)

            def shared_hidden(c):
                dve.wait_ge(shared_silu, c + 1)
                dve.tensor_tensor(sh_hidT[:, c, :], sh_silu[:, c, :], bank[5 + 2 * c][:, 0:SEQ], ALU.mult).then_inc(shared_hid, 1)

            shared_hidden(0)

            dve.wait_ge(lines_done, 1)
            lines = bank[3][:, 0:3 * N_EXPERTS].rearrange("p (t e) -> p t e", t=3)
            dve.scalar_tensor_tensor(out=place[:, :, 0:N_EXPERTS], in0=lines[:, 0:TILES, :], scalar=1.0, in1=chosen,
                                     op0=ALU.add, op1=ALU.mult)
            step(dve.tensor_reduce(most, lines[:, TILES, :], AX_X, ALU.max))
            step(dve.tensor_scalar(over_f, most, SLOTS + 0.5, None, ALU.is_gt))
            dve.tensor_copy(over, over_f).then_inc(over_ready, 1)
            dve.wait_ge(const_ready, 2)

            def choose_for(q, j):
                shape = [P, TILES, 2, SLOTS]
                dve.tensor_tensor(choose[j][:, :, :].rearrange("p t (e s) -> p t e s", e=2),
                                  place[:, :, bass.ds(2 * q, 2)].unsqueeze(3).to_broadcast(shape),
                                  place_ids[:, :].unsqueeze(1).unsqueeze(1).to_broadcast(shape), ALU.is_equal).then_inc(choose_ready, 1)

            def weigh(q, j, rnd):
                shape = [P, TILES, 2, SLOTS]
                dve.wait_ge(choose_ready, rnd * (PAIRS + 1) + q + 1)
                dve.tensor_tensor(choose_w[j][:, :, :].rearrange("p t (e s) -> p t e s", e=2),
                                  weight[:, :, bass.ds(2 * q, 2)].unsqueeze(3).to_broadcast(shape),
                                  choose[j][:, :, :].rearrange("p t (e s) -> p t e s", e=2), ALU.mult).then_inc(choose_w_ready, 1)

            def take_hi(q, rnd):
                dve.wait_ge(gather_hi, rnd * PAIRS + q + 1)
                dve.tensor_copy(xg[:, 4:8, :], R_HI[:, :].rearrange("p (k n) -> p k n", k=4)).then_inc(xg_hi, 1)

            def form_choiceT(q, j, rnd):
                dve.wait_ge(turned_ready, rnd * (PAIRS + 1) + q + 1)
                dve.tensor_scalar(choiceT[j][:, :], choice_wT[:, :], 0.0, None, ALU.is_gt).then_inc(choice_ready, 1)

            def pair(p, j, rnd, last):
                if not last:
                    if not static_zero(p, rnd):
                        dve.wait_ge(turned, rnd * (PAIRS + 1) + p)
                    choose_for(p + 2, (j + 2) % UNROLL)
                dve.wait_ge(silu_done, rnd * PAIRS + p + 1)
                dve.scalar_tensor_tensor(out=hid[:, :], in0=silu_sb[:, :], scalar=place_weight[j], in1=R_GU[:, FF:2 * FF],
                                         op0=ALU.mult, op1=ALU.mult).then_inc(hid_ready, 1)
                if not last:
                    weigh(p + 2, (j + 2) % UNROLL, rnd)
                    take_hi(p + 1, rnd)
                    form_choiceT(p + 1, (j + 1) % UNROLL, rnd)
                for half, b in enumerate((R_LO, R_HI)):
                    cols = slice(512 * half, 512 * half + 512)
                    dve.wait_ge(y_top_ready, 2 * (rnd * PAIRS + p) + half + 1)
                    dve.tensor_tensor(y_rest[:, cols], b[:, :], y_top[:, cols].bitcast(F32), ALU.subtract).then_inc(y_ready, 1)

            def all_pairs(rnd):
                for q in range(2):
                    choose_for(q, q)
                    weigh(q, q, rnd)
                if static_zero(rnd):
                    shared_hidden(1)
                take_hi(0, rnd)
                form_choiceT(0, 0, rnd)
                pair(0, 0, rnd, False)
                with dve.Fori(0, (PAIRS - 2) // UNROLL) as it:
                    for i in range(UNROLL):
                        pair(it * UNROLL + (1 + i), (1 + i) % UNROLL, rnd, False)
                pair(PAIRS - 1, (PAIRS - 1) % UNROLL, rnd, True)

            all_pairs(0)
            dve.wait_ge(over_ready, 1)
            more = dve.value_load(over[0:1, 0:1], min_val=0, max_val=1)
            with dve.If(more == 1):
                with dve.Fori(1, ROUNDS) as rnd:
                    dve.wait_ge(turned, rnd * (PAIRS + 1))
                    dve.tensor_scalar(place_ids[:, :], place_ids[:, :], float(SLOTS), None, ALU.add).then_inc(round_ready, 1)
                    dve.wait_ge(round_ready, rnd)
                    all_pairs(rnd)
            layer_norm(1, ln2_gb, ln2_in, acc, moe_done)

        @block.tensor
        def _(pe):
            def turn(banks, done):
                for t in range(TILES):
                    for g in range(2):
                        for kk in range(4):
                            k = 4 * g + kk
                            last = pe.transpose(banks[2 * t + g][:, kk * P:(kk + 1) * P], h_sb[:, t, k * P:(k + 1) * P], ident[:, :])
                        last.then_inc(done, 1)

            pe.wait_ge(const_ready, 1)
            for t in range(TILES):
                pe.wait_ge(x_in[t], 16)
            turn([bank[4], bank[5], bank[6], bank[7]], x_turned)
            pe.wait_ge(xT_act, 2)
            pe.wait_ge(xT_dve, 2)

            def project(u):
                b = bank[u % 2]
                if u >= 2:
                    who, count = evacuated(u - 2)
                    pe.wait_ge(proj_act if who == "act" else proj_dve, count)
                if u == 0:
                    pe.wait_ge(kv_swa_in, 16)
                    w, _ = chunk_view(0)
                    for t in range(TILES):
                        for k in range(KC):
                            last = pe.matmul(b[:, t * P:(t + 1) * P], xT[:, k, t * P:(t + 1) * P], w[:, k, 640:768],
                                             start=(k == 0), stop=(k == KC - 1))
                else:
                    _, _, hi, lo = unit_weights(u)
                    if u == 1:
                        pe.wait_ge(xT_hi_ready, 4)
                        pe.wait_ge(xT_lo_ready, 4)
                    if u < QKV_UNITS:
                        pe.wait_ge(w_lo_ready, u)
                        x_hi = xT_hi
                    else:
                        pe.wait_ge(w_lo_gate, u - QKV_UNITS + 1)
                        x_hi = xT_hi_kept
                    if u == QKV_UNITS:
                        pe.wait_ge(xT_kept, 1)
                    if u in (14, 15):
                        for t in range(TILES):
                            toks = slice(t * P, (t + 1) * P)
                            for k in range(KC):
                                for i, (a, w) in enumerate(((x_hi, hi), (x_hi, lo), (xT_lo, hi))):
                                    last = pe.matmul(b[:, 256 * t:256 * t + 256], a[:, k, toks], w[:, k, :],
                                                     start=(k == 0 and i == 0), stop=(k == KC - 1 and i == 2))
                    else:
                        for k in range(KC):
                            for i, (w, a) in enumerate(((hi, x_hi), (lo, x_hi), (hi, xT_lo))):
                                last = pe.matmul(b[:, 0:SEQ], w[:, k, :], a[:, k, :],
                                                 start=(k == 0 and i == 0), stop=(k == KC - 1 and i == 2))
                last.then_inc(proj_done, 1)

            for u in range(QKV_UNITS):
                project(u)

            def score(pr):
                q = q_swa[:, pr, :] if pr < SWA_PAIRS else q_moba[:, pr - SWA_PAIRS, :]
                k = k_swa if pr < SWA_PAIRS else k_moba[:, pr - SWA_PAIRS, :]
                for h in range(2):
                    rows = slice(64 * h, 64 * h + 64)
                    if pr >= 1:
                        pe.wait_ge(biased_done, 2 * (pr - 1) + h + 1)
                    pe.matmul(bank[2 + h][:, 0:256], q[rows, P:SEQ], k[rows, 0:SEQ], start=True, stop=True)
                    pe.matmul(bank[2 + h][:, 256:384], q[rows, 0:P], k[rows, 0:P], start=True, stop=True).then_inc(scores_done, 1)

            def turn_prob(pr):
                for h in range(2):
                    pe.wait_ge(prob_ready, 2 * pr + h + 1)
                    if pr >= 1:
                        pe.wait_ge(probT_ready, 2 * (pr - 1) + h + 1)
                    for to, fr in ((0, 256), (128, 0), (256, 128)):
                        last = pe.transpose(bank[5 + h][:, to:to + P], prob[:, pr % 2, h, fr:fr + P], ident[:, :])
                    last.then_inc(prob_turned, 1)

            def times_v(pr):
                pe.wait_ge(probT_ready, 2 * pr + 2)
                if pr >= 1:
                    pe.wait_ge(att_ready, pr)
                for h, (_, head) in enumerate(heads_of(pr)):
                    rows = slice(64 * h, 64 * h + 64)
                    if pr < SWA_PAIRS:
                        v = [v_swa[:, t, 64 * h:64 * h + 64] for t in range(TILES)]
                    else:
                        v = [v_moba[:, t, 64 * head:64 * head + 64] for t in range(TILES)]
                    pe.matmul(bank[4][rows, 0:SEQ], v[0], probT[:, pr % 2, h, 0:256], start=True, stop=False)
                    last = pe.matmul(bank[4][rows, P:SEQ], v[1], probT[:, pr % 2, h, 256:384], start=False, stop=True)
                last.then_inc(pv_done, 1)

            pe.wait_ge(proj_act, QKV_UNITS // 2)
            pe.wait_ge(proj_dve, QKV_UNITS // 2)
            score(0)
            for pr in range(HEAD_PAIRS):
                project(QKV_UNITS + 2 * pr)
                if pr >= 1:
                    times_v(pr - 1)
                if pr < HEAD_PAIRS - 1:
                    score(pr + 1)
                project(QKV_UNITS + 2 * pr + 1)
                turn_prob(pr)
            times_v(HEAD_PAIRS - 1)

            pe.wait_ge(att_lo_pool, 1)
            pe.wait_ge(biased_done, 2 * HEAD_PAIRS)
            for j in range(KC):
                pe.wait_ge(branch_lo_ready, j + 1)
                if j >= 2:
                    pe.wait_ge(mixed, j - 1)
                for b in range(2):
                    lo = branch_weights(b, j)[1]
                    hi = branch_hi[BRANCH_PLACE[j]]
                    for c in range(4):
                        i = 4 * b + c
                        if j == 0 and i >= SWA_PAIRS:
                            pe.wait_ge(att_lo_dve, 1 if i < HEAD_PAIRS - 1 else 2)
                        for n, (w, a) in enumerate(((hi[:, i, :], att_hi), (lo[:, c, :], att_hi), (hi[:, i, :], att_lo))):
                            last = pe.matmul(bank[2 + 2 * (j % 2) + b][:, 0:SEQ], w, a[:, i, :],
                                             start=(c == 0 and n == 0), stop=(c == 3 and n == 2))
                last.then_inc(branch_done, 1)

            def project_out(k, t):
                pe.wait_ge(mix_ready, k + 1)
                pe.wait_ge(out_lo_ready, k + 1)
                hi, lo = out_hi[OUT_PLACE[k]], out_weights(k)[1]
                toks = slice(t * P, (t + 1) * P)
                for half in range(2):
                    cols = slice(512 * half, 512 * half + 512)
                    for n, (a, w) in enumerate(((mix_hi, hi), (mix_lo, hi), (mix_hi, lo))):
                        last = pe.matmul(w_out_bank[2 * t + half][:, :], a[:, k, toks], w[:, cols],
                                         start=(k == 0 and n == 0), stop=(k == KC - 1 and n == 2))
                return last

            pe.wait_ge(proj_act, QKV_UNITS // 2 + GATE_UNITS)
            for k in range(KC // 2):
                for t in range(TILES):
                    last = project_out(k, t)
                last.then_inc(out_step, 1)
            for t in range(TILES):
                for k in range(KC // 2, KC):
                    last = project_out(k, t)
                last.then_inc(w_out_done, 1)

            for t in range(TILES):
                for g in range(2):
                    pe.wait_ge((ln_dve, ln_pool)[g], t + 1)
                    for kk in range(4):
                        k = 4 * g + kk
                        last = pe.transpose(bank[2 + 2 * t + g][:, kk * P:(kk + 1) * P], h_sb[:, t, k * P:(k + 1) * P], ident[:, :])
                    last.then_inc(h_turned, 1)
                pe.wait_ge(hT_act, 2 + t)
                if t == 0:
                    pe.wait_ge(router_in, 16)
                else:
                    pe.wait_ge(hT_dve, 1)
                for k in range(KC):
                    last = pe.matmul(bank[0][:, t * P:(t + 1) * P], hT[:, k, t * P:(t + 1) * P],
                                     wr_sb[:, k, :].unsqueeze(1).to_broadcast([P, 2, N_EXPERTS]),
                                     start=(k == 0), stop=(k == KC - 1))
            last.then_inc(logits_done, 1)

            def find_places():
                pe.wait_ge(const_ready, 2)
                pe.wait_ge(chosen_ready, 1)
                cols = [slice(i * N_EXPERTS, (i + 1) * N_EXPERTS) for i in range(3)]
                pe.matmul(bank[3][:, cols[0]], before[:, :], chosen[:, 0, :], start=True, stop=True)
                pe.matmul(bank[3][:, cols[1]], ones[:, :], chosen[:, 0, :], start=True, stop=False)
                pe.matmul(bank[3][:, cols[1]], before[:, :], chosen[:, 1, :], start=False, stop=True)
                pe.matmul(bank[3][:, cols[2]], ones[:, :], chosen[:, 0, :], start=True, stop=False)
                pe.matmul(bank[3][:, cols[2]], ones[:, :], chosen[:, 1, :], start=False, stop=True).then_inc(lines_done, 1)

            pe.wait_ge(shared_in, 48)
            for c in range(2):
                for i, w in enumerate((slot_gate(4), slot_up(4))):
                    if (c, i) == (1, 1):
                        find_places()
                    for k in range(KC):
                        last = pe.matmul(bank[4 + 2 * c + i][:, 0:SEQ], w[:, k, c * P:(c + 1) * P], hT[:, k, :],
                                         start=(k == 0), stop=(k == KC - 1))
                last.then_inc(shared_gu, 1)
            def shared_down():
                pe.wait_ge(shared_hid, 2)
                for t in range(TILES):
                    for half in range(2):
                        for c in range(2):
                            last = pe.matmul(acc[2 * t + half][:, :], sh_hidT[:, c, t * P:(t + 1) * P],
                                             slot_down(4)[:, c, 512 * half:512 * half + 512],
                                             start=(c == 0), stop=(c == 1))
                last.then_inc(shared_done, 1)

            def gather(q, j, rnd):
                pe.wait_ge(choose_ready, rnd * (PAIRS + 1) + q + 1)
                for g, (b, done) in enumerate(((R_LO, gather_lo), (R_HI, gather_hi))):
                    for kk in range(4):
                        k = 4 * g + kk
                        for t in range(TILES):
                            for i, part in enumerate(h_part):
                                last = pe.matmul(b[:, kk * P:(kk + 1) * P], part[:, t, k * P:(k + 1) * P], choose[j][:, t, :],
                                                 start=(t == 0 and i == 0), stop=(t == TILES - 1 and i == 2))
                    last.then_inc(done, 1)

            def turn_choice(q, j, rnd):
                pe.wait_ge(choose_w_ready, rnd * (PAIRS + 1) + q + 1)
                for t in range(TILES):
                    last = pe.transpose(R_T[:, 256 + t * P:256 + (t + 1) * P], choose_w[j][:, t, :], ident[:, :])
                return last

            def scatter(j, done=None):
                for t in range(TILES):
                    for half in range(2):
                        for y in (y_top, y_rest):
                            last = pe.matmul(acc[2 * t + half][:, :], choiceT[j][:, t * P:(t + 1) * P],
                                             y[:, 512 * half:512 * half + 512], start=False, stop=False, skip_group_check=True)
                    if done is not None:
                        last.then_inc(done, 1)

            def pair(p, turn_no, j, rnd, first, last_pair):
                fill = rnd * PER_ROUND[j] + turn_no + 1
                for i in range(2):
                    pe.wait_ge(gate_up_in[2 * j + i], fill * 32)
                for k in range(KC):
                    for i in range(2):
                        last = pe.matmul(R_GU[64 * i:64 * i + 64, :], xg[:, k, 64 * i:64 * i + 64],
                                         slot_gate_up(2 * j + i)[:, k, :, :], start=(k == 0), stop=(k == KC - 1))
                last.then_inc(gate_up_done, 1)
                if static_zero(p, rnd):
                    shared_down()
                if not last_pair:
                    if not first:
                        pe.wait_ge(y_ready, 2 * (rnd * PAIRS + p))
                    gather(p + 1, (j + 1) % UNROLL, rnd)
                    turn_choice(p + 1, (j + 1) % UNROLL, rnd)
                pe.wait_ge(hid_ready, rnd * PAIRS + p + 1)
                for c in range(FF // P):
                    last = pe.transpose(R_T[:, c * P:(c + 1) * P], hid[:, c * P:(c + 1) * P], ident[:, :])
                last.then_inc(turned, 1)
                if not first:
                    if last_pair:
                        pe.wait_ge(y_ready, 2 * (rnd * PAIRS + p))
                    pe.wait_ge(choice_ready, rnd * PAIRS + p)
                    scatter((j - 1) % UNROLL)
                pe.wait_ge(turned_ready, rnd * (PAIRS + 1) + p + 2)
                if not last_pair:
                    pe.wait_ge(xg_lo, rnd * PAIRS + p + 2)
                    pe.wait_ge(xg_hi, rnd * PAIRS + p + 2)
                for i in range(2):
                    pe.wait_ge(down_in[2 * j + i], fill * 16)
                for half, (b, done) in enumerate(((R_LO, down_lo), (R_HI, down_hi))):
                    for c in range(FF // P):
                        for i in range(2):
                            last = pe.matmul(b[64 * i:64 * i + 64, :], hidT[:, c * P + 64 * i:c * P + 64 * i + 64],
                                             slot_down(2 * j + i)[:, c, 512 * half:512 * half + 512],
                                             start=(c == 0), stop=(c == FF // P - 1))
                    last.then_inc(done, 1)

            def all_pairs(rnd):
                gather(0, 0, rnd)
                turn_choice(0, 0, rnd).then_inc(turned, 1)
                pe.wait_ge(xg_lo, rnd * PAIRS + 1)
                pe.wait_ge(xg_hi, rnd * PAIRS + 1)
                pe.wait_ge(turned_ready, rnd * (PAIRS + 1) + 1)
                pair(0, 0, 0, rnd, True, False)
                with pe.Fori(0, (PAIRS - 2) // UNROLL) as it:
                    for i in range(UNROLL):
                        p = 1 + i
                        pair(it * UNROLL + p, it + p // UNROLL, p % UNROLL, rnd, False, False)
                last = PAIRS - 1
                pair(last, last // UNROLL, last % UNROLL, rnd, False, True)

            pe.wait_ge(part_ready, 3)
            pe.wait_ge(over_ready, 1)
            all_pairs(0)
            more = pe.value_load(over[0:1, 0:1], min_val=0, max_val=1)
            with pe.If(more == 1):
                with pe.Fori(1, ROUNDS) as rnd:
                    pe.wait_ge(y_ready, 2 * rnd * PAIRS)
                    scatter((PAIRS - 1) % UNROLL)
                    all_pairs(rnd)
                pe.wait_ge(y_ready, 2 * ROUNDS * PAIRS)
            pe.wait_ge(y_ready, 2 * PAIRS)
            scatter((PAIRS - 1) % UNROLL, moe_done)


_INS = ["x", "w_in", "swa_sinks", "w_branch_swa", "w_branch_moba", "w_out", "ln1_g", "ln1_b", "w_router", "router_bias",
        "w_exp_gate", "w_exp_up", "w_exp_down", "w_sh_gate", "w_sh_up", "w_sh_down", "ln2_g", "ln2_b"]


def kernel(**inputs):
    import numpy as np
    import concourse.bacc as bacc
    from concourse.bass_utils import run_bass_kernel_spmd

    nc = bacc.Bacc("TRN2", target_bir_lowering=False, num_devices=1)
    arrays, args = {}, []
    for name in _INS:
        a = np.ascontiguousarray(inputs[name])
        arrays[f"in_{name}_dram"] = a
        args.append(nc.dram_tensor(f"in_{name}_dram", a.shape, mybir.dt.from_np(a.dtype), kind="ExternalInput").ap())
    out = nc.dram_tensor("out_0_dram", (1, SEQ, D), F32, kind="ExternalOutput").ap()
    block_program(nc, *args, out)
    r = run_bass_kernel_spmd(nc, [arrays], core_ids=[0])
    return r.results[0]["out_0_dram"]
```

```python
from contextlib import ExitStack

import concourse.bass as bass
from concourse import mybir

F32 = mybir.dt.float32
F32R = mybir.dt.float32r
BF16 = mybir.dt.bfloat16
I32 = mybir.dt.int32
ALU = mybir.AluOpType
ACT = mybir.ActivationFunctionType
AX_X = mybir.AxisListType.X

P = 128
SEQ = 256
TILES = SEQ // P
D = 1024
KC = D // P
HEAD_DIM = 64
SWA_HEADS = 8
MOBA_HEADS = 8
N_EXPERTS = 64
N_GROUPS = 8
PER_GROUP = N_EXPERTS // N_GROUPS
TOPK_GROUPS = 4
FF = 256
ROUTED_SCALE = 2.5
ALPHA = 2.0 ** 0.25
LN_EPS = 1e-5
NEG_INF = -1e30
BIG = 3e38

IN_COLS = 4352
CHUNK = 768
N_CHUNKS = -(-IN_COLS // CHUNK)
K_COL = 512
GATE_COL = 2304

RING = 6
SLOT = 3 * KC * FF
W_UP = KC * FF
W_DOWN = 2 * KC * FF
SLOTS = 64
PAIRS = N_EXPERTS // 2
ROUNDS = SEQ // SLOTS
UNROLL = RING // 2
LOADS_PEELED = UNROLL
WARM_UP = 18
EXTRA = 2


SWA_PAIRS = SWA_HEADS // 2
HEAD_PAIRS = (SWA_HEADS + MOBA_HEADS) // 2
SLOPES = [2.0 ** (-8.0 * (i + 1) / (SWA_HEADS + MOBA_HEADS)) for i in range(SWA_HEADS + MOBA_HEADS)]
ATT_SCALE = HEAD_DIM ** -0.5

QKV_UNITS = 16
GATE_UNITS = 2 * D // P
UNITS = QKV_UNITS + GATE_UNITS
FIRST_OF_CHUNK = (12, 16, 22, 28)


def heads_of(pair):
    if pair < SWA_PAIRS:
        return [(pair, pair), (pair + SWA_PAIRS, pair + SWA_PAIRS)]
    c = pair - SWA_PAIRS
    return [(SWA_HEADS + 2 * c + i, 2 * c + i) for i in range(2)]


def ln_columns(layer_norm, tile):
    edge = {(0, 0): D, (0, 1): 768, (1, 0): 512, (1, 1): 832}[layer_norm, tile]
    return slice(0, edge), slice(edge, D)


def evacuated(unit):
    if unit < QKV_UNITS:
        return ("act" if unit % 2 == 0 else "dve"), unit // 2 + 1
    return "act", QKV_UNITS // 2 + unit - QKV_UNITS + 1


def block_program(nc, x, w_in, swa_sinks, w_branch_swa, w_branch_moba, w_out, ln1_g, ln1_b, w_router, router_bias,
                  w_exp_gate, w_exp_up, w_exp_down, w_sh_gate, w_sh_up, w_sh_down, ln2_g, ln2_b, out):
    with ExitStack() as ctx:
        def sem(name):
            return ctx.enter_context(nc.semaphore(name))

        bank = [ctx.enter_context(nc.psum_tensor(f"bank{i}", [P, 512], F32)) for i in range(8)]

        ring_at, h_at = 0, RING * SLOT
        const_at = h_at + TILES * D
        gates_at = const_at + 1024
        work_at = gates_at + GATE_UNITS * SEQ
        sbuf_base = -(-nc.sbuf_base // 32) * 32
        sbuf_end = nc.sbuf_usable_end

        def at(name, offset, shape, dt=F32):
            n = mybir.dt.size(dt)
            for s in shape:
                n *= s
            assert sbuf_base + 4 * offset + n <= sbuf_end, name
            return nc.alloc_sbuf_tensor_at(name, [P, *shape], dt, offset=sbuf_base + 4 * offset)

        ring = at("ring", ring_at, [RING, SLOT])
        h_sb = at("h_sb", h_at, [TILES, D])
        ident = at("ident", const_at, [P])
        before = at("before", const_at + 128, [P], BF16)
        ones = at("ones", const_at + 192, [P], BF16)
        place_ids = at("place_ids", const_at + 256, [SLOTS])
        wr_sb = at("wr_sb", const_at + 320, [KC, N_EXPERTS])
        bias_r = at("bias_r", const_at + 832, [N_EXPERTS])[:, :]
        alpha_ident = at("alpha_ident", const_at + 896, [P])
        gates = at("gates", gates_at, [GATE_UNITS, SEQ])
        tables = at("tables", gates_at, [GATE_UNITS * SEQ])
        att = at("att", work_at, [HEAD_PAIRS, SEQ])
        q_swa, q_moba = att[:, 0:SWA_PAIRS, :], att[:, SWA_PAIRS:HEAD_PAIRS, :]
        k_swa = at("k_swa", work_at + 2048, [SEQ])[:, :]
        v_swa = at("v_swa", work_at + 2304, [TILES, P])[:, :, :]
        k_moba = at("k_moba", work_at + 2560, [4, SEQ])
        v_moba = at("v_moba", work_at + 3584, [TILES, 512])
        prob = at("prob", work_at + 4608, [2, 2, 384])
        hT = at("hT", work_at + 6144, [KC, SEQ])
        dist_swa = at("dist_swa", work_at + 8192, [384])
        dist_moba = at("dist_moba", work_at + 8576, [384])
        xT = at("xT", work_at + 2560, [KC, SEQ])
        xT_lo = at("xT_lo", work_at + 6144, [KC, SEQ], F32R)
        xT_hi = at("xT_hi", gates_at, [KC, SEQ], F32R)
        xT_hi_kept = at("xT_hi_kept", ring_at + SLOT + 4 * D, [KC, SEQ], F32R)
        chunk_lo = [at(f"chunk_lo{c}", ring_at + c * SLOT, [SLOT], F32R) for c in range(N_CHUNKS)]
        w_hi = [at(f"w_hi{i}", gates_at + KC * SEQ + i * D, [KC, P], F32R) for i in range(2)]
        w_hi += [at("w_hi2", ring_at + (RING - 1) * SLOT + W_DOWN, [KC, P], F32R)]
        w_hi_gate = [at(f"w_hi_gate{i}", ring_at + 2 * (i // 2) * SLOT + (4 + i % 2) * D, [KC, P], F32R) for i in range(4)]
        w_hi_v = [at("w_hi_v0", ring_at + 4 * D, [KC, SEQ], F32R), at("w_hi_v1", gates_at + KC * SEQ, [KC, SEQ], F32R)]
        q_lo = [at("q_lo0", work_at + 1024, [KC, P], F32R), at("q_lo1", work_at + 4608, [KC, P], F32R)]
        SLOT_3 = ring_at + 3 * SLOT
        att_lo = at("att_lo", work_at, [HEAD_PAIRS, SEQ], F32R)
        att_hi = at("att_hi", SLOT_3 + 2 * D, [HEAD_PAIRS, SEQ], F32R)
        mix_lo = at("mix_lo", gates_at, [KC, SEQ], F32R)
        mix_hi = at("mix_hi", gates_at + KC * SEQ, [KC, SEQ], F32R)
        branch_hi_at = [slot * SLOT + ring_at + i * D for slot in (3, 0, 1) for i in (4, 5)]
        branch_hi = [at(f"branch_hi{i}", a, [KC, P], F32R) for i, a in enumerate(branch_hi_at)]
        out_hi_at = [work_at + 6144, work_at + 7168, work_at + 4608] + [SLOT_3 + i * D for i in (4, 5, 2, 3)]
        out_hi = [at(f"out_hi{i}", a, [D], F32R) for i, a in enumerate(out_hi_at)]
        ln1_gb = at("ln1_gb", work_at + 2560, [2, D])
        sh_silu = at("sh_silu", work_at + 3072, [2, SEQ])
        h_part = [at(f"h_part{i}", work_at + 1024 * i, [TILES, D], BF16) for i in range(3)]
        y_top = at("y_top", work_at + 3072, [D], F32R)
        y_rest = at("y_rest", work_at + 4096, [D], F32R)
        choiceT = [at(f"choiceT{i}", work_at + 6272 + 256 * i, [SEQ], F32R) for i in range(3)]
        choose = [at(f"choose{i}", work_at + 5888 + 128 * i, [TILES, P], BF16) for i in range(3)]
        choose_w = [at(f"choose_w{i}", work_at + 5120 + 256 * i, [TILES, P]) for i in range(3)]
        xg = at("xg", work_at + 7040, [KC, P])
        silu_sb = at("silu_sb", work_at + 8064, [FF])
        hid = at("hid", work_at + 8320, [FF])
        hidT = at("hidT", work_at + 8576, [FF])
        choice_wT = at("choice_wT", work_at + 8832, [SEQ])

        def piece(base, at, shape):
            n = 1
            for s in shape:
                n *= s
            v = base[:, at:at + n]
            if len(shape) == 2:
                v = v.rearrange("p (a b) -> p a b", b=shape[1])
            if len(shape) == 3:
                v = v.rearrange("p (a b c) -> p a b c", b=shape[1], c=shape[2])
            return v

        tail = ring[:, RING - 1, W_DOWN:SLOT]
        probT = piece(tail, 0, (2, 2, 384))
        row_max = piece(tail, 1536, (16, 2))
        neg_max = piece(tail, 1568, (16, 2))
        row_sum = piece(tail, 1600, (16, 2))
        sink_exp = piece(tail, 1632, (16, 2))
        inv_sum = piece(tail, 1664, (16, 2))
        sinks = piece(tail, 1696, (SWA_HEADS,))
        sinks8 = piece(tail, 1704, (SWA_HEADS,))
        PLACED = N_EXPERTS + EXTRA
        sh_hidT = piece(tables, 0, (2, SEQ))
        r_exp = piece(tables, 0, (TILES, N_EXPERTS))
        r_one = piece(tables, 128, (TILES, N_EXPERTS))
        score = piece(tables, 256, (TILES, N_EXPERTS))
        biased = piece(tables, 384, (TILES, N_EXPERTS))
        top_in_group = piece(tables, 512, (TILES * N_GROUPS, 8))
        group_sum = piece(tables, 640, (TILES, 2 * N_GROUPS))
        group_top = piece(tables, 672, (TILES, 8))
        group_pick = piece(tables, 688, (TILES, 8))
        group_marked = piece(tables, 704, (TILES, 2 * N_GROUPS))
        group_on = piece(tables, 736, (TILES * N_GROUPS, 1))
        group_off = piece(tables, 752, (TILES * N_GROUPS, 1))
        masked = piece(tables, 768, (TILES, N_EXPERTS))
        expert_top = piece(tables, 896, (TILES, 8))
        expert_marked = piece(tables, 912, (TILES, N_EXPERTS))
        weight_sum = piece(tables, 1040, (TILES, 1))
        weight_inv = piece(tables, 1042, (TILES, 1))
        most = piece(tables, 1044, (1,))
        over_f = piece(tables, 1045, (1,))
        over = piece(tables, 1046, (1,)).bitcast(I32)
        masked_sum = piece(tables, 1088, (TILES, N_EXPERTS))
        chosen = piece(tables, 1280, (TILES * N_EXPERTS // 2,)).bitcast(BF16).rearrange("p (t e) -> p t e", t=TILES)
        weight = piece(tables, 1408, (TILES, PLACED))
        place = piece(tables, 1544, (TILES, PLACED))
        place_weight = [piece(tables, 1680 + 2 * i, (1,)) for i in range(3)]
        h_rem = piece(tables, 1792, (TILES, D))
        ln_tables = at("ln_tables", work_at + 8192, [64])
        ln_stats = piece(ln_tables, 0, (TILES, 12))
        ln_mv = piece(ln_tables, 24, (TILES, 2))
        ln_rstd = piece(ln_tables, 28, (TILES, 1))
        ln_var = piece(ln_tables, 30, (TILES, 1))
        ln_root = piece(ln_tables, 32, (TILES, 1))
        ln_shift = piece(ln_tables, 34, (TILES, 1))
        unused = piece(ln_tables, 36, (1,))
        sh_down = piece(tables, 1792, (FF // P, D))
        ln2_gb = piece(ring[:, RING - 2, :], 0, (2, D))


        x_in = [sem(f"x_in{t}") for t in range(TILES)]
        w_in_in = [sem(f"w_in_in{c}") for c in range(N_CHUNKS)]
        chunk_1_in = [sem("chunk_1_in0"), sem("chunk_1_in1")]
        kv_swa_in, q_swa_in = sem("kv_swa_in"), [sem("q_swa_in0"), sem("q_swa_in1")]
        branch_in = [sem("branch_swa_in"), sem("branch_moba_in")]
        w_out_in = [sem(f"w_out_in{i}") for i in range(3)]
        shared_in, sinks_in, router_in, bias_in = sem("shared_in"), sem("sinks_in"), sem("router_in"), sem("bias_in")
        ln1_in, ln2_in = sem("ln1_in"), sem("ln2_in")
        gate_up_in = [[sem(f"gate_up_in{s}_{half}") for half in range(2)] for s in range(RING)]
        down_in = [sem(f"down_in{s}") for s in range(RING)]
        out_done = sem("out_done")
        pool_step, const_ready = sem("pool_step"), sem("const_ready")
        dve_step = sem("dve_step")
        x_turned, xT_act, xT_dve = sem("x_turned"), sem("xT_act"), sem("xT_dve")
        xT_hi_ready, xT_lo_ready, xT_kept = sem("xT_hi_ready"), sem("xT_lo_ready"), sem("xT_kept")
        w_hi_ready, w_lo_ready, w_lo_gate = sem("w_hi_ready"), sem("w_lo_ready"), sem("w_lo_gate")
        proj_done, proj_act, proj_dve = sem("proj_done"), sem("proj_act"), sem("proj_dve")
        scores_done, biased_done, max_done, exp_done = sem("scores_done"), sem("biased_done"), sem("max_done"), sem("exp_done")
        prob_ready, prob_turned, probT_ready = sem("prob_ready"), sem("prob_turned"), sem("probT_ready")
        gate_sum, gate_ready = sem("gate_sum"), sem("gate_ready")
        pv_done, att_ready = sem("pv_done"), sem("att_ready")
        att_hi_ready, att_lo_pool, att_lo_dve = sem("att_hi_ready"), sem("att_lo_pool"), sem("att_lo_dve")
        branch_hi_ready, branch_lo_ready = sem("branch_hi_ready"), sem("branch_lo_ready")
        out_hi_ready, out_lo_pool, out_lo_dve, out_step = sem("out_hi_ready"), sem("out_lo_pool"), sem("out_lo_dve"), sem("out_step")
        mixed, mix_hi_ready, mix_ready = sem("mixed"), sem("mix_hi_ready"), sem("mix_ready")
        branch_done, w_out_done = sem("branch_done"), sem("w_out_done")
        ln_var_ready, ln_root_ready, ln_rstd_ready, ln_norm = sem("ln_var_ready"), sem("ln_root_ready"), sem("ln_rstd_ready"), sem("ln_norm")
        ln_dve, ln_pool = sem("ln_dve"), sem("ln_pool")
        h_turned, hT_act, hT_dve = sem("h_turned"), sem("hT_act"), sem("hT_dve")
        logits_done, logit_exp = sem("logits_done"), sem("logit_exp")
        chosen_ready, lines_done, over_ready = sem("chosen_ready"), sem("lines_done"), sem("over_ready")
        shared_gu, shared_silu, shared_hid, shared_down_in = sem("shared_gu"), sem("shared_silu"), sem("shared_hid"), sem("shared_down_in")
        choose_ready, choose_w_ready = sem("choose_ready"), sem("choose_w_ready")
        gather_lo, gather_hi, xg_lo, xg_hi = sem("gather_lo"), sem("gather_hi"), sem("xg_lo"), sem("xg_hi")
        gate_up_done, silu_done, hid_ready = sem("gate_up_done"), sem("silu_done"), sem("hid_ready")
        turned, turned_ready = sem("turned"), sem("turned_ready")
        down_lo, down_hi, y_top_ready, y_ready = sem("down_lo"), sem("down_hi"), sem("y_top_ready"), sem("y_ready")
        choice_ready, part_ready, rem_ready = sem("choice_ready"), sem("part_ready"), sem("rem_ready")
        moe_done, round_ready = sem("moe_done"), sem("round_ready")

        R_LO, R_HI, R_GU, R_T = bank[0], bank[1], bank[2], bank[3]
        acc = [bank[4], bank[5], bank[6], bank[7]]
        w_out_bank = [bank[0], bank[1], bank[6], bank[7]]

        def static_zero(*counts):
            return all(isinstance(c, int) for c in counts) and sum(counts) == 0

        def slot_gate(s):
            return ring[:, s, 0:W_UP].rearrange("p (k f) -> p k f", k=KC)

        def slot_up(s):
            return ring[:, s, W_UP:W_DOWN].rearrange("p (k f) -> p k f", k=KC)

        def slot_gate_up(s):
            return ring[:, s, 0:W_DOWN].rearrange("p (g k f) -> p k g f", g=2, k=KC)

        def slot_down(s):
            return ring[:, s, W_DOWN:SLOT].rearrange("p (c n) -> p c n", c=FF // P)

        def chunk_view(c):
            w = min(CHUNK, IN_COLS - c * CHUNK)
            return ring[:, c, 0:KC * w].rearrange("p (k n) -> p k n", k=KC), w

        block = ctx.enter_context(nc.Block())

        PER_ROUND = [len(range(s, PAIRS, UNROLL)) for s in range(UNROLL)]

        def unit_outputs():
            res = []
            for u in range(QKV_UNITS):
                b = bank[u % 2]
                if u == 0:
                    res.append((v_swa, b[:, 0:SEQ].rearrange("p (t n) -> p t n", t=TILES)))
                elif u == 1:
                    res.append((k_swa, b[:, 0:SEQ]))
                elif u < 6:
                    res.append((q_swa[:, u - 2, :], b[:, 0:SEQ]))
                elif u < 10:
                    res.append((q_moba[:, u - 6, :], b[:, 0:SEQ]))
                elif u < 14:
                    res.append((k_moba[:, u - 10, :], b[:, 0:SEQ]))
                else:
                    half = slice(256 * (u - 14), 256 * (u - 13))
                    res.append((v_moba[:, :, half], b[:, :].rearrange("p (t n) -> p t n", t=TILES)))
            return res

        def unit_weights(u):
            if 2 <= u < 6:
                w, _ = chunk_view(0)
                w = w[:, :, 0:K_COL].rearrange("p k (g h d) -> p k g h d", g=2, h=SWA_PAIRS)[:, :, :, u - 2, :]
                return 0, w, w_hi[u % 3], q_lo[u % 2]
            if u == 1:
                col, width = K_COL, P
            elif u < 14:
                col, width = 768 + P * (u - 6), P
            elif u < QKV_UNITS:
                col, width = 1792 + 256 * (u - 14), 256
            else:
                col, width = GATE_COL + P * (u - QKV_UNITS), P
            c, off = col // CHUNK, col % CHUNK
            full = min(CHUNK, IN_COLS - c * CHUNK)
            lo = chunk_lo[c][:, 0:KC * full].rearrange("p (k n) -> p k n", k=KC)[:, :, off:off + width]
            hi = w_hi[u % 3] if u < 14 else w_hi_v[u - 14] if u < QKV_UNITS else w_hi_gate[u % 4]
            return c, chunk_view(c)[0][:, :, off:off + width], hi, lo

        def split_hi(act, u):
            c, w, hi, _ = unit_weights(u)
            if u == 1:
                act.wait_ge(kv_swa_in, 16)
            elif u in (2, 4):
                act.wait_ge(q_swa_in[u // 2 - 1], 32)
            elif u in (6, 9):
                act.wait_ge(chunk_1_in[u // 3 - 2], 16)
            elif u in FIRST_OF_CHUNK:
                act.wait_ge(w_in_in[c], 16)
            if u < 4:
                done = 0
            elif u < 14:
                done = u - 2
            elif u < 20:
                done = {14: 6, 15: 14, 16: 15, 17: 15, 18: 16, 19: 16}[u]
            else:
                done = u - 3
            if done:
                act.wait_ge(proj_done, done)
            if 2 <= u < 6:
                hi = hi[:, :, :].rearrange("p k (g d) -> p k g d", g=2)
            else:
                hi = hi[:, :, :]
            act.activation(hi, w, ACT.Copy).then_inc(w_hi_ready, 1)

        def split_lo(eng, u):
            _, w, hi, lo = unit_weights(u)
            eng.wait_ge(w_hi_ready, u)
            hi, lo = hi[:, :, :], lo[:, :, :]
            if 2 <= u < 6:
                hi = hi.rearrange("p k (g d) -> p k g d", g=2)
                lo = lo.rearrange("p k (g d) -> p k g d", g=2)
            if u in (4, 5):
                eng.wait_ge(proj_done, u - 1)
            eng.tensor_tensor(lo, w, hi.bitcast(F32), ALU.subtract).then_inc(w_lo_ready if u < QKV_UNITS else w_lo_gate, 1)

        def branch_weights(b, j):
            cols = slice(j * P, (j + 1) * P)
            return (ring[:, b, 0:4 * D].rearrange("p (c n) -> p c n", c=4)[:, :, cols],
                    chunk_lo[b][:, 0:4 * D].rearrange("p (c n) -> p c n", c=4)[:, :, cols])

        def out_weights(k):
            slot, row = (2, k) if k < 6 else (3, k - 6)
            return ring[:, slot, row * D:(row + 1) * D], chunk_lo[slot][:, row * D:(row + 1) * D]

        def split_out_lo(eng, k, done):
            eng.wait_ge(out_hi_ready, k + 1)
            w, lo = out_weights(k)
            eng.tensor_tensor(lo, w, out_hi[OUT_PLACE[k]][:, :].bitcast(F32), ALU.subtract).then_inc(done, 1)

        OUT_BY_POOL = 4
        BRANCH_PLACE = [0, 1, 2, 3, 4, 5, 0, 1]
        OUT_PLACE = [2, 0, 1, 3, 4, 5, 6, 2]

        @block.sync
        def _(sp):
            def load_gate_up(experts):
                for half in range(2):
                    ks = slice(KC // 2 * half, KC // 2 * (half + 1))
                    for e, slot in experts:
                        for to, w in ((slot_gate(slot), w_exp_gate), (slot_up(slot), w_exp_up)):
                            sp.dma_start(to[:, ks, :], w[0, e].rearrange("(k p) f -> p k f", p=P)[:, ks, :]).then_inc(gate_up_in[slot][half], 16)

            def load_down(e, slot):
                sp.dma_start(slot_down(slot), w_exp_down[0, e].rearrange("(c p) n -> p c n", p=P)).then_inc(down_in[slot], 16)

            def load_expert(e, slot):
                load_gate_up([(e, slot)])
                load_down(e, slot)

            def load_pair(q, j, rnd):
                sp.wait_ge(gate_up_done, rnd * PAIRS + q - (UNROLL - 1))
                load_gate_up([(2 * q + i, 2 * j + i) for i in range(2)])
                sp.wait_ge(down_hi, rnd * PAIRS + q - (UNROLL - 1))
                for i in range(2):
                    load_down(2 * q + i, 2 * j + i)

            sp.dma_start(h_sb[:, 0, :], x[0, 0:P, :]).then_inc(x_in[0], 16)
            w_in_v = w_in[0].rearrange("(k p) n -> p k n", p=P)
            for c in range(N_CHUNKS):
                v, w = chunk_view(c)
                if c == 0:
                    sp.dma_start(v[:, :, K_COL:w], w_in_v[:, :, K_COL:w]).then_inc(kv_swa_in, 16)
                    for part in range(2):
                        for g in range(2):
                            first = K_COL // 2 * g + P * part
                            sp.dma_start(v[:, :, first:first + P], w_in_v[:, :, first:first + P]).then_inc(q_swa_in[part], 16)
                elif c == 1:
                    for half in range(2):
                        first = CHUNK // 2 * half
                        sp.dma_start(v[:, :, first:first + CHUNK // 2], w_in_v[:, :, CHUNK + first:CHUNK + first + CHUNK // 2]
                                     ).then_inc(chunk_1_in[half], 16)
                else:
                    sp.dma_start(v, w_in_v[:, :, c * CHUNK:c * CHUNK + w]).then_inc(w_in_in[c], 16)
            sp.wait_ge(proj_done, 6)
            b0 = ring[:, 0, 0:4 * D].rearrange("p (c n) -> p c n", c=4)
            for i in range(2):
                sp.dma_start(b0[64 * i:64 * i + 64], w_branch_swa[0, 256 * i:256 * i + 256].rearrange("(c p) n -> p c n", p=64)).then_inc(branch_in[0], 16)
            sp.wait_ge(proj_done, 12)
            sp.dma_start(ring[:, 1, 0:4 * D].rearrange("p (c n) -> p c n", c=4),
                         w_branch_moba[0].rearrange("(c p) n -> p c n", p=P)).then_inc(branch_in[1], 16)
            w_out_v = w_out[0].rearrange("(k p) n -> p k n", p=P)
            sp.wait_ge(proj_done, QKV_UNITS)
            sp.dma_start(ring[:, 2, 0:4 * D].rearrange("p (k n) -> p k n", k=4), w_out_v[:, 0:4]).then_inc(w_out_in[0], 16)
            sp.wait_ge(proj_done, QKV_UNITS + 6)
            sp.dma_start(ring[:, 3, 0:2 * D].rearrange("p (k n) -> p k n", k=2), w_out_v[:, 6:8]).then_inc(w_out_in[1], 16)
            sp.wait_ge(proj_done, QKV_UNITS + 12)
            sp.dma_start(slot_gate(4), w_sh_gate[0].rearrange("(k p) f -> p k f", p=P)).then_inc(shared_in, 16)
            sp.dma_start(slot_up(4), w_sh_up[0].rearrange("(k p) f -> p k f", p=P)).then_inc(shared_in, 16)
            load_down(4, 4)
            sp.wait_ge(att_ready, HEAD_PAIRS)
            sp.wait_ge(proj_done, UNITS)
            sp.dma_start(ring[:, 2, 4 * D:6 * D].rearrange("p (k n) -> p k n", k=2), w_out_v[:, 4:6]).then_inc(w_out_in[2], 16)
            for i, v in enumerate((ln1_g, ln1_b)):
                sp.dma_start(ln1_gb[:, i, :], v[0:1, :].partition_broadcast(P)).then_inc(ln1_in, 16)
            load_expert(5, 5)
            sp.wait_ge(branch_done, KC)
            for e in (0, 1):
                load_expert(e, e)
            sp.wait_ge(w_out_done, 2)
            for e in (2, 3):
                load_expert(e, e)
            sp.wait_ge(shared_gu, 2)
            load_gate_up([(4, 4)])
            sp.wait_ge(part_ready, 3)
            sp.dma_start(sh_down, w_sh_down[0].rearrange("(c p) n -> p c n", p=P)).then_inc(shared_down_in, 16)

            def load_rest(rnd):
                turns = (PAIRS - LOADS_PEELED) // UNROLL
                with sp.Fori(1, 1 + turns) as it:
                    for j in range(UNROLL):
                        load_pair(it * UNROLL + j, j, rnd)
                for q in range(LOADS_PEELED + turns * UNROLL, PAIRS):
                    load_pair(q, q % UNROLL, rnd)

            load_rest(0)
            sp.wait_ge(over_ready, 1)
            more = sp.value_load(over[0:1, 0:1], min_val=0, max_val=1)
            with sp.If(more == 1):
                with sp.Fori(1, ROUNDS) as rnd:
                    sp.wait_ge(down_hi, rnd * PAIRS)
                    for q in range(LOADS_PEELED):
                        for i in range(2):
                            load_expert(2 * q + i, 2 * q + i)
                    load_rest(rnd)
                sp.wait_ge(down_hi, ROUNDS * PAIRS)
            sp.wait_ge(down_hi, PAIRS - 2)
            for i, v in enumerate((ln2_g, ln2_b)):
                sp.dma_start(ln2_gb[:, i, :], v[0:1, :].partition_broadcast(P)).then_inc(ln2_in, 16)
            for t in range(TILES):
                for cols, done, before in zip(ln_columns(1, t), (ln_dve, ln_pool), (TILES, TILES - 1)):
                    sp.wait_ge(done, before + t + 1)
                    sp.dma_start(out[0, t * P:(t + 1) * P, cols], h_sb[:, t, cols]).then_inc(out_done, 16)
            sp.wait_ge(out_done, 2 * 16 * TILES)

        @block.gpsimd
        def _(pool):
            n = 0

            def step(ins):
                nonlocal n
                n += 1
                ins.then_inc(pool_step, 1)
                pool.wait_ge(pool_step, n)

            step(pool.memset(ident[:, :], 0.0))
            pool.affine_select(out=ident[:, :], in_=ident[:, :], compare_op=ALU.not_equal, fill=1.0,
                               base=0, pattern=[[-1, P]], channel_multiplier=1).then_inc(const_ready, 1)
            for dist in (dist_swa, dist_moba):
                step(pool.iota(dist[:, 0:256], [[1, 256]], base=-P, channel_multiplier=-1, allow_small_or_imprecise_dtypes=True))
                step(pool.iota(dist[:, 256:384], [[1, P]], base=0, channel_multiplier=-1, allow_small_or_imprecise_dtypes=True))
                step(pool.affine_select(out=dist[:, 0:256], in_=dist[:, 0:256], compare_op=ALU.is_ge, fill=NEG_INF,
                                        base=P, pattern=[[-1, 256]], channel_multiplier=1))
                step(pool.affine_select(out=dist[:, 256:384], in_=dist[:, 256:384], compare_op=ALU.is_ge, fill=NEG_INF,
                                        base=0, pattern=[[-1, P]], channel_multiplier=1))
            step(pool.affine_select(out=dist_swa[:, 0:256], in_=dist_swa[:, 0:256], compare_op=ALU.is_gt, fill=NEG_INF,
                                    base=0, pattern=[[1, 256]], channel_multiplier=-1))
            step(pool.memset(ones[:, :], 1.0))
            step(pool.affine_select(out=before[:, :], in_=ones[:, :], compare_op=ALU.is_gt, fill=0.0,
                                    base=0, pattern=[[1, P]], channel_multiplier=-1))
            step(pool.memset(alpha_ident[:, :], 0.0))
            step(pool.affine_select(out=alpha_ident[:, :], in_=alpha_ident[:, :], compare_op=ALU.not_equal, fill=ALPHA,
                                    base=0, pattern=[[-1, P]], channel_multiplier=1))
            pool.iota(place_ids[:, :], [[1, SLOTS]], base=1, channel_multiplier=0,
                      allow_small_or_imprecise_dtypes=True).then_inc(const_ready, 1)
            pool.wait_ge(proj_done, 12)
            pool.wait_ge(xT_hi_ready, 4)
            pool.tensor_copy(xT_hi_kept[:, :, :], xT_hi[:, :, :].bitcast(F32)).then_inc(xT_kept, 1)
            for u in range(QKV_UNITS, QKV_UNITS + 4):
                split_lo(pool, u)

            def split_branch_lo(j):
                pool.wait_ge(branch_hi_ready, j + 1)
                for b in range(2):
                    w, lo = branch_weights(b, j)
                    hi = branch_hi[BRANCH_PLACE[j]][:, 4 * b:4 * b + 4, :]
                    last = pool.tensor_tensor(lo, w, hi.bitcast(F32), ALU.subtract)
                last.then_inc(branch_lo_ready, 1)

            for pr in range(HEAD_PAIRS):
                if pr < HEAD_PAIRS - 2:
                    split_lo(pool, QKV_UNITS + 2 * pr + 4)
                else:
                    split_branch_lo(pr - (HEAD_PAIRS - 2))
                pool.wait_ge(proj_act, QKV_UNITS // 2 + 2 * pr + 2)
                g = gates[:, 2 * pr:2 * pr + 2, :]
                pool.tensor_scalar(g, g, 1.0, None, ALU.add).then_inc(gate_sum, 1)
                if pr < HEAD_PAIRS - 2:
                    split_lo(pool, QKV_UNITS + 2 * pr + 5)
                if pr == HEAD_PAIRS - 2:
                    pool.wait_ge(att_hi_ready, 1)
                    a = slice(0, SWA_PAIRS)
                    pool.tensor_tensor(att_lo[:, a, :], att[:, a, :], att_hi[:, a, :].bitcast(F32), ALU.subtract).then_inc(att_lo_pool, 1)
            for j in range(2, KC):
                split_branch_lo(j)
            for k in range(OUT_BY_POOL):
                split_out_lo(pool, k, out_lo_pool)
            for l, (gb, loaded) in enumerate(((ln1_gb, ln1_in), (ln2_gb, ln2_in))):
                pool.wait_ge(loaded, 32)
                for t in range(TILES):
                    cols = ln_columns(l, t)[1]
                    if cols.start == D:
                        continue
                    v = h_sb[:, t, cols]
                    pool.wait_ge(ln_norm, l * TILES + t)
                    step(pool.tensor_tensor(v, v, gb[:, 0, cols], ALU.mult))
                    pool.tensor_tensor(v, v, gb[:, 1, cols], ALU.add).then_inc(ln_pool, 1)
                if l == 0:
                    pool.wait_ge(part_ready, 1)
                    pool.tensor_tensor(h_rem, h_sb[:, :, :], h_part[0][:, :, :], ALU.subtract).then_inc(rem_ready, 1)
                    pool.wait_ge(rem_ready, 1)
                    pool.wait_ge(part_ready, 2)
                    pool.tensor_tensor(h_part[2][:, :, :], h_rem, h_part[1][:, :, :], ALU.subtract).then_inc(part_ready, 1)

        @block.scalar
        def _(act):
            act.dma_start(h_sb[:, 1, :], x[0, P:2 * P, :]).then_inc(x_in[1], 16)
            act.dma_start(sinks, swa_sinks[0:1, :].partition_broadcast(P)).then_inc(sinks_in, 16)
            act.dma_start(bias_r, router_bias[0:1, :].partition_broadcast(P)).then_inc(bias_in, 16)
            act.dma_start(wr_sb[:, :, :], w_router[0].rearrange("(k p) e -> p k e", p=P)).then_inc(router_in, 16)
            for t in range(TILES):
                act.wait_ge(x_turned, 2 * t + 1)
                act.activation(xT[:, 0:4, t * P:(t + 1) * P], bank[4 + 2 * t][:, :].rearrange("p (k n) -> p k n", k=4),
                               ACT.Copy).then_inc(xT_act, 1)
            for t in range(TILES):
                for g in range(2):
                    if g == 1:
                        act.wait_ge(xT_dve, t + 1)
                    act.activation(xT_hi[:, 4 * g:4 * g + 4, t * P:(t + 1) * P],
                                   bank[4 + 2 * t + g][:, :].rearrange("p (k n) -> p k n", k=4), ACT.Copy).then_inc(xT_hi_ready, 1)
            units = unit_outputs()
            for u in range(1, 4):
                split_hi(act, u)
            for u in range(QKV_UNITS):
                if u % 2 == 0:
                    act.wait_ge(proj_done, u + 1)
                    act.activation(units[u][0], units[u][1], ACT.Copy).then_inc(proj_act, 1)
                if 1 <= u <= 11:
                    split_hi(act, u + 3)
                elif u == 13:
                    split_hi(act, 15)
                elif u == 14:
                    split_hi(act, 16)
                    split_hi(act, 17)
            act.wait_ge(sinks_in, 16)

            def exponentials(pr):
                for h in range(2):
                    i = 2 * pr + h
                    act.wait_ge(max_done, i + 1)
                    for part, cols in enumerate((slice(0, 256), slice(256, 384))):
                        p_ap = prob[:, pr % 2, h, cols]
                        last = act.activation(p_ap, p_ap, ACT.Exp, bias=neg_max[:, i, part:part + 1], scale=ATT_SCALE,
                                              accum_out=row_sum[:, i, part:part + 1])
                    if pr < SWA_PAIRS:
                        head = heads_of(pr)[h][1]
                        last = act.activation(sink_exp[:, i, :], neg_max[:, i, :], ACT.Exp, bias=sinks[:, head:head + 1])
                    last.then_inc(exp_done, 1)

            def gate_exp(g):
                act.wait_ge(proj_done, QKV_UNITS + g + 1)
                act.activation(gates[:, g, :], bank[g % 2][:, 0:SEQ], ACT.Exp, scale=-1.0).then_inc(proj_act, 1)

            def take_att(pr):
                att = q_swa[:, pr, :] if pr < SWA_PAIRS else q_moba[:, pr - SWA_PAIRS, :]
                act.wait_ge(pv_done, pr + 1)
                act.activation(att, bank[4][:, 0:SEQ], ACT.Copy).then_inc(att_ready, 1)

            def split_att_hi(first, end):
                act.wait_ge(att_ready, end)
                act.wait_ge(proj_done, QKV_UNITS + 6)
                act.activation(att_hi[:, first:end, :], att[:, first:end, :], ACT.Copy).then_inc(att_hi_ready, 1)

            def split_branch_hi(j):
                if j == 0:
                    act.wait_ge(branch_in[0], 32)
                    act.wait_ge(branch_in[1], 16)
                    act.wait_ge(proj_done, QKV_UNITS + 6)
                elif j == 2:
                    act.wait_ge(proj_done, UNITS)
                elif j >= 6:
                    act.wait_ge(branch_done, j - 5)
                for b in range(2):
                    last = act.activation(branch_hi[BRANCH_PLACE[j]][:, 4 * b:4 * b + 4, :], branch_weights(b, j)[0], ACT.Copy)
                last.then_inc(branch_hi_ready, 1)

            def split_out_hi(k):
                if k == 0:
                    act.wait_ge(w_out_in[0], 16)
                    act.wait_ge(prob_turned, 2 * HEAD_PAIRS)
                elif k in (3, 4, 5):
                    act.wait_ge(branch_done, k + 4 if k < 5 else KC)
                elif k == 7:
                    act.wait_ge(out_step, 1)
                if k == 4:
                    act.wait_ge(w_out_in[2], 16)
                if k == 6:
                    act.wait_ge(w_out_in[1], 16)
                act.activation(out_hi[OUT_PLACE[k]][:, :], out_weights(k)[0], ACT.Copy).then_inc(out_hi_ready, 1)

            exponentials(0)
            for u in (18, 19):
                split_hi(act, u)
            for pr in range(HEAD_PAIRS):
                gate_exp(2 * pr)
                if pr >= 1:
                    take_att(pr - 1)
                if pr < HEAD_PAIRS - 2:
                    split_hi(act, QKV_UNITS + 2 * pr + 4)
                else:
                    split_branch_hi(pr - (HEAD_PAIRS - 2))
                if pr == HEAD_PAIRS - 1:
                    split_att_hi(SWA_PAIRS, HEAD_PAIRS - 1)
                if pr < HEAD_PAIRS - 1:
                    exponentials(pr + 1)
                gate_exp(2 * pr + 1)
                for h in range(2):
                    act.wait_ge(prob_turned, 2 * pr + h + 1)
                    if pr >= 2:
                        act.wait_ge(pv_done, pr - 1)
                    act.activation(probT[:, pr % 2, h, :], bank[5 + h][:, 0:384], ACT.Copy).then_inc(probT_ready, 1)
                if pr < HEAD_PAIRS - 2:
                    split_hi(act, QKV_UNITS + 2 * pr + 5)
                if pr == HEAD_PAIRS - 2:
                    split_att_hi(0, SWA_PAIRS)
            take_att(HEAD_PAIRS - 1)
            split_att_hi(HEAD_PAIRS - 1, HEAD_PAIRS)
            for j in range(2, 6):
                split_branch_hi(j)
            for j in range(KC):
                if j in (1, 2):
                    split_branch_hi(5 + j)
                if j in (3, 4, 5):
                    split_out_hi(j - 3)
                act.wait_ge(mixed, j + 1)
                act.activation(mix_hi[:, j, :], gates[:, j, :], ACT.Copy).then_inc(mix_hi_ready, 1)
            for k in range(3, KC):
                split_out_hi(k)

            def load_table(function):
                act.activation(unused, ident[:, 0:1], function)

            def root(l, t):
                act.wait_ge(ln_var_ready, l * TILES + t + 1)
                act.activation(ln_root[:, t, :], ln_var[:, t, :], ACT.Sqrt).then_inc(ln_root_ready, 1)

            def take_turned_h(t, g):
                act.wait_ge(h_turned, 2 * t + g + 1)
                act.activation(hT[:, 4 * g:4 * g + 4, t * P:(t + 1) * P],
                               bank[2 + g][:, :].rearrange("p (k n) -> p k n", k=4), ACT.Copy).then_inc(hT_act, 1)

            def centre(l, t):
                act.wait_ge(ln_rstd_ready, l * TILES + t + 1)
                start = ln_columns(l, t)[1].start
                for half in range(2):
                    a, b = max(512 * half, start), 512 * half + 512
                    if a < b:
                        v = h_sb[:, t, a:b]
                        src = acc[2 * t + half][:, a - 512 * half:512] if l else v
                        last = act.activation(v, src, ACT.Identity, bias=ln_shift[:, t, :], scale=ln_rstd[:, t, :])
                last.then_inc(ln_norm, 1)

            act.wait_ge(const_ready, 1)
            load_table(ACT.Sqrt)
            root(0, 0)
            take_turned_h(0, 0)
            take_turned_h(0, 1)
            root(0, 1)
            centre(0, 1)
            load_table(ACT.Exp)
            take_turned_h(1, 0)
            act.wait_ge(ln_dve, TILES)
            act.wait_ge(ln_pool, 1)
            act.activation(h_part[0][:, :, :], h_sb[:, :, :], ACT.Copy).then_inc(part_ready, 1)
            act.wait_ge(logits_done, 1)
            act.activation(r_exp, bank[0][:, 0:2 * P].rearrange("p (t e) -> p t e", t=TILES)[:, :, 0:N_EXPERTS],
                           ACT.Exp, scale=-1.0).then_inc(logit_exp, 1)
            act.wait_ge(rem_ready, 1)
            act.activation(h_part[1][:, :, :], h_rem, ACT.Copy).then_inc(part_ready, 1)
            for c in range(2):
                act.wait_ge(shared_gu, c + 1)
                act.activation(sh_silu[:, c, :], bank[4 + 2 * c][:, 0:SEQ], ACT.Silu).then_inc(shared_silu, 1)

            def take_lo(n, rnd):
                act.wait_ge(gather_lo, rnd * PAIRS + n + 1)
                act.activation(xg[:, 0:4, :], R_LO[:, :].rearrange("p (k n) -> p k n", k=4), ACT.Copy).then_inc(xg_lo, 1)

            def take_turned(p, j, rnd, what):
                act.wait_ge(turned, rnd * (PAIRS + 1) + p + 2)
                if "hidden" in what:
                    last = act.activation(hidT[:, :], R_T[:, 0:FF], ACT.Copy)
                if "choice" in what:
                    if not static_zero(p + 1, rnd):
                        act.wait_ge(choice_ready, rnd * PAIRS + p + 1)
                    last = act.activation(choice_wT[:, :], R_T[:, 256:512], ACT.Copy, accum_out=place_weight[(j + 1) % UNROLL])
                last.then_inc(turned_ready, 1)

            def pair(p, j, rnd, last):
                act.wait_ge(gate_up_done, rnd * PAIRS + p + 1)
                if not static_zero(p, rnd):
                    act.wait_ge(hid_ready, rnd * PAIRS + p)
                act.activation(silu_sb[:, :], R_GU[:, 0:FF], ACT.Silu).then_inc(silu_done, 1)
                if not last:
                    take_lo(p + 1, rnd)
                take_turned(p, j, rnd, "hidden" if last else "hidden and choice")
                for half, (b, done) in enumerate(((R_LO, down_lo), (R_HI, down_hi))):
                    act.wait_ge(done, rnd * PAIRS + p + 1)
                    act.activation(y_top[:, 512 * half:512 * half + 512], b[:, :], ACT.Copy).then_inc(y_top_ready, 1)

            def all_pairs(rnd):
                take_lo(0, rnd)
                take_turned(-1, UNROLL - 1, rnd, "choice")
                pair(0, 0, rnd, False)
                with act.Fori(0, (PAIRS - 2) // UNROLL) as it:
                    for i in range(UNROLL):
                        pair(it * UNROLL + (1 + i), (1 + i) % UNROLL, rnd, False)
                pair(PAIRS - 1, (PAIRS - 1) % UNROLL, rnd, True)

            all_pairs(0)
            more = act.value_load(over[0:1, 0:1], min_val=0, max_val=1)
            with act.If(more == 1):
                with act.Fori(1, ROUNDS) as rnd:
                    all_pairs(rnd)
            load_table(ACT.Sqrt)
            for t in range(TILES):
                root(1, t)
                centre(1, t)

        @block.vector
        def _(dve):
            n = 0

            def step(ins):
                nonlocal n
                n += 1
                ins.then_inc(dve_step, 1)
                dve.wait_ge(dve_step, n)

            for t in range(TILES):
                dve.wait_ge(x_turned, 2 * t + 2)
                dve.tensor_copy(xT[:, 4:8, t * P:(t + 1) * P],
                                bank[5 + 2 * t][:, :].rearrange("p (k n) -> p k n", k=4)).then_inc(xT_dve, 1)
            units = unit_outputs()
            for t in range(TILES):
                for g in range(2):
                    dve.wait_ge(xT_hi_ready, 2 * t + g + 1)
                    if g == 0:
                        dve.wait_ge(xT_act, t + 1)
                    v = (slice(None), slice(4 * g, 4 * g + 4), slice(t * P, (t + 1) * P))
                    if g == 1:
                        dve.wait_ge(xT_dve, t + 1)
                    dve.tensor_tensor(xT_lo[v], xT[v], xT_hi[v].bitcast(F32), ALU.subtract).then_inc(xT_lo_ready, 1)
            for u in range(1, 4):
                split_lo(dve, u)

            def take_unit(u):
                dve.wait_ge(proj_done, u + 1)
                dve.tensor_copy(units[u][0], units[u][1]).then_inc(proj_dve, 1)

            for u in range(1, QKV_UNITS - 1):
                if u % 2 == 1:
                    take_unit(u)
                if u + 3 < QKV_UNITS:
                    split_lo(dve, u + 3)
            dve.wait_ge(sinks_in, 16)
            step(dve.tensor_scalar(sinks8, sinks, 1.0 / ATT_SCALE, None, ALU.mult))
            dve.wait_ge(const_ready, 2)

            parts = (slice(0, 256), slice(256, 384))

            def bias(pr):
                dist = dist_swa if pr < SWA_PAIRS else dist_moba
                for h, (slope, head) in enumerate(heads_of(pr)):
                    i = 2 * pr + h
                    p_ap = prob[:, pr % 2, h, :]
                    dve.wait_ge(scores_done, i + 1)
                    if pr >= 2:
                        dve.wait_ge(prob_turned, i - 3)
                    dve.scalar_tensor_tensor(out=p_ap, in0=dist[:, :], scalar=SLOPES[slope] / ATT_SCALE,
                                             in1=bank[2 + h][:, 0:384], op0=ALU.mult, op1=ALU.add).then_inc(biased_done, 1)
                    dve.wait_ge(biased_done, i + 1)
                    for part, cols in enumerate(parts):
                        last = dve.tensor_reduce(row_max[:, i, part:part + 1], p_ap[:, cols], AX_X, ALU.max)
                    step(last)
                    if pr < SWA_PAIRS:
                        dve.tensor_scalar(neg_max[:, i, :], row_max[:, i, :], sinks8[:, head:head + 1], -ATT_SCALE,
                                          ALU.max, ALU.mult).then_inc(max_done, 1)
                    else:
                        dve.tensor_scalar(neg_max[:, i, :], row_max[:, i, :], -ATT_SCALE, None, ALU.mult).then_inc(max_done, 1)

            def divide(pr):
                for h in range(2):
                    i = 2 * pr + h
                    dve.wait_ge(exp_done, i + 1)
                    if pr < SWA_PAIRS:
                        step(dve.tensor_tensor(row_sum[:, i, :], row_sum[:, i, :], sink_exp[:, i, :], ALU.add))
                    step(dve.reciprocal(inv_sum[:, i, :], row_sum[:, i, :]))
                    for part, cols in enumerate(parts):
                        p_ap = prob[:, pr % 2, h, cols]
                        last = dve.tensor_scalar(p_ap, p_ap, inv_sum[:, i, part:part + 1], None, ALU.mult)
                    last.then_inc(prob_ready, 1)

            def sigmoid(pr):
                dve.wait_ge(gate_sum, pr + 1)
                g = gates[:, 2 * pr:2 * pr + 2, :]
                dve.reciprocal(g, g).then_inc(gate_ready, 1)

            bias(0)
            take_unit(QKV_UNITS - 1)
            for pr in range(HEAD_PAIRS):
                divide(pr)
                if pr < HEAD_PAIRS - 1:
                    bias(pr + 1)
                if pr >= 1:
                    sigmoid(pr - 1)
            for group, a in enumerate((slice(SWA_PAIRS, HEAD_PAIRS - 1), slice(HEAD_PAIRS - 1, HEAD_PAIRS))):
                dve.wait_ge(att_hi_ready, group + 2)
                dve.tensor_tensor(att_lo[:, a, :], att[:, a, :], att_hi[:, a, :].bitcast(F32), ALU.subtract).then_inc(att_lo_dve, 1)
            def mix_rest(j):
                dve.wait_ge(mix_hi_ready, j + 1)
                dve.tensor_tensor(mix_lo[:, j, :], gates[:, j, :], mix_hi[:, j, :].bitcast(F32), ALU.subtract).then_inc(mix_ready, 1)

            dve.wait_ge(gate_ready, HEAD_PAIRS - 1)
            for j in range(KC):
                if j == KC - 2:
                    dve.wait_ge(gate_ready, HEAD_PAIRS + 1)
                dve.wait_ge(branch_done, j + 1)
                for b in range(2):
                    g = gates[:, KC * b + j, :]
                    last = dve.tensor_tensor(g, g, bank[2 + 2 * (j % 2) + b][:, 0:SEQ], ALU.mult)
                step(last)
                dve.tensor_tensor(gates[:, j, :], gates[:, j, :], gates[:, KC + j, :], ALU.add).then_inc(mixed, 1)
                if j >= 1:
                    mix_rest(j - 1)
                if j in (2, 4):
                    if j == 2:
                        dve.wait_ge(gate_sum, HEAD_PAIRS)
                    g = gates[:, GATE_UNITS - 2 + (j == 4), :]
                    dve.reciprocal(g, g).then_inc(gate_ready, 1)
            mix_rest(KC - 1)
            for k in range(OUT_BY_POOL, KC):
                split_out_lo(dve, k, out_lo_dve)

            def layer_norm(l, gb, loaded, banks, banks_done):
                for t in range(TILES):
                    dve.wait_ge(banks_done, t + 1)
                    halves = [h_sb[:, t, 512 * half:512 * half + 512] for half in range(2)]
                    if l == 0:
                        for half in range(2):
                            last = dve.scalar_tensor_tensor(out=halves[half], in0=halves[half], scalar=ALPHA,
                                                            in1=banks[2 * t + half][:, :], op0=ALU.mult, op1=ALU.add)
                        step(last)
                    else:
                        halves = [banks[2 * t + half][:, :] for half in range(2)]
                    for half in range(2):
                        last = dve.bn_stats(ln_stats[:, t, 6 * half:6 * half + 6], halves[half])
                    step(last)
                    step(dve.bn_aggr(ln_mv[:, t, :], ln_stats[:, t, :]))
                    dve.tensor_scalar(ln_var[:, t, :], ln_mv[:, t, 1:2], LN_EPS, None, ALU.add).then_inc(ln_var_ready, 1)
                    if t == 0:
                        dve.wait_ge(loaded, 32)
                    cols = ln_columns(l, t)[0]
                    v = h_sb[:, t, cols]
                    for half in range(2):
                        a, b = 512 * half, min(512 * half + 512, cols.stop)
                        if a < b:
                            last = dve.scalar_tensor_tensor(out=h_sb[:, t, a:b], in0=halves[half][:, 0:b - a], scalar=ln_mv[:, t, 0:1],
                                                            in1=gb[:, 0, a:b], op0=ALU.subtract, op1=ALU.mult)
                    step(last)
                    dve.wait_ge(ln_root_ready, l * TILES + t + 1)
                    step(dve.reciprocal(ln_rstd[:, t, :], ln_root[:, t, :]))
                    dve.scalar_tensor_tensor(out=ln_shift[:, t, :], in0=ln_mv[:, t, 0:1], scalar=-1.0, in1=ln_rstd[:, t, :],
                                             op0=ALU.mult, op1=ALU.mult).then_inc(ln_rstd_ready, 1)
                    dve.scalar_tensor_tensor(out=v, in0=v, scalar=ln_rstd[:, t, :], in1=gb[:, 1, cols],
                                             op0=ALU.mult, op1=ALU.add).then_inc(ln_dve, 1)

            layer_norm(0, ln1_gb, ln1_in, w_out_bank, w_out_done)

            dve.memset(group_sum, -BIG)
            dve.memset(group_pick, -BIG)
            dve.memset(weight, 0.0)
            step(dve.memset(place, 0.0))

            dve.wait_ge(h_turned, 2 * TILES)
            dve.tensor_copy(hT[:, 4:8, P:SEQ], bank[3][:, :].rearrange("p (k n) -> p k n", k=4)).then_inc(hT_dve, 1)

            dve.wait_ge(logit_exp, 1)
            step(dve.tensor_scalar(r_one, r_exp, 1.0, None, ALU.add))
            step(dve.reciprocal(score, r_one))
            dve.wait_ge(bias_in, 16)
            step(dve.tensor_tensor(biased, score, bias_r.unsqueeze(1).to_broadcast([P, TILES, N_EXPERTS]), ALU.add))
            groups = biased.rearrange("p t (g e) -> p (t g) e", e=PER_GROUP)
            for g in range(TILES * N_GROUPS):
                last = dve.max(top_in_group[:, g, :], groups[:, g, :])
            step(last)
            top2 = top_in_group.rearrange("p (t g) e -> p t g e", t=TILES)
            step(dve.tensor_tensor(group_sum[:, :, 0:N_GROUPS], top2[:, :, :, 0], top2[:, :, :, 1], ALU.add))
            for t in range(TILES):
                last = dve.max(group_top[:, t, :], group_sum[:, t, :])
            step(last)
            step(dve.tensor_copy(group_pick[:, :, 0:TOPK_GROUPS], group_top[:, :, 0:TOPK_GROUPS]))
            for t in range(TILES):
                last = dve.match_replace(out=group_marked[:, t, :], in_to_replace=group_pick[:, t, :],
                                         in_values=group_sum[:, t, :], imm_value=BIG)
            step(last)
            step(dve.tensor_scalar(group_on.rearrange("p (t g) o -> p t (g o)", t=TILES), group_marked[:, :, 0:N_GROUPS],
                                   BIG, None, ALU.is_equal))
            step(dve.tensor_scalar(group_off, group_on, -NEG_INF, NEG_INF, ALU.mult, ALU.add))
            spread = [P, TILES * N_GROUPS, PER_GROUP]
            masked_g = masked.rearrange("p t (g e) -> p (t g) e", e=PER_GROUP)
            masked_sum_g = masked_sum.rearrange("p t (g e) -> p (t g) e", e=PER_GROUP)
            step(dve.tensor_tensor(masked_g, groups, group_on.to_broadcast(spread), ALU.mult))
            step(dve.tensor_tensor(masked_sum_g, masked_g, group_off.to_broadcast(spread), ALU.add))
            for t in range(TILES):
                last = dve.max(expert_top[:, t, :], masked_sum[:, t, :])
            step(last)
            for t in range(TILES):
                last = dve.match_replace(out=expert_marked[:, t, :], in_to_replace=expert_top[:, t, :],
                                         in_values=masked_sum[:, t, :], imm_value=BIG)
            step(last)
            dve.tensor_scalar(chosen, expert_marked, BIG, None, ALU.is_equal).then_inc(chosen_ready, 1)
            dve.wait_ge(chosen_ready, 1)
            step(dve.tensor_tensor(masked, score, chosen, ALU.mult))
            step(dve.tensor_reduce(weight_sum, masked, AX_X, ALU.add))
            step(dve.reciprocal(weight_inv, weight_sum))
            for t in range(TILES):
                last = dve.tensor_scalar(weight[:, t, 0:N_EXPERTS], masked[:, t, :], weight_inv[:, t, :], ROUTED_SCALE,
                                         ALU.mult, ALU.mult)
            step(last)

            def shared_hidden(c):
                dve.wait_ge(shared_silu, c + 1)
                dve.tensor_tensor(sh_hidT[:, c, :], sh_silu[:, c, :], bank[5 + 2 * c][:, 0:SEQ], ALU.mult).then_inc(shared_hid, 1)

            shared_hidden(0)

            dve.wait_ge(lines_done, 1)
            lines = bank[3][:, 0:3 * N_EXPERTS].rearrange("p (t e) -> p t e", t=3)
            dve.scalar_tensor_tensor(out=place[:, :, 0:N_EXPERTS], in0=lines[:, 0:TILES, :], scalar=1.0, in1=chosen,
                                     op0=ALU.add, op1=ALU.mult)
            step(dve.tensor_reduce(most, lines[:, TILES, :], AX_X, ALU.max))
            step(dve.tensor_scalar(over_f, most, SLOTS + 0.5, None, ALU.is_gt))
            dve.tensor_copy(over, over_f).then_inc(over_ready, 1)
            dve.wait_ge(const_ready, 2)

            def choose_for(q, j):
                shape = [P, TILES, 2, SLOTS]
                dve.tensor_tensor(choose[j][:, :, :].rearrange("p t (e s) -> p t e s", e=2),
                                  place[:, :, bass.ds(2 * q, 2)].unsqueeze(3).to_broadcast(shape),
                                  place_ids[:, :].unsqueeze(1).unsqueeze(1).to_broadcast(shape), ALU.is_equal).then_inc(choose_ready, 1)

            def weigh(q, j, rnd):
                shape = [P, TILES, 2, SLOTS]
                dve.wait_ge(choose_ready, rnd * (PAIRS + 1) + q + 1)
                dve.tensor_tensor(choose_w[j][:, :, :].rearrange("p t (e s) -> p t e s", e=2),
                                  weight[:, :, bass.ds(2 * q, 2)].unsqueeze(3).to_broadcast(shape),
                                  choose[j][:, :, :].rearrange("p t (e s) -> p t e s", e=2), ALU.mult).then_inc(choose_w_ready, 1)

            def take_hi(q, rnd):
                dve.wait_ge(gather_hi, rnd * PAIRS + q + 1)
                dve.tensor_copy(xg[:, 4:8, :], R_HI[:, :].rearrange("p (k n) -> p k n", k=4)).then_inc(xg_hi, 1)

            def form_choiceT(q, j, rnd):
                dve.wait_ge(turned_ready, rnd * (PAIRS + 1) + q + 1)
                dve.tensor_scalar(choiceT[j][:, :], choice_wT[:, :], 0.0, None, ALU.is_gt).then_inc(choice_ready, 1)

            def pair(p, j, rnd, last):
                if not last:
                    if not static_zero(p, rnd):
                        dve.wait_ge(turned, rnd * (PAIRS + 1) + p)
                    choose_for(p + 2, (j + 2) % UNROLL)
                dve.wait_ge(silu_done, rnd * PAIRS + p + 1)
                dve.scalar_tensor_tensor(out=hid[:, :], in0=silu_sb[:, :], scalar=place_weight[j], in1=R_GU[:, FF:2 * FF],
                                         op0=ALU.mult, op1=ALU.mult).then_inc(hid_ready, 1)
                if not last:
                    weigh(p + 2, (j + 2) % UNROLL, rnd)
                    take_hi(p + 1, rnd)
                    form_choiceT(p + 1, (j + 1) % UNROLL, rnd)
                for half, b in enumerate((R_LO, R_HI)):
                    cols = slice(512 * half, 512 * half + 512)
                    dve.wait_ge(y_top_ready, 2 * (rnd * PAIRS + p) + half + 1)
                    dve.tensor_tensor(y_rest[:, cols], b[:, :], y_top[:, cols].bitcast(F32), ALU.subtract).then_inc(y_ready, 1)

            def all_pairs(rnd):
                for q in range(2):
                    choose_for(q, q)
                    weigh(q, q, rnd)
                if static_zero(rnd):
                    shared_hidden(1)
                take_hi(0, rnd)
                form_choiceT(0, 0, rnd)
                pair(0, 0, rnd, False)
                with dve.Fori(0, (PAIRS - 2) // UNROLL) as it:
                    for i in range(UNROLL):
                        pair(it * UNROLL + (1 + i), (1 + i) % UNROLL, rnd, False)
                pair(PAIRS - 1, (PAIRS - 1) % UNROLL, rnd, True)

            all_pairs(0)
            dve.wait_ge(over_ready, 1)
            more = dve.value_load(over[0:1, 0:1], min_val=0, max_val=1)
            with dve.If(more == 1):
                with dve.Fori(1, ROUNDS) as rnd:
                    dve.wait_ge(turned, rnd * (PAIRS + 1))
                    dve.tensor_scalar(place_ids[:, :], place_ids[:, :], float(SLOTS), None, ALU.add).then_inc(round_ready, 1)
                    dve.wait_ge(round_ready, rnd)
                    all_pairs(rnd)
            layer_norm(1, ln2_gb, ln2_in, acc, moe_done)

        @block.tensor
        def _(pe):
            pe.wait_ge(const_ready, 1)
            for _ in range(WARM_UP):
                pe.transpose(bank[0][:, 0:P], ident[:, :], ident[:, :])
            for t in range(TILES):
                pe.wait_ge(x_in[t], 16)
                for g in range(2):
                    for kk in range(4):
                        k = 4 * g + kk
                        last = pe.transpose(bank[4 + 2 * t + g][:, kk * P:(kk + 1) * P], h_sb[:, t, k * P:(k + 1) * P], ident[:, :])
                    last.then_inc(x_turned, 1)
            pe.wait_ge(xT_act, 2)
            pe.wait_ge(xT_dve, 2)

            def project(u):
                b = bank[u % 2]
                if u >= 2:
                    who, count = evacuated(u - 2)
                    pe.wait_ge(proj_act if who == "act" else proj_dve, count)
                if u == 0:
                    pe.wait_ge(kv_swa_in, 16)
                    w, _ = chunk_view(0)
                    for t in range(TILES):
                        for k in range(KC):
                            last = pe.matmul(b[:, t * P:(t + 1) * P], xT[:, k, t * P:(t + 1) * P], w[:, k, 640:768],
                                             start=(k == 0), stop=(k == KC - 1))
                else:
                    _, _, hi, lo = unit_weights(u)
                    if u == 1:
                        pe.wait_ge(xT_hi_ready, 4)
                        pe.wait_ge(xT_lo_ready, 4)
                    if u < QKV_UNITS:
                        pe.wait_ge(w_lo_ready, u)
                        x_hi = xT_hi
                    else:
                        pe.wait_ge(w_lo_gate, u - QKV_UNITS + 1)
                        x_hi = xT_hi_kept
                    if u == QKV_UNITS:
                        pe.wait_ge(xT_kept, 1)
                    if u in (14, 15):
                        for t in range(TILES):
                            toks = slice(t * P, (t + 1) * P)
                            for k in range(KC):
                                for i, (a, w) in enumerate(((x_hi, hi), (x_hi, lo), (xT_lo, hi))):
                                    last = pe.matmul(b[:, 256 * t:256 * t + 256], a[:, k, toks], w[:, k, :],
                                                     start=(k == 0 and i == 0), stop=(k == KC - 1 and i == 2))
                    else:
                        for k in range(KC):
                            for i, (w, a) in enumerate(((hi, x_hi), (lo, x_hi), (hi, xT_lo))):
                                last = pe.matmul(b[:, 0:SEQ], w[:, k, :], a[:, k, :],
                                                 start=(k == 0 and i == 0), stop=(k == KC - 1 and i == 2))
                last.then_inc(proj_done, 1)

            def score(pr):
                q = q_swa[:, pr, :] if pr < SWA_PAIRS else q_moba[:, pr - SWA_PAIRS, :]
                k = k_swa if pr < SWA_PAIRS else k_moba[:, pr - SWA_PAIRS, :]
                for h in range(2):
                    rows = slice(64 * h, 64 * h + 64)
                    if pr >= 1:
                        pe.wait_ge(biased_done, 2 * (pr - 1) + h + 1)
                    pe.matmul(bank[2 + h][:, 0:256], q[rows, P:SEQ], k[rows, 0:SEQ], start=True, stop=True)
                    pe.matmul(bank[2 + h][:, 256:384], q[rows, 0:P], k[rows, 0:P], start=True, stop=True).then_inc(scores_done, 1)

            def turn_prob(pr):
                for h in range(2):
                    pe.wait_ge(prob_ready, 2 * pr + h + 1)
                    if pr >= 1:
                        pe.wait_ge(probT_ready, 2 * (pr - 1) + h + 1)
                    for to, fr in ((0, 256), (128, 0), (256, 128)):
                        last = pe.transpose(bank[5 + h][:, to:to + P], prob[:, pr % 2, h, fr:fr + P], ident[:, :])
                    last.then_inc(prob_turned, 1)

            def times_v(pr):
                pe.wait_ge(probT_ready, 2 * pr + 2)
                if pr >= 1:
                    pe.wait_ge(att_ready, pr)
                for h, (_, head) in enumerate(heads_of(pr)):
                    rows = slice(64 * h, 64 * h + 64)
                    if pr < SWA_PAIRS:
                        v = [v_swa[:, t, 64 * h:64 * h + 64] for t in range(TILES)]
                    else:
                        v = [v_moba[:, t, 64 * head:64 * head + 64] for t in range(TILES)]
                    pe.matmul(bank[4][rows, 0:SEQ], v[0], probT[:, pr % 2, h, 0:256], start=True, stop=False)
                    last = pe.matmul(bank[4][rows, P:SEQ], v[1], probT[:, pr % 2, h, 256:384], start=False, stop=True)
                last.then_inc(pv_done, 1)

            for u in range(QKV_UNITS - 1):
                project(u)
            pe.wait_ge(proj_act, 2)
            pe.wait_ge(proj_dve, 1)
            score(0)
            project(QKV_UNITS - 1)
            for pr in range(HEAD_PAIRS):
                project(QKV_UNITS + 2 * pr)
                if pr >= 1:
                    times_v(pr - 1)
                if pr == 0:
                    pe.wait_ge(proj_act, QKV_UNITS // 2)
                    pe.wait_ge(proj_dve, QKV_UNITS // 2)
                if pr < HEAD_PAIRS - 1:
                    score(pr + 1)
                project(QKV_UNITS + 2 * pr + 1)
                turn_prob(pr)

            def branch(j, first, end):
                pe.wait_ge(branch_lo_ready, j + 1)
                hi = branch_hi[BRANCH_PLACE[j]]
                for i in range(first, end):
                    b, c = i // SWA_PAIRS, i % SWA_PAIRS
                    lo = branch_weights(b, j)[1]
                    for n, (w, a) in enumerate(((hi[:, i, :], att_hi), (lo[:, c, :], att_hi), (hi[:, i, :], att_lo))):
                        last = pe.matmul(bank[2 + 2 * (j % 2) + b][:, 0:SEQ], w, a[:, i, :],
                                         start=(c == 0 and n == 0), stop=(c == 3 and n == 2))
                if end == HEAD_PAIRS:
                    last.then_inc(branch_done, 1)

            pe.wait_ge(att_lo_pool, 1)
            pe.wait_ge(biased_done, 2 * HEAD_PAIRS)
            branch(0, 0, SWA_PAIRS)
            times_v(HEAD_PAIRS - 1)
            pe.wait_ge(att_lo_dve, 1)
            branch(0, SWA_PAIRS, HEAD_PAIRS - 1)
            pe.wait_ge(att_ready, HEAD_PAIRS)
            branch(1, 0, SWA_PAIRS)
            pe.wait_ge(att_lo_dve, 2)
            branch(0, HEAD_PAIRS - 1, HEAD_PAIRS)
            branch(1, SWA_PAIRS, HEAD_PAIRS)
            for j in range(2, KC):
                pe.wait_ge(mixed, j - 1)
                branch(j, 0, HEAD_PAIRS)

            def project_out(k, t):
                pe.wait_ge(mix_ready, k + 1)
                if k < OUT_BY_POOL:
                    pe.wait_ge(out_lo_pool, k + 1)
                else:
                    pe.wait_ge(out_lo_dve, k + 1 - OUT_BY_POOL)
                hi, lo = out_hi[OUT_PLACE[k]], out_weights(k)[1]
                toks = slice(t * P, (t + 1) * P)
                for half in range(2):
                    cols = slice(512 * half, 512 * half + 512)
                    for n, (a, w) in enumerate(((mix_hi, hi), (mix_lo, hi), (mix_hi, lo))):
                        last = pe.matmul(w_out_bank[2 * t + half][:, :], a[:, k, toks], w[:, cols],
                                         start=(k == 0 and n == 0), stop=(k == KC - 1 and n == 2))
                return last

            pe.wait_ge(proj_act, QKV_UNITS // 2 + GATE_UNITS)
            def turn_h(t):
                pe.wait_ge(ln_dve, t + 1)
                for k in range(KC):
                    if k == ln_columns(0, t)[1].start // P:
                        pe.wait_ge(ln_pool, t)
                    last = pe.transpose(bank[2 + k // 4][:, k % 4 * P:(k % 4 + 1) * P], h_sb[:, t, k * P:(k + 1) * P], ident[:, :])
                    if k % 4 == 3:
                        last.then_inc(h_turned, 1)

            for k in range(2):
                for t in range(TILES):
                    last = project_out(k, t)
                last.then_inc(out_step, 1)
            for t in range(TILES):
                for k in range(2, KC):
                    if (t, k) == (1, KC - 1):
                        turn_h(0)
                    last = project_out(k, t)
                last.then_inc(w_out_done, 1)

            def route(t):
                for k in range(KC):
                    last = pe.matmul(bank[0][:, t * P:(t + 1) * P], hT[:, k, t * P:(t + 1) * P],
                                     wr_sb[:, k, :].unsqueeze(1).to_broadcast([P, 2, N_EXPERTS]),
                                     start=(k == 0), stop=(k == KC - 1))
                return last

            def shared_unit(t, c, i):
                w = (slot_gate(4), slot_up(4))[i]
                for k in range(KC):
                    last = pe.matmul(bank[4 + 2 * c + i][:, t * P:(t + 1) * P], w[:, k, c * P:(c + 1) * P],
                                     hT[:, k, t * P:(t + 1) * P], start=(k == 0), stop=(k == KC - 1))
                return last

            pe.wait_ge(hT_act, 2)
            pe.wait_ge(router_in, 16)
            route(0)
            pe.wait_ge(shared_in, 32)
            shared_unit(0, 0, 0)
            shared_unit(0, 0, 1)
            turn_h(1)
            shared_unit(0, 1, 0)
            pe.wait_ge(hT_act, 3)
            pe.wait_ge(hT_dve, 1)
            route(1).then_inc(logits_done, 1)
            shared_unit(0, 1, 1)
            shared_unit(1, 0, 0)
            shared_unit(1, 0, 1).then_inc(shared_gu, 1)

            shared_unit(1, 1, 0)
            pe.wait_ge(const_ready, 2)
            pe.wait_ge(chosen_ready, 1)
            cols = [slice(i * N_EXPERTS, (i + 1) * N_EXPERTS) for i in range(3)]
            pe.matmul(bank[3][:, cols[0]], before[:, :], chosen[:, 0, :], start=True, stop=True)
            pe.matmul(bank[3][:, cols[1]], ones[:, :], chosen[:, 0, :], start=True, stop=False)
            pe.matmul(bank[3][:, cols[1]], before[:, :], chosen[:, 1, :], start=False, stop=True)
            pe.matmul(bank[3][:, cols[2]], ones[:, :], chosen[:, 0, :], start=True, stop=False)
            pe.matmul(bank[3][:, cols[2]], ones[:, :], chosen[:, 1, :], start=False, stop=True).then_inc(lines_done, 1)
            shared_unit(1, 1, 1).then_inc(shared_gu, 1)

            def shared_down(t, half):
                pe.wait_ge(shared_down_in, 16)
                for c in range(2):
                    pe.matmul(acc[2 * t + half][:, :], sh_hidT[:, c, t * P:(t + 1) * P], sh_down[:, c, 512 * half:512 * half + 512],
                              start=False, stop=False, skip_group_check=True)

            def gather(q, j, rnd):
                pe.wait_ge(choose_ready, rnd * (PAIRS + 1) + q + 1)
                for g, (b, done) in enumerate(((R_LO, gather_lo), (R_HI, gather_hi))):
                    for kk in range(4):
                        k = 4 * g + kk
                        for t in range(TILES):
                            for i, part in enumerate(h_part):
                                last = pe.matmul(b[:, kk * P:(kk + 1) * P], part[:, t, k * P:(k + 1) * P], choose[j][:, t, :],
                                                 start=(t == 0 and i == 0), stop=(t == TILES - 1 and i == 2))
                    last.then_inc(done, 1)

            def turn_choice(q, j, rnd):
                pe.wait_ge(choose_w_ready, rnd * (PAIRS + 1) + q + 1)
                for t in range(TILES):
                    last = pe.transpose(R_T[:, 256 + t * P:256 + (t + 1) * P], choose_w[j][:, t, :], ident[:, :])
                return last

            def scatter(j, halves=(0, 1), opens=False):
                last = []
                for t in range(TILES):
                    for half in halves:
                        for y in (y_top, y_rest):
                            product = pe.matmul(acc[2 * t + half][:, :], choiceT[j][:, t * P:(t + 1) * P],
                                                y[:, 512 * half:512 * half + 512], start=opens and y is y_top, stop=False,
                                                skip_group_check=True)
                    last.append(product)
                return last

            def add_input(t, halves):
                for half in halves:
                    pe.matmul(acc[2 * t + half][:, :], alpha_ident[:, :], h_sb[:, t, 512 * half:512 * half + 512],
                              start=False, stop=False, skip_group_check=True)

            def pair(p, turn_no, j, rnd, first, last_pair, shared=()):
                fill = rnd * PER_ROUND[j] + turn_no + 1
                last_of_all = last_pair and static_zero(rnd)
                if last_of_all:
                    add_input(0, (0, 1))
                for k in range(KC):
                    if k % (KC // 2) == 0:
                        for i in range(2):
                            pe.wait_ge(gate_up_in[2 * j + i][k // (KC // 2)], fill * 32)
                    for i in range(2):
                        last = pe.matmul(R_GU[64 * i:64 * i + 64, :], xg[:, k, 64 * i:64 * i + 64],
                                         slot_gate_up(2 * j + i)[:, k, :, :], start=(k == 0), stop=(k == KC - 1))
                last.then_inc(gate_up_done, 1)
                if not last_pair:
                    if not first:
                        pe.wait_ge(y_ready, 2 * (rnd * PAIRS + p))
                    gather(p + 1, (j + 1) % UNROLL, rnd)
                    turn_choice(p + 1, (j + 1) % UNROLL, rnd)
                if last_of_all:
                    add_input(1, (0,))
                pe.wait_ge(hid_ready, rnd * PAIRS + p + 1)
                for c in range(FF // P):
                    last = pe.transpose(R_T[:, c * P:(c + 1) * P], hid[:, c * P:(c + 1) * P], ident[:, :])
                last.then_inc(turned, 1)
                if not first:
                    if last_pair:
                        pe.wait_ge(y_ready, 2 * (rnd * PAIRS + p))
                    pe.wait_ge(choice_ready, rnd * PAIRS + p)
                    opens = static_zero(p - 1, rnd)
                    if opens:
                        pe.wait_ge(shared_hid, 2)
                    scatter((j - 1) % UNROLL, opens=opens)
                    for t, half in shared:
                        shared_down(t, half)
                pe.wait_ge(turned_ready, rnd * (PAIRS + 1) + p + 2)
                if not last_pair:
                    pe.wait_ge(xg_lo, rnd * PAIRS + p + 2)
                    pe.wait_ge(xg_hi, rnd * PAIRS + p + 2)
                for i in range(2):
                    pe.wait_ge(down_in[2 * j + i], fill * 16)
                for half, (b, done) in enumerate(((R_LO, down_lo), (R_HI, down_hi))):
                    for c in range(FF // P):
                        for i in range(2):
                            last = pe.matmul(b[64 * i:64 * i + 64, :], hidT[:, c * P + 64 * i:c * P + 64 * i + 64],
                                             slot_down(2 * j + i)[:, c, 512 * half:512 * half + 512],
                                             start=(c == 0), stop=(c == FF // P - 1))
                    last.then_inc(done, 1)
                if last_of_all:
                    add_input(1, (1,))

            def all_pairs(rnd):
                gather(0, 0, rnd)
                turn_choice(0, 0, rnd).then_inc(turned, 1)
                pe.wait_ge(xg_lo, rnd * PAIRS + 1)
                pe.wait_ge(xg_hi, rnd * PAIRS + 1)
                pe.wait_ge(turned_ready, rnd * (PAIRS + 1) + 1)
                pair(0, 0, 0, rnd, True, False)
                peeled = 0
                if static_zero(rnd):
                    peeled = 1
                    for i, shared in enumerate((((0, 0),), ((0, 1),), ((1, 0), (1, 1)))):
                        p = 1 + i
                        pair(p, p // UNROLL, p % UNROLL, rnd, False, False, shared)
                with pe.Fori(peeled, (PAIRS - 2) // UNROLL) as it:
                    for i in range(UNROLL):
                        p = 1 + i
                        pair(it * UNROLL + p, it + p // UNROLL, p % UNROLL, rnd, False, False)
                last = PAIRS - 1
                pair(last, last // UNROLL, last % UNROLL, rnd, False, True)

            pe.wait_ge(part_ready, 3)
            pe.wait_ge(over_ready, 1)
            all_pairs(0)
            more = pe.value_load(over[0:1, 0:1], min_val=0, max_val=1)
            with pe.If(more == 1):
                with pe.Fori(1, ROUNDS) as rnd:
                    pe.wait_ge(y_ready, 2 * rnd * PAIRS)
                    scatter((PAIRS - 1) % UNROLL)
                    all_pairs(rnd)
                pe.wait_ge(y_ready, 2 * ROUNDS * PAIRS)
            for half in range(2):
                pe.wait_ge(y_ready, 2 * PAIRS - 1 + half)
                last = scatter((PAIRS - 1) % UNROLL, (half,))
            for product in last:
                product.then_inc(moe_done, 1)


_INS = ["x", "w_in", "swa_sinks", "w_branch_swa", "w_branch_moba", "w_out", "ln1_g", "ln1_b", "w_router", "router_bias",
        "w_exp_gate", "w_exp_up", "w_exp_down", "w_sh_gate", "w_sh_up", "w_sh_down", "ln2_g", "ln2_b"]


def kernel(**inputs):
    import numpy as np
    import concourse.bacc as bacc
    from concourse.bass_utils import run_bass_kernel_spmd

    nc = bacc.Bacc("TRN2", target_bir_lowering=False, num_devices=1)
    arrays, args = {}, []
    for name in _INS:
        a = np.ascontiguousarray(inputs[name])
        arrays[f"in_{name}_dram"] = a
        args.append(nc.dram_tensor(f"in_{name}_dram", a.shape, mybir.dt.from_np(a.dtype), kind="ExternalInput").ap())
    out = nc.dram_tensor("out_0_dram", (1, SEQ, D), F32, kind="ExternalOutput").ap()
    block_program(nc, *args, out)
    r = run_bass_kernel_spmd(nc, [arrays], core_ids=[0])
    return r.results[0]["out_0_dram"]
```
